# Optimizing a Trainium2 kernel written in Bass

```python
import math
import jax
import jax.numpy as jnp
from jax import lax
import numpy as np

D_MODEL = 1024
BATCH = 1
SEQ = 1024
DEPTH = 2

GRID_W = 64
CTX_LEN = 256
N_EVEN = (DEPTH + 1) // 2
N_ODD = DEPTH // 2
EPS = 1e-6
ROPE_BASE = 10000.0
Q_BLOCK = 128
FFN_HIDDEN = ((8 * D_MODEL + 3 * 256 - 1) // (3 * 256)) * 256

HG_WIDTH = D_MODEL // 2
HG_HEAD_DIM = 128
HG_HEADS = HG_WIDTH // HG_HEAD_DIM
HG_CHUNK = 64
HY_WIDTH = D_MODEL - HG_WIDTH
HY_BANDS = 16
HY_EMB = 2 * HY_BANDS + 1
HY_FILTER_DIM = 64
HY_TARGET = 1e-2
HY_STEEP_PCT = 0.3
HY_GENTLE_PCT = 1.5
EVEN_IN = 5 * HG_WIDTH + 3 * HY_WIDTH
EVEN_OUT = HG_WIDTH + HY_WIDTH
DA_WIDTH = D_MODEL // 2
DA_HEAD_DIM = 64
DA_HEADS = DA_WIDTH // (2 * DA_HEAD_DIM)
DA_V_DIM = 2 * DA_HEAD_DIM
MLA_HEADS = 4
MLA_NOPE = 64
MLA_ROPE = 32
MLA_V = 128
MLA_Q_RANK = D_MODEL // 4
MLA_KV_RANK = D_MODEL // 8
ODD_IN = 3 * DA_WIDTH + MLA_Q_RANK + MLA_KV_RANK + MLA_ROPE
ODD_OUT = DA_HEADS * DA_V_DIM + MLA_HEADS * MLA_V

kernel_name = 'hybrid_hgrn2_hyena_diffattn_mla_dit'

def rms_norm(x, g):
    xf = x.astype(jnp.float32)
    y = xf * lax.rsqrt(jnp.mean(xf * xf, axis=-1, keepdims=True) + EPS)
    return (y * g.astype(jnp.float32)).astype(x.dtype)

def modulate(h, shift, scale):
    return h * (1 + scale) + shift

def swiglu(h, w_gu, w_down):
    g, u = jnp.split(h @ w_gu, 2, axis=-1)
    return (jax.nn.silu(g) * u) @ w_down

def rope_1d(x, pos):
    half = x.shape[-1] // 2
    inv = ROPE_BASE ** (-jnp.arange(half, dtype=jnp.float32) / half)
    ang = pos.astype(jnp.float32)[:, None] * inv
    cos, sin = jnp.cos(ang), jnp.sin(ang)
    xf = x.astype(jnp.float32)
    x1, x2 = xf[..., :half], xf[..., half:]
    return jnp.concatenate([x1 * cos - x2 * sin, x2 * cos + x1 * sin], axis=-1).astype(x.dtype)

def rope_2d(x, row, col):
    h = x.shape[-1] // 2
    return jnp.concatenate([rope_1d(x[..., :h], row), rope_1d(x[..., h:], col)], axis=-1)

def heads_to_tokens(o):
    b_, h_, l_, d_ = o.shape
    return o.transpose(0, 2, 1, 3).reshape(b_, l_, h_ * d_)

def block_attention(q, k, v, scale):
    b_, h_, lq, dq = q.shape
    nb = lq // Q_BLOCK
    qb = q.reshape(b_, h_, nb, Q_BLOCK, dq).transpose(2, 0, 1, 3, 4)

    def one(qi):
        s = jnp.einsum('bhqd,bhkd->bhqk', qi, k, preferred_element_type=jnp.float32) * scale
        p = jax.nn.softmax(s, axis=-1)
        return jnp.einsum('bhqk,bhkd->bhqd', p.astype(v.dtype), v)

    o = lax.map(one, qb)
    return o.transpose(1, 2, 0, 3, 4).reshape(b_, h_, lq, v.shape[-1])

def chunk_scan(q, k, v, log_f, s0):
    b_, h_, length, _ = q.shape
    dv = v.shape[-1]
    n = length // HG_CHUNK

    def chunks(t):
        return t.reshape(b_, h_, n, HG_CHUNK, t.shape[-1]).transpose(2, 0, 1, 3, 4)

    mask = jnp.tril(jnp.ones((HG_CHUNK, HG_CHUNK), dtype=bool))[:, :, None]

    def step(s, inp):
        qc, kc, vc, gc = inp
        cum = jnp.cumsum(gc, axis=-2)
        rel = cum[..., :, None, :] - cum[..., None, :, :]
        dec = jnp.exp(jnp.where(mask, rel, -jnp.inf))
        attn = jnp.einsum('bhtd,bhsd,bhtsd->bhts', qc, kc, dec)
        o = jnp.einsum('bhtd,bhde->bhte', qc * jnp.exp(cum), s) + jnp.einsum('bhts,bhse->bhte', attn, vc)
        last = cum[..., -1:, :]
        s = jnp.exp(last[..., 0, :])[..., None] * s + jnp.einsum('bhsd,bhse->bhde', kc * jnp.exp(last - cum), vc)
        return s, o

    s_fin, o = lax.scan(step, s0, (chunks(q), chunks(k), chunks(v), chunks(log_f)))
    return o.transpose(1, 2, 0, 3, 4).reshape(b_, h_, length, dv), s_fin

def hgrn2_mixer(z_lat, z_ctx, lb, out_norm_g):
    def split_heads(t):
        b_, l_, _ = t.shape
        return t.astype(jnp.float32).reshape(b_, l_, HG_HEADS, HG_HEAD_DIM).transpose(0, 2, 1, 3)

    def prep(z):
        q, ff, fb, i, g = jnp.split(z, 5, axis=-1)
        return split_heads(q), split_heads(ff), split_heads(fb), split_heads(i), g

    def gate(zf, lbd):
        lbh = lbd.reshape(HG_HEADS, 1, HG_HEAD_DIM)
        f = lbh + (1.0 - lbh) * jax.nn.sigmoid(zf)
        return jnp.log(f), 1.0 - f

    def flip(t):
        return jnp.flip(t, axis=2)

    def bidir(q, ff, fb, i, s_f, s_b):
        lf, kf = gate(ff, lb[0])
        lbk, kb = gate(fb, lb[1])
        o_f, s_f = chunk_scan(q, kf, i, lf, s_f)
        o_b, s_b = chunk_scan(flip(q), flip(kb), flip(i), flip(lbk), s_b)
        return o_f + flip(o_b), s_f, s_b

    def readout(o, g):
        o = heads_to_tokens(rms_norm(o, out_norm_g))
        return (o * jax.nn.silu(g.astype(jnp.float32))).astype(g.dtype)

    qc, ffc, fbc, ic, gc = prep(z_ctx)
    s0 = jnp.zeros((z_ctx.shape[0], HG_HEADS, HG_HEAD_DIM, HG_HEAD_DIM), jnp.float32)
    o_c, s_f, s_b = bidir(qc, ffc, fbc, ic, s0, s0)
    ql, ffl, fbl, il, gl = prep(z_lat)
    o_l, _, _ = bidir(ql, ffl, fbl, il, s_f, s_b)
    return readout(o_l, gl), readout(o_c, gc)

def hyena_filter(length, w1, b1, fr1, w2, b2, fr2, w3):
    f32 = jnp.float32
    t = jnp.linspace(0.0, 1.0, length, dtype=f32)[:, None]
    w = 2.0 * math.pi * jnp.arange(length, dtype=f32)[:, None] / length
    bands = jnp.linspace(1e-4, HY_BANDS - 1, HY_BANDS, dtype=f32)[None, :]
    z = jnp.concatenate([t, jnp.cos(bands * w), -jnp.sin(bands * w)], axis=-1)
    h = jnp.sin(fr1.astype(f32) * (z @ w1.astype(f32) + b1.astype(f32)))
    h = jnp.sin(fr2.astype(f32) * (h @ w2.astype(f32) + b2.astype(f32)))
    h = (h @ w3.astype(f32)).reshape(length, 2, HY_WIDTH)
    d_lo = -math.log(HY_TARGET) / HY_GENTLE_PCT
    d_hi = -math.log(HY_TARGET) / HY_STEEP_PCT
    deltas = jnp.linspace(d_lo, d_hi, HY_WIDTH, dtype=f32)
    h = h * jnp.exp(-t * deltas)[:, None, :]
    h_fwd, h_bwd = h[:, 0], h[:, 1]
    filt = jnp.concatenate([h_fwd, jnp.zeros((1, HY_WIDTH), f32), h_bwd[: length - 1][::-1]], axis=0)
    return filt / jnp.sum(jnp.abs(filt), axis=0, keepdims=True)

def hyena_mixer(z, short_w, short_b, filt, skip):
    length = z.shape[1]
    zp = jnp.pad(z, ((0, 0), (1, 1), (0, 0)))
    zc = zp[:, :-2] * short_w[0] + zp[:, 1:-1] * short_w[1] + zp[:, 2:] * short_w[2] + short_b
    x0, x1, v = jnp.split(zc, 3, axis=-1)
    u = (x1 * v).astype(jnp.float32)
    uf = jnp.fft.rfft(u, n=2 * length, axis=1)
    ff = jnp.fft.rfft(filt, n=2 * length, axis=0)
    y = jnp.fft.irfft(uf * ff[None], n=2 * length, axis=1)[:, :length]
    y = y + skip.astype(jnp.float32) * u
    return (x0.astype(jnp.float32) * y).astype(z.dtype)

def even_mixer(h_lat, h_ctx, w_in, w_out, lb, out_norm_g, short_w, short_b, filt_params, skip, need_ctx):
    z_lat = h_lat @ w_in
    z_ctx = h_ctx @ w_in
    na = 5 * HG_WIDTH
    a_lat, a_ctx = hgrn2_mixer(z_lat[..., :na], z_ctx[..., :na], lb, out_norm_g)
    b_lat = hyena_mixer(z_lat[..., na:], short_w, short_b, hyena_filter(h_lat.shape[1], *filt_params), skip)
    y_lat = jnp.concatenate([a_lat, b_lat], axis=-1) @ w_out
    if not need_ctx:
        return y_lat, None
    b_ctx = hyena_mixer(z_ctx[..., na:], short_w, short_b, hyena_filter(h_ctx.shape[1], *filt_params), skip)
    y_ctx = jnp.concatenate([a_ctx, b_ctx], axis=-1) @ w_out
    return y_lat, y_ctx

def diff_heads(z, row, col, rotate):
    b_, l_, _ = z.shape
    q, k, v = jnp.split(z, 3, axis=-1)

    def qk(t):
        t = t.reshape(b_, l_, DA_HEADS, 2, DA_HEAD_DIM).transpose(0, 3, 2, 1, 4).reshape(b_, 2 * DA_HEADS, l_, DA_HEAD_DIM)
        return rope_2d(t, row, col) if rotate else t

    v = v.reshape(b_, l_, DA_HEADS, DA_V_DIM).transpose(0, 2, 1, 3)
    return qk(q), qk(k), jnp.concatenate([v, v], axis=1)

def diff_readout(o, lam, lam_init, subln_g):
    b_, _, l_, _ = o.shape
    o = o.reshape(b_, 2, DA_HEADS, l_, DA_V_DIM)
    o = o[:, 0] - lam.astype(o.dtype) * o[:, 1]
    o = rms_norm(o, subln_g) * (1.0 - lam_init)
    return heads_to_tokens(o)

def mla_heads(z, q_norm_g, w_uq, kv_norm_g, w_ukv, row, col, rotate):
    b_, l_, _ = z.shape
    cq = z[..., :MLA_Q_RANK]
    ckv = z[..., MLA_Q_RANK:MLA_Q_RANK + MLA_KV_RANK]
    kr = z[..., MLA_Q_RANK + MLA_KV_RANK:][:, None]
    q = (rms_norm(cq, q_norm_g) @ w_uq).reshape(b_, l_, MLA_HEADS, MLA_NOPE + MLA_ROPE).transpose(0, 2, 1, 3)
    kv = (rms_norm(ckv, kv_norm_g) @ w_ukv).reshape(b_, l_, MLA_HEADS, MLA_NOPE + MLA_V).transpose(0, 2, 1, 3)
    q_nope, q_rope = q[..., :MLA_NOPE], q[..., MLA_NOPE:]
    k_nope, v = kv[..., :MLA_NOPE], kv[..., MLA_NOPE:]
    if rotate:
        q_rope = rope_2d(q_rope, row, col)
        kr = rope_2d(kr, row, col)
    q = jnp.concatenate([q_nope, q_rope], axis=-1)
    k = jnp.concatenate([k_nope, jnp.broadcast_to(kr, (b_, MLA_HEADS, l_, MLA_ROPE))], axis=-1)
    return q, k, v

def odd_mixer(h_lat, h_ctx, row, col, w_in, w_out, lam_p, lam_init, subln_g, q_norm_g, w_uq, kv_norm_g, w_ukv, need_ctx):
    z_lat = h_lat @ w_in
    z_ctx = h_ctx @ w_in
    nc = 3 * DA_WIDTH
    lp = lam_p.astype(jnp.float32)
    lam = jnp.exp(jnp.sum(lp[0] * lp[1])) - jnp.exp(jnp.sum(lp[2] * lp[3])) + lam_init
    qa, ka, va = diff_heads(z_lat[..., :nc], row, col, True)
    qa_c, ka_c, va_c = diff_heads(z_ctx[..., :nc], row, col, False)
    qm, km, vm = mla_heads(z_lat[..., nc:], q_norm_g, w_uq, kv_norm_g, w_ukv, row, col, True)
    qm_c, km_c, vm_c = mla_heads(z_ctx[..., nc:], q_norm_g, w_uq, kv_norm_g, w_ukv, row, col, False)
    sa = DA_HEAD_DIM ** -0.5
    sm = (MLA_NOPE + MLA_ROPE) ** -0.5
    oa = block_attention(qa, jnp.concatenate([ka, ka_c], axis=2), jnp.concatenate([va, va_c], axis=2), sa)
    om = block_attention(qm, jnp.concatenate([km, km_c], axis=2), jnp.concatenate([vm, vm_c], axis=2), sm)
    y_lat = jnp.concatenate([diff_readout(oa, lam, lam_init, subln_g), heads_to_tokens(om)], axis=-1) @ w_out
    if not need_ctx:
        return y_lat, None
    oa_c = block_attention(qa_c, ka_c, va_c, sa)
    om_c = block_attention(qm_c, km_c, vm_c, sm)
    y_ctx = jnp.concatenate([diff_readout(oa_c, lam, lam_init, subln_g), heads_to_tokens(om_c)], axis=-1) @ w_out
    return y_lat, y_ctx

def setup_inputs(seed: int = 0) -> dict:
    key = jax.random.key(seed)
    keys = iter(jax.random.split(key, 64))

    def nrm(shape, scale):
        return scale * jax.random.normal(next(keys), shape, jnp.float32)

    def gain(shape):
        return 1.0 + nrm(shape, 0.02)

    D = D_MODEL
    return {
        'x': nrm((BATCH, SEQ, D), 1.0),
        'c': nrm((BATCH, D), 1.0),
        'ctx': nrm((BATCH, CTX_LEN, D), 1.0),
        'c_ctx': nrm((D,), 1.0),
        'ada_w': nrm((DEPTH, D, 6 * D), 0.5 * D ** -0.5),
        'ada_b': nrm((DEPTH, 6 * D), 0.02),
        'norm_mix_g': gain((DEPTH, D)),
        'norm_ffn_g': gain((DEPTH, D)),
        'ffn_w_gu': nrm((DEPTH, D, 2 * FFN_HIDDEN), D ** -0.5),
        'ffn_w_down': nrm((DEPTH, FFN_HIDDEN, D), FFN_HIDDEN ** -0.5),
        'ev_w_in': nrm((N_EVEN, D, EVEN_IN), D ** -0.5),
        'ev_w_out': nrm((N_EVEN, EVEN_OUT, D), EVEN_OUT ** -0.5),
        'hg_lower_bound': nrm((N_EVEN, 2, HG_WIDTH), 1.0),
        'hg_out_norm_g': gain((N_EVEN, HG_HEAD_DIM)),
        'hy_short_w': nrm((N_EVEN, 3, 3 * HY_WIDTH), 3 ** -0.5),
        'hy_short_b': nrm((N_EVEN, 3 * HY_WIDTH), 0.02),
        'hy_filt_w1': nrm((N_EVEN, HY_EMB, HY_FILTER_DIM), HY_EMB ** -0.5),
        'hy_filt_b1': nrm((N_EVEN, HY_FILTER_DIM), 0.02),
        'hy_filt_freq1': 1.0 + nrm((N_EVEN, HY_FILTER_DIM), 0.1),
        'hy_filt_w2': nrm((N_EVEN, HY_FILTER_DIM, HY_FILTER_DIM), HY_FILTER_DIM ** -0.5),
        'hy_filt_b2': nrm((N_EVEN, HY_FILTER_DIM), 0.02),
        'hy_filt_freq2': 1.0 + nrm((N_EVEN, HY_FILTER_DIM), 0.1),
        'hy_filt_w3': nrm((N_EVEN, HY_FILTER_DIM, 2 * HY_WIDTH), HY_FILTER_DIM ** -0.5),
        'hy_skip': nrm((N_EVEN, HY_WIDTH), 0.5),
        'od_w_in': nrm((N_ODD, D, ODD_IN), D ** -0.5),
        'od_w_out': nrm((N_ODD, ODD_OUT, D), ODD_OUT ** -0.5),
        'da_lambda': nrm((N_ODD, 4, DA_HEAD_DIM), 0.1),
        'da_subln_g': gain((N_ODD, DA_V_DIM)),
        'mla_q_norm_g': gain((N_ODD, MLA_Q_RANK)),
        'mla_w_uq': nrm((N_ODD, MLA_Q_RANK, MLA_HEADS * (MLA_NOPE + MLA_ROPE)), MLA_Q_RANK ** -0.5),
        'mla_kv_norm_g': gain((N_ODD, MLA_KV_RANK)),
        'mla_w_ukv': nrm((N_ODD, MLA_KV_RANK, MLA_HEADS * (MLA_NOPE + MLA_V)), MLA_KV_RANK ** -0.5),
        'final_norm_g': gain((D,)),
    }

def reference(x, c, ctx, c_ctx, ada_w, ada_b, norm_mix_g, norm_ffn_g, ffn_w_gu, ffn_w_down, ev_w_in, ev_w_out, hg_lower_bound, hg_out_norm_g, hy_short_w, hy_short_b, hy_filt_w1, hy_filt_b1, hy_filt_freq1, hy_filt_w2, hy_filt_b2, hy_filt_freq2, hy_filt_w3, hy_skip, od_w_in, od_w_out, da_lambda, da_subln_g, mla_q_norm_g, mla_w_uq, mla_kv_norm_g, mla_w_ukv, final_norm_g):
    n_lat = x.shape[1]
    rows = n_lat // GRID_W
    tok = jnp.arange(rows * GRID_W)
    row = tok // GRID_W
    col = tok % GRID_W
    p_lb = jax.nn.softmax(hg_lower_bound.astype(jnp.float32), axis=0)
    lower_bounds = jnp.cumsum(p_lb, axis=0) - p_lb[0:1]
    sc = jax.nn.silu(c)
    scc = jax.nn.silu(c_ctx)
    h, hc = x, ctx
    for i in range(DEPTH):
        need_ctx = i < DEPTH - 1
        m = jnp.split(sc @ ada_w[i] + ada_b[i], 6, axis=-1)
        mc = jnp.split(scc @ ada_w[i] + ada_b[i], 6, axis=-1)
        hn = modulate(rms_norm(h, norm_mix_g[i]), m[0][:, None], m[1][:, None])
        hcn = modulate(rms_norm(hc, norm_mix_g[i]), mc[0], mc[1])
        if i % 2 == 0:
            e = i // 2
            filt_params = (hy_filt_w1[e], hy_filt_b1[e], hy_filt_freq1[e], hy_filt_w2[e], hy_filt_b2[e], hy_filt_freq2[e], hy_filt_w3[e])
            y, yc = even_mixer(hn, hcn, ev_w_in[e], ev_w_out[e], lower_bounds[e], hg_out_norm_g[e], hy_short_w[e], hy_short_b[e], filt_params, hy_skip[e], need_ctx)
        else:
            o = i // 2
            lam_init = 0.8 - 0.6 * math.exp(-0.3 * i)
            y, yc = odd_mixer(hn, hcn, row, col, od_w_in[o], od_w_out[o], da_lambda[o], lam_init, da_subln_g[o], mla_q_norm_g[o], mla_w_uq[o], mla_kv_norm_g[o], mla_w_ukv[o], need_ctx)
        h = h + m[2][:, None] * y
        h = h + m[5][:, None] * swiglu(modulate(rms_norm(h, norm_ffn_g[i]), m[3][:, None], m[4][:, None]), ffn_w_gu[i], ffn_w_down[i])
        if need_ctx:
            hc = hc + mc[2] * yc
            hc = hc + mc[5] * swiglu(modulate(rms_norm(hc, norm_ffn_g[i]), mc[3], mc[4]), ffn_w_gu[i], ffn_w_down[i])
    return rms_norm(h, final_norm_g)


_drawn_inputs = setup_inputs


def setup_inputs(seed=0):
    import zlib

    import numpy as np

    out = dict(_drawn_inputs(seed))
    spreads = {}
    factors = {'norm_mix_g': 6.494,
     'norm_ffn_g': 26.254,
     'hg_out_norm_g': 56.269,
     'hy_short_b': 8.0,
     'hy_filt_w1': 3.248,
     'hy_filt_b1': 8.0,
     'hy_filt_freq1': 8.0,
     'hy_filt_w2': 3.142,
     'hy_filt_b2': 8.0,
     'hy_filt_freq2': 8.0,
     'hy_filt_w3': 3.367,
     'da_lambda': 5.272,
     'da_subln_g': 200.0,
     'mla_q_norm_g': 155.504,
     'mla_w_uq': 3.246,
     'mla_kv_norm_g': 180.465,
     'final_norm_g': 7.393}
    for name, (base, spread) in spreads.items():
        noise = np.random.default_rng([zlib.crc32(name.encode()), seed]).standard_normal(out[name].shape)
        drawn = base * np.exp(spread * noise) if base else spread * noise
        out[name] = jnp.asarray(drawn.astype(out[name].dtype))
    for name, factor in factors.items():
        out[name] = (out[name] * factor).astype(out[name].dtype)
    return out
```

```python
import math
from contextlib import ExitStack

import numpy as np

import concourse.bass as bass
from concourse import mybir

F32 = mybir.dt.float32
F32R = mybir.dt.float32r
ALU = mybir.AluOpType
ACT = mybir.ActivationFunctionType
AX = mybir.AxisListType

P = 128
D = 1024
KT = D // P
LAT, CTX = 1024, 256
TOK = LAT + CTX
NT = TOK // P
LT = LAT // P
CT = CTX // P
EPS = 1e-6
FFN = ((8 * D + 3 * 256 - 1) // (3 * 256)) * 256
FT = FFN // P
FG = FT // 2
EVEN_IN = 4096
ODD_MAIN = 15
GRID_W = 64
ROPE_BASE = 10000.0
HW = 512
HY_EMB, HY_F = 33, 64
LAM_INIT = 0.8 - 0.6 * math.exp(-0.3)
HALF = 64
LEVELS = 7
MAGIC = 12582912.0
TWO_PI_A = 6.28125
TWO_PI_B = float(np.float32(np.float64(2 * math.pi) - 6.28125))
TWO_PI_C = float(np.float32(2 * math.pi - 6.28125 - np.float64(np.float32(2 * math.pi - 6.28125))))
PI_CLAMP = 3.1415925

V1_ADA, V1_C, V1_CC, V1_FIN = 0, 96, 104, 112
V1_ROWS = 120
V2_MIX, V2_FFN, V2_SW, V2_SB, V2_SKIP, V2_HG, V2_SUB, V2_QN, V2_KVN = 0, 16, 32, 68, 80, 84, 85, 86, 88
V2_ROWS = 89

FULL_CHUNKS = [(0, 512), (512, 512), (1024, 256)]
LAT_CHUNKS = [(0, 512), (512, 512)]

GEMMS = [("in0", 32), ("out0", 8), ("ffn0", 6 * FG), ("in1", 16), ("out1", 8), ("ffn1", 6 * FG)]
SLAB0, USE0 = {}, {}
_s = _u = 0
for _n, _k in GEMMS:
    SLAB0[_n], USE0[_n] = _s, _u
    _s += _k
    _u += 12 * FG if _n.startswith("ffn") else _k
PHASES = [("load", 2), ("ada", 3), ("norm0", 3), ("in0", 2), ("hyena", 3), ("hgrn", 3), ("mix0", 2), ("out0", 2),
          ("normf0", 3), ("ffn0", 3), ("norm1", 3), ("in1", 2), ("attn", 3), ("mix1", 2), ("out1", 2),
          ("normf1", 3), ("ffn1", 3), ("final", 3)]
BEFORE = {}
_c = 0
for _n, _k in PHASES:
    BEFORE[_n] = _c
    _c += _k


def constants():
    f = np.float32
    out = {"ident": np.eye(P, dtype=f)}
    s, t = np.meshgrid(np.arange(P), np.arange(P), indexing="ij")
    masks = [(s // (2 << l) == t // (2 << l)) & ((s >> l) % 2 != (t >> l) % 2) for l in range(LEVELS)]
    out["levelmask"] = np.stack([np.eye(P, dtype=bool)] + masks, 1).astype(f)
    pos, negt, negts = [], [], []
    for L in (LAT, CTX):
        tt = np.linspace(0.0, 1.0, L, dtype=f)[:, None]
        w = (2.0 * math.pi * np.arange(L, dtype=f)[:, None] / L).astype(f)
        bands = np.linspace(1e-4, 15, 16, dtype=f)[None, :]
        pos.append(np.concatenate([tt, np.cos(bands * w), -np.sin(bands * w)], -1).astype(f).T)
        negt.append(-tt[:, 0])
        negts.append(-np.concatenate([tt[:1, 0], tt[:-1, 0]]))
    out["pos"] = np.ascontiguousarray(np.concatenate(pos, 1))
    out["negt"] = np.ascontiguousarray(
        np.stack([np.concatenate(negt).reshape(NT, P).T, np.concatenate(negts).reshape(NT, P).T], 1)).astype(f)
    out["delta"] = np.linspace(-math.log(1e-2) / 1.5, -math.log(1e-2) / 0.3, HW, dtype=f)
    for name, L in (("lat", LAT), ("ctx", CTX)):
        n = L // P
        i = np.arange(L, dtype=np.int64)
        ang = math.pi / (2 * L) * (np.outer(i, 2 * i + 1) % (4 * L))
        c, sn = np.cos(ang).astype(f), np.sin(ang).astype(f)
        cs = np.stack([c, sn])
        out["dft_" + name] = np.ascontiguousarray(
            cs.reshape(2, n, P, n, P).transpose(3, 2, 0, 1, 4).reshape(n, P, 2, n * P))
        inv = np.stack([c.T, -sn.T])
        w = min(512, L)
        out["inv_" + name] = np.ascontiguousarray(
            inv.reshape(2, n, P, L // w, w).transpose(3, 1, 2, 0, 4))
    tok = np.arange(LAT)
    row, col = tok // GRID_W, tok % GRID_W

    def rope(width):
        half = width // 2
        q = half // 2
        inv = (ROPE_BASE ** (-np.arange(q, dtype=f) / q)).astype(f)
        cos, sin = np.zeros((width, LAT), f), np.zeros((width, LAT), f)
        rot = np.zeros((width, width), f)
        for part, where in enumerate((row, col)):
            ang = inv[:, None] * where[None].astype(f)
            for a in range(2):
                r = part * half + a * q
                cos[r:r + q], sin[r:r + q] = np.cos(ang), np.sin(ang)
            for d in range(q):
                x1, x2 = part * half + d, part * half + q + d
                rot[x2, x1] = -1.0
                rot[x1, x2] = 1.0
        return cos, sin, rot

    c, sn, r = rope(64)
    out["rope_da"] = np.ascontiguousarray(np.stack([np.tile(c, (2, 1)), np.tile(sn, (2, 1))], 1))
    out["rot_da"] = np.kron(np.eye(2, dtype=f), r)
    c, sn, r = rope(32)
    cc = np.concatenate([np.ones((64, LAT), f), c])
    ss = np.concatenate([np.zeros((64, LAT), f), sn])
    out["rope_mla"] = np.ascontiguousarray(np.stack([cc, ss], 1))
    rot = np.zeros((96, 96), f)
    rot[64:, 64:] = r
    out["rot_mla"] = rot
    return out


class Steps:

    def __init__(self, eng, sem):
        self.eng, self.sem, self.base, self.k = eng, sem, 0, 0

    def done(self, ins):
        ins.then_inc(self.sem, 1)
        self.k += 1

    def settle(self):
        self.eng.wait_ge(self.sem, self.base + self.k)

    def link(self, ins):
        self.done(ins)
        self.settle()

    def enter(self, i, per):
        self.saved, self.per = self.base + self.k, per
        self.base, self.k = self.saved + i * per, 0

    def leave(self, n):
        assert self.k == self.per, (self.k, self.per)
        self.base, self.k = self.saved + n * self.per, 0


SCRATCH = {"zT": (32, P, TOK), "mixT": (KT, P, TOK), "uT": (4, P, TOK + 4)}


def build(nc, T, out, scratch):
    with ExitStack() as ctx:
        def sem(name):
            return ctx.enter_context(nc.semaphore(name))

        fence = ctx.enter_context(nc.sbuf_tensor("fence", [P, 212000 - 128], mybir.dt.uint8))
        START = 16512
        END = START + 212000 - 256
        size = {F32: 4, F32R: 4}

        class Area:
            def __init__(self, at):
                self.at = at

            def __call__(self, name, shape, dt=F32):
                n = int(np.prod(shape[1:])) * size[dt]
                t = nc.alloc_sbuf_tensor_at(name, shape, dt, offset=self.at)
                self.at += (n + 31) // 32 * 32
                assert self.at <= END, (name, self.at - END)
                return t

        keep = Area(START)
        XT = keep("XT", [P, KT, TOK])
        raw = [keep(f"raw{b}", [P, KT, P]) for b in range(2)]
        WH = [keep(f"WH{b}", [P, KT, P], F32R) for b in range(2)]
        WL = [keep(f"WL{b}", [P, KT, P], F32R) for b in range(2)]
        ident = keep("ident", [P, P])
        ones = keep("ones", [P, P])
        vc1 = keep("vc1", [P, V1_ROWS])
        vc2 = keep("vc2", [P, V2_ROWS])
        mod = keep("mod", [P, 96, 2])
        gsc = keep("gsc", [P, 4, KT, 2])
        one_p = keep("one_p", [P, KT])
        csc = keep("csc", [P, KT, 2])
        lam = keep("lam", [P, 8])
        fcol = keep("fcol", [HY_F, 4])
        AREA = keep.at
        a = Area(AREA)
        AH = a("AH", [P, KT, TOK], F32R)
        AL = a("AL", [P, KT, TOK], F32R)
        AREA_B = a.at

        PS = [ctx.enter_context(nc.psum_tensor(f"PS{b}", [P, 1536], F32)) for b in range(2)]
        PM = ctx.enter_context(nc.psum_tensor("PM", [P, 1024], F32))

        one_there = sem("one_there")
        phase_done = sem("phase_done")
        raw_full = [sem(f"raw_full{b}") for b in range(2)]
        high_done = [sem(f"high_done{b}") for b in range(2)]
        w_ready = [sem(f"w_ready{b}") for b in range(2)]
        acc_full = [sem(f"acc_full{b}") for b in range(2)]
        acc_free = [sem(f"acc_free{b}") for b in range(2)]
        dve_step, act_step, pe_step = sem("dve_step"), sem("act_step"), sem("pe_step")

        def enter(eng, name):
            if BEFORE[name]:
                eng.wait_ge(phase_done, BEFORE[name])

        def leave(eng, last=None):
            eng.sem_inc(phase_done, 1)

        zT, mixT = scratch["zT"], scratch["mixT"]
        uT_s = scratch["uT"]

        def slab_in(w, k_rows=D):
            return w.rearrange("(k p) n -> p k n", p=P)

        w_src = {
            "in0": slab_in(T["ev_w_in"][0]), "out0": slab_in(T["ev_w_out"][0]),
            "in1": slab_in(T["od_w_in"][0]), "out1": slab_in(T["od_w_out"][0]),
            "gu0": slab_in(T["ffn_w_gu"][0]), "gu1": slab_in(T["ffn_w_gu"][1]),
        }
        down = [T["ffn_w_down"][l].rearrange("(g j p) n -> g p j n", j=2, p=P) for l in range(2)]

        def sp_slab(sp, n, src, dst=None):
            b, use = n
            sp.wait_ge(w_ready[b], use)
            sp.dma_start(raw[b][:] if dst is None else dst(b), src).then_inc(raw_full[b], 16)

        def sp_linear(sp, name, src, slabs):
            base = SLAB0[name] // 2
            with sp.Fori(0, slabs // 2) as i:
                for b in range(2):
                    sp_slab(sp, (b, base + i), src[:, :, bass.ds(i * (2 * P) + b * P, P)])

        def sp_ffn(sp, l):
            base = SLAB0[f"ffn{l}"] // 2
            gu = w_src[f"gu{l}"]

            def up(i, at):
                for j in range(2):
                    for half in range(2):
                        sp_slab(sp, (half, at + j), gu[:, :, bass.ds(i * 256 + (half * FFN + j * P), P)])

            def dn(i, at):
                for b in range(2):
                    sp_slab(sp, (b, at), down[l][i, :, :, b * 512:(b + 1) * 512],
                            lambda b: raw[b][:].rearrange("p (j a) c -> p j (a c)", j=2))

            up(0, base)
            with sp.Fori(0, FG - 1) as i:
                up(i + 1, base + 2 + i * 3)
                dn(i, base + 4 + i * 3)
            dn(FG - 1, base + 2 + 3 * (FG - 1))

        def pool_slab(pool, b, n, freed):
            pool.wait_ge(raw_full[b], 16 * (n + 1) if isinstance(n, int) else n * 16 + 16)
            pool.wait_ge(*freed)
            pool.tensor_tensor(WH[b][:], raw[b][:], one_p[:].unsqueeze(2).broadcast_to([P, KT, P]),
                               ALU.mult).then_inc(high_done[b], 1)
            pool.wait_ge(high_done[b], n + 1)
            pool.tensor_tensor(WL[b][:], raw[b][:], WH[b][:].bitcast(F32), ALU.subtract).then_inc(w_ready[b], 1)

        def pool_linear(pool, name):
            base, use = SLAB0[name] // 2, USE0[name] // 2
            with pool.Fori(0, dict(GEMMS)[name] // 2) as i:
                for b in range(2):
                    pool_slab(pool, b, base + i, (acc_full[b], use + i))

        def pool_ffn(pool, l):
            s, u = SLAB0[f"ffn{l}"] // 2, USE0[f"ffn{l}"] // 2

            def up(s, u, after_down):
                for j in range(2):
                    for b in range(2):
                        freed = (acc_full[1], u - 2) if after_down and (j, b) == (0, 0) else (acc_full[b], u + j)
                        pool_slab(pool, b, s + j, freed)

            def dn(s, u, after_down):
                for b in range(2):
                    pool_slab(pool, b, s, (acc_full[1], u - 2) if after_down and b == 0 else (acc_full[b], u))

            up(s, u, False)
            up(s + 2, u + 2, False)
            dn(s + 4, u + 4, False)
            with pool.Fori(1, FG - 1) as i:
                up(s + 2 + i * 3, u + 2 + i * 6, True)
                dn(s + 4 + i * 3, u + 4 + i * 6, False)
            dn(s + 2 + 3 * (FG - 1), u + 2 + 6 * (FG - 1), True)

        def products(pe, acc, chunks, kts, wh, wl, xh, xl):
            last = len(kts) - 1
            for n, k in enumerate(kts):
                for m, (w, x) in enumerate(((wh, xh), (wh, xl), (wl, xh))):
                    for at, width in chunks:
                        ins = pe.matmul(acc[:, at:at + width], w(k), x(k, at, width),
                                        start=(n == 0 and m == 0), stop=(n == last and m == 2),
                                        skip_group_check=True)
            return ins

        def full_slab(pe, b, chunks):
            return products(pe, PS[b], chunks, range(KT),
                            lambda k: WH[b][:, k, :], lambda k: WL[b][:, k, :],
                            lambda k, at, w: AH[:, k, at:at + w], lambda k, at, w: AL[:, k, at:at + w])

        def pe_linear(pe, name, slabs, chunks):
            base, use = SLAB0[name] // 2, USE0[name] // 2
            with pe.Fori(0, slabs // 2) as i:
                for b in range(2):
                    pe.wait_ge(w_ready[b], base + i + 1)
                    pe.wait_ge(acc_free[b], use + i)
                    full_slab(pe, b, chunks).then_inc(acc_full[b], 1)
            for b in range(2):
                pe.wait_ge(acc_full[b], use + slabs // 2)

        nb = Area(AREA_B)
        nsq = [nb(f"nsq{b}", [P, TOK]) for b in range(2)]
        ntmp = [nb(f"ntmp{b}", [P, TOK]) for b in range(2)]
        nhn = [nb(f"nhn{b}", [P, TOK]) for b in range(2)]
        nrs = nb("nrs", [P, TOK])
        s_sq = [sem(f"s_sq{b}") for b in range(2)]
        s_ss = sem("s_ss")
        s_ssum = sem("s_ssum")
        s_root = sem("s_root")
        s_scaled = sem("s_scaled")
        s_hn = sem("s_hn")
        s_low = sem("s_low")
        NORMS = ["norm0", "normf0", "norm1", "normf1", "final"]

        def norm_chunks(name):
            return LAT_CHUNKS if name in ("normf1", "final") else FULL_CHUNKS

        def norm_pe(pe, name):
            enter(pe, name)
            z = NORMS.index(name)
            for k in range(KT):
                pe.wait_ge(s_sq[k % 2], 4 * z + k // 2 + 1)
                for at, w in norm_chunks(name):
                    ins = pe.matmul(PS[0][:, at:at + w], ones[:], nsq[k % 2][:, at:at + w], start=(k == 0),
                                    stop=(k == KT - 1), skip_group_check=True)
                ins.then_inc(s_ss, 1)
            pe.wait_ge(s_ss, KT * (z + 1))
            leave(pe)

        def norm_act(act, st, name, split=True):
            enter(act, name)
            z = NORMS.index(name)
            n = LAT if len(norm_chunks(name)) == 2 else TOK
            for k in range(KT):
                if k >= 2:
                    act.wait_ge(s_ss, KT * z + k - 1)
                act.activation(nsq[k % 2][:, :n], XT[:, k, :n], ACT.Square).then_inc(s_sq[k % 2], 1)
            act.wait_ge(s_ss, KT * (z + 1))
            act.activation(nrs[:, :n], PS[0][:, :n], ACT.Sqrt, bias=eps_col[:, 0:1], scale=1.0 / D).then_inc(s_root, 1)
            if not split:
                act.wait_ge(s_root, z + 1)
                return
            l = 0 if name in ("norm0", "normf0") else 1
            which = 0 if name in ("norm0", "norm1") else 1
            g, shift = l * 2 + which, l * 48 + which * 24
            for k in range(KT):
                act.wait_ge(s_scaled, KT * z + k + 1)
                if k >= 2:
                    act.wait_ge(s_low, KT * z + k - 1)
                for seg in range(2 if n == TOK else 1):
                    at, w = ((0, LAT), (LAT, CTX))[seg]
                    st.done(act.activation(nhn[k % 2][:, at:at + w], ntmp[k % 2][:, at:at + w], ACT.Identity,
                                           bias=mod[:, shift + k, seg:seg + 1], scale=gsc[:, g, k, seg:seg + 1]))
                st.settle()
                act.activation(AH[:, k, :n], nhn[k % 2][:, :n], ACT.Copy).then_inc(s_hn, 1)
            act.wait_ge(s_hn, KT * (z + 1))
            leave(act)

        def norm_dve(dve, st, name):
            enter(dve, name)
            z = NORMS.index(name)
            n = LAT if len(norm_chunks(name)) == 2 else TOK
            dve.wait_ge(s_root, z + 1)
            st.link(dve.reciprocal(nrs[:, :n], nrs[:, :n]))

            def scale(k):
                if k >= 2:
                    dve.wait_ge(s_hn, KT * z + k - 1)
                dve.tensor_tensor(ntmp[k % 2][:, :n], XT[:, k, :n], nrs[:, :n], ALU.mult).then_inc(s_scaled, 1)

            def low(k):
                dve.wait_ge(s_hn, KT * z + k + 1)
                dve.tensor_tensor(AL[:, k, :n], nhn[k % 2][:, :n], AH[:, k, :n].bitcast(F32),
                                  ALU.subtract).then_inc(s_low, 1)

            scale(0)
            for k in range(KT):
                if k + 1 < KT:
                    scale(k + 1)
                low(k)
            dve.wait_ge(s_low, KT * (z + 1))
            leave(dve)

        eps_col = keep_eps = nc.alloc_sbuf_tensor_at("eps_col", [P, 1], F32, offset=END)

        lb_ = Area(AREA_B)
        xs = [lb_(f"xs{b}", [P, D]) for b in range(2)]
        vr1 = lb_("vr1", [V1_ROWS, P])
        vr2 = lb_("vr2", [V2_ROWS, P])
        lrow = lb_("lrow", [P, 4, HALF])
        lprod = lb_("lprod", [P, 2, HALF])
        const_full = sem("const_full")
        xs_full = [sem(f"xs_full{b}") for b in range(2)]
        xs_turned = [sem(f"xs_turned{b}") for b in range(2)]
        xt_there = [sem(f"xt_there{b}") for b in range(2)]
        vec_turned = sem("vec_turned")
        once = sem("once")
        x_rows = T["x"].rearrange("a (t p) d -> (a t) p d", p=P)
        ctx_rows = T["ctx"].rearrange("a (t p) d -> (a t) p d", p=P)

        def rows(ap):
            return ap.rearrange("(r p) -> r p", p=P)

        def load_sp(sp):
            n = 0

            def ld(dst, src):
                nonlocal n
                sp.dma_start(dst, src).then_inc(const_full, 16)
                n += 1

            ld(ident[:], T["ident"])
            ld(vr1[V1_ADA:V1_ADA + 96, :], T["ada_b"].rearrange("l (r p) -> (l r) p", p=P))
            ld(vr1[V1_C:V1_C + 8, :], T["c"].rearrange("a (r p) -> (a r) p", p=P))
            ld(vr1[V1_CC:V1_CC + 8, :], rows(T["c_ctx"]))
            ld(vr1[V1_FIN:V1_FIN + 8, :], rows(T["final_norm_g"]))
            ld(vr2[V2_MIX:V2_MIX + 16, :], T["norm_mix_g"].rearrange("l (r p) -> (l r) p", p=P))
            ld(vr2[V2_FFN:V2_FFN + 16, :], T["norm_ffn_g"].rearrange("l (r p) -> (l r) p", p=P))
            ld(vr2[V2_SW:V2_SW + 36, :], T["hy_short_w"].rearrange("a l (r p) -> (a l r) p", p=P))
            ld(vr2[V2_SB:V2_SB + 12, :], T["hy_short_b"].rearrange("a (r p) -> (a r) p", p=P))
            ld(vr2[V2_SKIP:V2_SKIP + 4, :], T["hy_skip"].rearrange("a (r p) -> (a r) p", p=P))
            ld(vr2[V2_HG:V2_HG + 1, :], T["hg_out_norm_g"])
            ld(vr2[V2_SUB:V2_SUB + 1, :], T["da_subln_g"])
            ld(vr2[V2_QN:V2_QN + 2, :], T["mla_q_norm_g"].rearrange("a (r p) -> (a r) p", p=P))
            ld(vr2[V2_KVN:V2_KVN + 1, :], T["mla_kv_norm_g"])
            ld(lrow[:], T["da_lambda"][0].partition_broadcast(P))
            for j, name in enumerate(("hy_filt_b1", "hy_filt_freq1", "hy_filt_b2", "hy_filt_freq2")):
                ld(fcol[:, j:j + 1], T[name].rearrange("a f -> f a"))
            assert n == N_CONST

            def tile(b, use, src):
                sp.wait_ge(xs_turned[b], use)
                sp.dma_start(xs[b][:], src).then_inc(xs_full[b], 16)

            with sp.Fori(0, LT // 2) as i:
                for b in range(2):
                    tile(b, i, x_rows[i * 2 + b])
            for b in range(2):
                tile(b, LT // 2, ctx_rows[b])

        N_CONST = 19

        def load_pe(pe):
            pe.wait_ge(const_full, 16 * N_CONST)
            pe.transpose(PM[:, 0:V1_ROWS], vr1[:], ident[:V1_ROWS, :V1_ROWS])
            pe.transpose(PM[:, 128:128 + V2_ROWS], vr2[:], ident[:V2_ROWS, :V2_ROWS]).then_inc(vec_turned, 1)

            def tile(b, use):
                pe.wait_ge(xs_full[b], 16 * (use + 1))
                pe.wait_ge(xt_there[b], use)
                for k in range(KT):
                    ins = pe.transpose(PS[b][:, k * P:(k + 1) * P], xs[b][:, k * P:(k + 1) * P], ident[:])
                ins.then_inc(xs_turned[b], 1)

            with pe.Fori(0, NT // 2) as i:
                for b in range(2):
                    tile(b, i)
            for b in range(2):
                pe.wait_ge(xs_turned[b], NT // 2)
            leave(pe)

        def load_dve(dve, st):
            st.link(dve.memset(ones[:], 1.0))
            st.link(dve.memset(eps_col[:], EPS))
            dve.wait_ge(vec_turned, 1)
            st.link(dve.tensor_copy(vc1[:], PM[:, 0:V1_ROWS]))
            st.link(dve.tensor_copy(vc2[:], PM[:, 128:128 + V2_ROWS]))
            st.link(dve.tensor_tensor(lprod[:, 0, :], lrow[:, 0, :], lrow[:, 1, :], ALU.mult))
            st.link(dve.tensor_tensor(lprod[:, 1, :], lrow[:, 2, :], lrow[:, 3, :], ALU.mult))
            st.link(dve.tensor_reduce(lam[:, 0:2], lprod[:], AX.X, ALU.add))
            with dve.Fori(0, NT // 2) as i:
                for b in range(2):
                    dve.wait_ge(xs_turned[b], i + 1)
                    dve.tensor_copy(XT[:, :, bass.ds(i * (2 * P) + b * P, P)],
                                    PS[b][:, 0:D].rearrange("p (k c) -> p k c", c=P)).then_inc(xt_there[b], 1)
            for b in range(2):
                dve.wait_ge(xt_there[b], NT // 2)
            leave(dve)

        ab = Area(AREA)
        NADA = 4
        aw = [ab(f"aw{b}", [P, KT, 256]) for b in range(NADA)]
        aw_full = [sem(f"aw_full{b}") for b in range(NADA)]
        aw_used = [sem(f"aw_used{b}") for b in range(NADA)]
        csc_there = sem("csc_there")
        ada_w = T["ada_w"].rearrange("l (k p) n -> l p k n", p=P)
        PER = 6 * D // 256 // NADA

        def ada_sp(sp):
            for l in range(2):
                with sp.Fori(0, PER) as i:
                    for b in range(NADA):
                        sp.wait_ge(aw_used[b], l * PER + i)
                        sp.dma_start(aw[b][:], ada_w[l][:, :, bass.ds(i * (NADA * 256) + b * 256, 256)]).then_inc(aw_full[b], 16)

        def ada_act(act, st):
            enter(act, "ada")
            st.done(act.activation(csc[:, :, 0], vc1[:, V1_C:V1_C + 8], ACT.Silu))
            st.done(act.activation(csc[:, :, 1], vc1[:, V1_CC:V1_CC + 8], ACT.Silu))
            st.settle()
            act.sem_inc(csc_there, 1)
            st.link(act.activation(lam[:, 2:4], lam[:, 0:2], ACT.Exp))
            leave(act)

        def ada_pe(pe):
            enter(pe, "ada")
            pe.wait_ge(csc_there, 1)
            with pe.Fori(0, 2 * PER) as i:
                for b in range(NADA):
                    pe.wait_ge(aw_full[b], 16 * (i + 1))
                    for j in range(2):
                        for k in range(KT):
                            ins = pe.matmul(PM[:, bass.ds(i * (4 * NADA) + 4 * b + 2 * j, 2)], aw[b][:, k, j * P:(j + 1) * P],
                                            csc[:, k, :], start=(k == 0), stop=(k == KT - 1), skip_group_check=True)
                    ins.then_inc(aw_used[b], 1)
            for b in range(NADA):
                pe.wait_ge(aw_used[b], 2 * PER)
            leave(pe)

        def ada_dve(dve, st):
            enter(dve, "ada")
            for b in range(NADA):
                dve.wait_ge(aw_used[b], 2 * PER)
            st.link(dve.tensor_tensor(mod[:], PM[:, 0:192].rearrange("p (n c) -> p n c", c=2),
                                      vc1[:, V1_ADA:V1_ADA + 96].unsqueeze(2).broadcast_to([P, 96, 2]), ALU.add))
            for l in range(2):
                for which, v in enumerate((V2_MIX, V2_FFN)):
                    sc = l * 48 + which * 24 + 8
                    st.link(dve.scalar_tensor_tensor(
                        gsc[:, l * 2 + which], mod[:, sc:sc + 8, :], 1.0,
                        vc2[:, v + l * 8:v + l * 8 + 8].unsqueeze(2).broadcast_to([P, 8, 2]), ALU.add, ALU.mult))
            dve.wait_ge(phase_done, BEFORE["ada"] + 2)
            st.link(dve.tensor_tensor(lam[:, 4:5], lam[:, 2:3], lam[:, 3:4], ALU.subtract))
            st.link(dve.tensor_scalar(lam[:, 5:6], lam[:, 4:5], LAM_INIT, -1.0, ALU.add, ALU.mult))
            st.link(dve.tensor_scalar(lam[:, 6:7], vc2[:, V2_SUB:V2_SUB + 1], 1.0 - LAM_INIT, None, ALU.mult))
            leave(dve)

        zb = Area(AREA_B)
        zst = [zb(f"zst{b}", [P, TOK]) for b in range(2)]
        z_there = [sem(f"z_there{b}") for b in range(2)]
        z_stored = [sem(f"z_stored{b}") for b in range(2)]
        Z0 = {"in0": 0, "in1": 16}

        def spill_act(act, name, slabs):
            enter(act, name)
            use, z0 = USE0[name] // 2, Z0[name]
            with act.Fori(0, slabs // 2) as i:
                for b in range(2):
                    act.wait_ge(acc_full[b], use + i + 1)
                    act.wait_ge(z_stored[b], 16 * (z0 + i))
                    act.activation(zst[b][:], PS[b][:, 0:TOK], ACT.Copy).then_inc(acc_free[b], 1)
                    act.wait_ge(acc_free[b], use + i + 1)
                    act.dma_start(zT[i * 2 + b], zst[b][:]).then_inc(z_stored[b], 16)
            for b in range(2):
                act.wait_ge(z_stored[b], 16 * (z0 + slabs // 2))
            leave(act)

        def in_pe(pe, name, slabs):
            enter(pe, name)
            pe_linear(pe, name, slabs, FULL_CHUNKS)
            leave(pe)

        mst = zst
        m_full = [sem(f"m_full{b}") for b in range(2)]
        m_high = [sem(f"m_high{b}") for b in range(2)]
        m_low = [sem(f"m_low{b}") for b in range(2)]

        def mix_sp(sp, l, n):
            enter(sp, f"mix{l}")
            with sp.Fori(0, KT // 2) as i:
                for b in range(2):
                    sp.wait_ge(m_low[b], l * (KT // 2) + i)
                    sp.dma_start(mst[b][:, :n], mixT[i * 2 + b][:, :n]).then_inc(m_full[b], 16)

        def mix_act(act, l, n):
            enter(act, f"mix{l}")
            with act.Fori(0, KT // 2) as i:
                for b in range(2):
                    act.wait_ge(m_full[b], 16 * (l * (KT // 2) + i + 1))
                    act.activation(AH[:, i * 2 + b, :n], mst[b][:, :n], ACT.Copy).then_inc(m_high[b], 1)
            for b in range(2):
                act.wait_ge(m_high[b], (l + 1) * (KT // 2))
            leave(act)

        def mix_dve(dve, l, n):
            enter(dve, f"mix{l}")
            with dve.Fori(0, KT // 2) as i:
                for b in range(2):
                    dve.wait_ge(m_high[b], l * (KT // 2) + i + 1)
                    dve.tensor_tensor(AL[:, i * 2 + b, :n], mst[b][:, :n], AH[:, i * 2 + b, :n].bitcast(F32),
                                      ALU.subtract).then_inc(m_low[b], 1)
            for b in range(2):
                dve.wait_ge(m_low[b], (l + 1) * (KT // 2))
            leave(dve)

        res_step = sem("res_step")

        def gated_add(dve, acc, k, gate, n):
            for seg in range(2 if n == TOK else 1):
                at, w = ((0, LAT), (LAT, CTX))[seg]
                ins = dve.scalar_tensor_tensor(XT[:, k, at:at + w], acc[:, at:at + w], gate(seg), XT[:, k, at:at + w],
                                               ALU.mult, ALU.add)
            return ins

        def out_pe(pe, l):
            enter(pe, f"out{l}")
            pe_linear(pe, f"out{l}", KT, FULL_CHUNKS if l == 0 else LAT_CHUNKS)
            leave(pe)

        def out_dve(dve, l):
            enter(dve, f"out{l}")
            use = USE0[f"out{l}"] // 2
            with dve.Fori(0, KT // 2) as i:
                for b in range(2):
                    dve.wait_ge(acc_full[b], use + i + 1)
                    gated_add(dve, PS[b], i * 2 + b,
                              lambda seg: mod[:, i * 2 + (l * 48 + 16 + b), seg:seg + 1],
                              TOK if l == 0 else LAT).then_inc(acc_free[b], 1)
            for b in range(2):
                dve.wait_ge(acc_free[b], use + KT // 2)
            leave(dve)

        fb_ = Area(AREA_B)
        HH = fb_("HH", [P, 4, TOK], F32R)
        HL = fb_("HL", [P, 4, TOK], F32R)
        sg = fb_("sg", [P, TOK])
        hid = fb_("hid", [P, TOK])
        hh_there = sem("hh_there")
        hl_there = sem("hl_there")

        def ffn_n(l):
            return TOK if l == 0 else LAT

        def ffn_pe(pe, l):
            name = f"ffn{l}"
            enter(pe, name)
            chunks = FULL_CHUNKS if l == 0 else LAT_CHUNKS
            slab, use = SLAB0[name] // 2, USE0[name] // 2

            def up(s, u):
                for j in range(2):
                    for b in range(2):
                        pe.wait_ge(w_ready[b], s + j + 1)
                        pe.wait_ge(acc_free[b], u + j)
                        full_slab(pe, b, chunks).then_inc(acc_full[b], 1)

            def dn(g, par, s, u):
                pe.wait_ge(hl_there, 2 * (l * FG + g + 1))
                for q in range(2):
                    pe.wait_ge(w_ready[q], s + 1)
                    wh = WH[q][:].rearrange("p (j a) c -> p j a c", j=2)
                    wl = WL[q][:].rearrange("p (j a) c -> p j a c", j=2)
                    for a4 in range(4):
                        b = a4 % 2
                        pe.wait_ge(acc_free[b], u + 2 * q + a4 // 2)
                        products(pe, PS[b], chunks, range(2),
                                 lambda k: wh[:, k, a4, :], lambda k: wl[:, k, a4, :],
                                 lambda k, at, w: HH[:, par * 2 + k, at:at + w],
                                 lambda k, at, w: HL[:, par * 2 + k, at:at + w]).then_inc(acc_full[b], 1)

            up(slab, use)
            with pe.Fori(0, (FG - 1) // 2) as i:
                for h in range(2):
                    up(slab + 2 + 3 * h + i * 6, use + 2 + 6 * h + i * 12)
                    dn(i * 2 + h, h, slab + 4 + 3 * h + i * 6, use + 4 + 6 * h + i * 12)
            dn(FG - 1, (FG - 1) % 2, slab + 2 + 3 * (FG - 1), use + 2 + 6 * (FG - 1))
            pe.wait_ge(acc_full[1], use + 6 * FG)
            leave(pe)

        def ffn_act(act, l):
            name = f"ffn{l}"
            enter(act, name)
            use, n = USE0[name] // 2, ffn_n(l)

            def up(g, par, u):
                for j in range(2):
                    at = 2 * l * FG + g * 2 + j
                    act.wait_ge(acc_full[0], u + j + 1)
                    act.wait_ge(hl_there, at)
                    act.activation(sg[:, :n], PS[0][:, :n], ACT.Silu).then_inc(acc_free[0], 1)
                    act.wait_ge(acc_free[1], u + j + 1)
                    act.activation(HH[:, par * 2 + j, :n], hid[:, :n], ACT.Copy).then_inc(hh_there, 1)

            up(0, 0, use)
            with act.Fori(0, (FG - 1) // 2) as i:
                for h in range(2):
                    act.wait_ge(acc_full[1], use + 2 + 6 * h + i * 12)
                    up(i * 2 + h + 1, 1 - h, use + 2 + 6 * h + i * 12)
            act.wait_ge(hh_there, 2 * (l + 1) * FG)
            leave(act)

        def ffn_dve(dve, l):
            name = f"ffn{l}"
            enter(dve, name)
            use, n = USE0[name] // 2, ffn_n(l)

            def up(g, par, u):
                for j in range(2):
                    at = 2 * l * FG + g * 2 + j
                    dve.wait_ge(acc_full[1], u + j + 1)
                    dve.wait_ge(acc_free[0], u + j + 1)
                    dve.wait_ge(hl_there, at)
                    dve.tensor_tensor(hid[:, :n], sg[:, :n], PS[1][:, :n], ALU.mult).then_inc(acc_free[1], 1)
                    dve.wait_ge(hh_there, at + 1)
                    dve.tensor_tensor(HL[:, par * 2 + j, :n], hid[:, :n], HH[:, par * 2 + j, :n].bitcast(F32),
                                      ALU.subtract).then_inc(hl_there, 1)

            def dn(u):
                for k in range(KT):
                    b = k % 2
                    dve.wait_ge(acc_full[b], u + k // 2 + 1)
                    gated_add(dve, PS[b], k, lambda seg: mod[:, l * 48 + 40 + k, seg:seg + 1], n).then_inc(acc_free[b], 1)

            up(0, 0, use)
            with dve.Fori(0, (FG - 1) // 2) as i:
                for h in range(2):
                    dve.wait_ge(acc_full[1], use + 2 + 6 * h + i * 12)
                    up(i * 2 + h + 1, 1 - h, use + 2 + 6 * h + i * 12)
                    dn(use + 4 + 6 * h + i * 12)
            dn(use + 2 + 6 * (FG - 1))
            for b in range(2):
                dve.wait_ge(acc_free[b], use + 6 * FG)
            leave(dve)

        PADW = TOK + 4
        ha = Area(AREA)
        zp = [ha(f"zp{j}", [P, PADW]) for j in range(3)]
        cv = [ha(f"cv{j}", [P, PADW]) for j in range(3)]
        R1_END = ha.at
        uTok = ha("uTok", [P, NT, HW])
        Pt = ha("Pt", [P, NT, HW])
        Mt = ha("Mt", [P, NT, HW])
        Y_AT = ha.at
        Y = ha("Y", [P, 2, NT, HW])
        invn = ha("invn", [P, 2, HW])
        negt = ha("negt", [P, 2, NT])
        r1 = Area(AREA)
        dslab = [r1(f"dslab{b}", [P, 2, LT, P]) for b in range(2)]
        ftmp = [r1(f"ftmp{j}", [P, HW]) for j in range(6)]
        assert r1.at <= R1_END
        ya = Area(Y_AT)
        pos = ya("pos", [HY_EMB, TOK])
        farg = ya("farg", [HY_F, TOK])
        fint = ya("fint", [HY_F, TOK])
        h1 = ya("h1", [HY_F, TOK])
        h2p = ya("h2p", [HY_F, TOK + 2])
        w1 = ya("w1", [HY_EMB, HY_F])
        w2 = ya("w2", [HY_F, HY_F])
        w3 = ya("w3", [HY_F, 2 * HW])
        delta = ya("delta", [P, HW])
        absum = [ya(f"absum{b}", [P, HW]) for b in range(2)]
        assert ya.at <= Y_AT + 2 * NT * HW * 4
        dec = [nc.alloc_sbuf_tensor_at(f"dec{b}", [P, 2, HW], F32, offset=AREA + b * 4096) for b in range(2)]
        fa = [nc.alloc_sbuf_tensor_at(f"fa{b}", [P, HW], F32, offset=AREA + 8192 + b * 2048) for b in range(2)]
        fg = [nc.alloc_sbuf_tensor_at(f"fg{b}", [P, HW], F32, offset=AREA + 12288 + b * 2048) for b in range(2)]
        yT = nc.alloc_sbuf_tensor_at("yT", [P, 4, TOK], F32, offset=R1_END)

        hz_full, hz_used = sem("hz_full"), sem("hz_used")
        u_there, u_turned, u_stored, utok_there = sem("u_there"), sem("u_turned"), sem("u_stored"), sem("utok_there")
        filt_in, mlp_full, sin_in, sin_out = sem("filt_in"), sem("mlp_full"), sem("sin_in"), sem("sin_out")
        tap_full, dec_there, tap_read, abs_there, abs_used = (
            sem("tap_full"), sem("dec_there"), sem("tap_read"), sem("abs_there"), sem("abs_used"))
        r1_free = sem("r1_free")
        ds_full = [sem(f"ds_full{b}") for b in range(2)]
        spec_full = [sem(f"spec_full{b}") for b in range(2)]
        spec_read = [sem(f"spec_read{b}") for b in range(2)]
        is_full = [sem(f"is_full{b}") for b in range(2)]
        is_used = [sem(f"is_used{b}") for b in range(2)]
        spec_there = sem("spec_there")
        y_full, y_read = sem("y_full"), sem("y_read")
        fz_full, fz_used, fo_there, fo_stored = sem("fz_full"), sem("fz_used"), sem("fo_there"), sem("fo_stored")
        SEGS = ((0, 1, LAT), (LAT, LAT + 3, CTX))
        N_FILT = 6
        INV = [("lat", th, kk) for th in range(2) for kk in range(LT)] + [("ctx", 0, kk) for kk in range(CT)]

        def hyena_sp(sp):
            enter(sp, "hyena")
            for dst, name in ((pos, "pos"), (w1, "hy_filt_w1"), (w2, "hy_filt_w2"), (w3, "hy_filt_w3"), (negt, "negt")):
                sp.dma_start(dst[:], T[name][0] if name.startswith("hy") else T[name]).then_inc(filt_in, 16)
            sp.dma_start(delta[:], T["delta"].partition_broadcast(P)).then_inc(filt_in, 16)
            with sp.Fori(0, 4) as c:
                sp.wait_ge(hz_used, c)
                for j, tile in ((0, 24), (1, 28)):
                    for t0, p0, w in SEGS:
                        sp.dma_start(zp[j][:, p0:p0 + w], zT[c + tile][:, t0:t0 + w]).then_inc(hz_full, 16)
            sp.wait_ge(r1_free, 1)
            with sp.Fori(0, LT // 2) as i:
                for b in range(2):
                    sp.wait_ge(spec_full[b], i)
                    sp.dma_start(dslab[b][:].rearrange("p q k c -> p q (k c)"), T["dft_lat"][i * 2 + b]).then_inc(ds_full[b], 16)
            for b in range(CT):
                sp.wait_ge(spec_full[b], LT // 2)
                sp.dma_start(dslab[b][:, :, 0:CT, :].rearrange("p q k c -> p q (k c)"), T["dft_ctx"][b]).then_inc(ds_full[b], 16)
            for n, (seg, th, kk) in enumerate(INV):
                b, use = n % 2, n // 2
                sp.wait_ge(spec_full[b], LT // 2 + 1) if use == 0 else sp.wait_ge(is_used[b], use)
                w = min(512, LAT if seg == "lat" else CTX)
                flat = dslab[b][:].rearrange("p q k c -> p (q k c)")[:, 0:2 * w].rearrange("p (q w) -> p q w", q=2)
                sp.dma_start(flat, T["inv_" + seg][th, kk]).then_inc(is_full[b], 16)
            sp.wait_ge(y_read, 3)
            sp.wait_ge(r1_free, 2)
            with sp.Fori(0, 4) as c:
                sp.wait_ge(fz_used, c)
                for t0, p0, w in SEGS:
                    sp.dma_start(zp[2][:, p0:p0 + w], zT[c + 20][:, t0:t0 + w]).then_inc(fz_full, 16)
                sp.dma_start(cv[2][:], uT_s[c]).then_inc(fz_full, 16)

        def zero_pads(dve, st, bufs):
            for t in bufs:
                for c0, c1 in ((0, 1), (LAT + 1, LAT + 3), (PADW - 1, PADW)):
                    st.done(dve.memset(t[:, c0:c1], 0.0))
            st.settle()

        def short_conv(dve, st, dst, src, tile):
            inner = slice(1, PADW - 1)

            def col(tap):
                return vc2[:, V2_SW + tap * 12 + tile:V2_SW + tap * 12 + tile + 1] if isinstance(tile, int) else \
                    vc2[:, bass.ds(tile + (V2_SW + tap * 12), 1)]

            bias = vc2[:, bass.ds(tile + V2_SB, 1)]
            st.link(dve.tensor_scalar(dst[:, inner], src[:, inner], col(1), bias, ALU.mult, ALU.add))
            st.link(dve.scalar_tensor_tensor(dst[:, inner], src[:, 0:PADW - 2], col(0), dst[:, inner], ALU.mult, ALU.add))
            st.link(dve.scalar_tensor_tensor(dst[:, inner], src[:, 2:PADW], col(2), dst[:, inner], ALU.mult, ALU.add))

        def hyena_dve(dve, st):
            enter(dve, "hyena")
            zero_pads(dve, st, zp[:2] + cv[2:])
            with dve.Fori(0, 4) as c:
                st.enter(c, 7)
                dve.wait_ge(hz_full, c * 64 + 64)
                short_conv(dve, st, cv[0], zp[0], c + 4)
                short_conv(dve, st, cv[1], zp[1], c + 8)
                dve.sem_inc(hz_used, 1)
                dve.wait_ge(u_turned, c)
                dve.wait_ge(u_stored, c * 16)
                st.link(dve.tensor_tensor(cv[2][:, 1:PADW - 1], cv[0][:, 1:PADW - 1], cv[1][:, 1:PADW - 1], ALU.mult))
                dve.sem_inc(u_there, 1)
                st.leave(4)
            st.link(dve.memset(h2p[:], 0.0))
            for layer in range(2):
                dve.wait_ge(mlp_full, layer + 1)
                if layer == 0:
                    dve.wait_ge(filt_in, 16 * N_FILT)
                st.link(dve.tensor_scalar(farg[:], PS[layer][:HY_F, 0:TOK], fcol[:, 2 * layer:2 * layer + 1],
                                          fcol[:, 2 * layer + 1:2 * layer + 2], ALU.add, ALU.mult))
                st.link(dve.tensor_scalar(fint[:], farg[:], 1.0 / (2 * math.pi), MAGIC, ALU.mult, ALU.add))
                st.link(dve.tensor_scalar(fint[:], fint[:], -MAGIC, None, ALU.add))
                for part in (TWO_PI_A, TWO_PI_B, TWO_PI_C):
                    st.link(dve.scalar_tensor_tensor(farg[:], fint[:], -part, farg[:], ALU.mult, ALU.add))
                st.link(dve.tensor_scalar(farg[:], farg[:], PI_CLAMP, -PI_CLAMP, ALU.min, ALU.max))
                dve.sem_inc(sin_in, 1)
                dve.wait_ge(sin_out, layer + 1)
            dve.wait_ge(u_turned, 4)
            dve.wait_ge(u_stored, 64)
            for tt in range(NT):
                b = tt % 2
                dve.wait_ge(tap_full, tt + 1)
                dve.wait_ge(dec_there, tt + 1)
                if tt >= 2:
                    dve.wait_ge(abs_used, tt - 1)
                st.done(dve.tensor_tensor(fa[b][:], PS[b][:, 0:HW], dec[b][:, 0, :], ALU.mult))
                st.link(dve.tensor_tensor(fg[b][:], PS[b][:, HW:2 * HW], dec[b][:, 1, :], ALU.mult))
                dve.sem_inc(tap_read, 1)
                st.done(dve.tensor_tensor(Pt[:, tt, :], fa[b][:], fg[b][:], ALU.add))
                st.done(dve.tensor_tensor(Mt[:, tt, :], fg[b][:], fa[b][:], ALU.subtract))
                st.done(dve.scalar_tensor_tensor(absum[b][:], fa[b][:], -1.0, fa[b][:], ALU.mult, ALU.max))
                st.link(dve.scalar_tensor_tensor(fg[b][:], fg[b][:], -1.0, fg[b][:], ALU.mult, ALU.max))
                st.link(dve.tensor_tensor(absum[b][:], absum[b][:], fg[b][:], ALU.add))
                dve.sem_inc(abs_there, 1)
            dve.wait_ge(abs_used, NT)
            st.link(dve.reciprocal(invn[:].rearrange("p s c -> p (s c)"), PM[:]))
            for s, L in ((0, LAT), (1, CTX)):
                st.done(dve.tensor_scalar(invn[:, s, :], invn[:, s, :], 1.0 / L, None, ALU.mult))
            st.settle()
            dve.sem_inc(r1_free, 1)

            def spectrum(b, use, kk, s):
                ur, ui, fr, fi = PS[b][:, 0:512], PS[b][:, 512:1024], PS[b][:, 1024:1536], PM[:, b * 512:(b + 1) * 512]
                dve.wait_ge(spec_full[b], use + 1)
                st.done(dve.tensor_tensor(ftmp[0][:], ur, invn[:, s, :], ALU.mult))
                st.link(dve.tensor_tensor(ftmp[1][:], ui, invn[:, s, :], ALU.mult))
                st.done(dve.tensor_tensor(ftmp[2][:], ftmp[0][:], fr, ALU.mult))
                st.done(dve.tensor_tensor(ftmp[3][:], ftmp[1][:], fi, ALU.mult))
                st.done(dve.tensor_tensor(ftmp[4][:], ftmp[0][:], fi, ALU.mult))
                st.link(dve.tensor_tensor(ftmp[5][:], ftmp[1][:], fr, ALU.mult))
                dve.sem_inc(spec_read[b], 1)
                st.done(dve.tensor_tensor(Y[:, 0, kk, :], ftmp[2][:], ftmp[3][:], ALU.add))
                st.link(dve.tensor_tensor(Y[:, 1, kk, :], ftmp[4][:], ftmp[5][:], ALU.subtract))

            with dve.Fori(0, LT // 2) as i:
                st.enter(i, 16)
                for b in range(2):
                    spectrum(b, i, i * 2 + b, 0)
                st.leave(LT // 2)
            for b in range(CT):
                spectrum(b, LT // 2, LT + b, 1)
            dve.sem_inc(spec_there, 1)
            dve.wait_ge(y_full, 3)
            dve.wait_ge(y_read, 3)
            zero_pads(dve, st, zp[2:])
            dve.sem_inc(r1_free, 1)
            with dve.Fori(0, 4) as c:
                st.enter(c, 7)
                dve.wait_ge(fz_full, c * 48 + 48)
                short_conv(dve, st, cv[0], zp[2], c)
                for t0, p0, w in SEGS:
                    st.done(dve.scalar_tensor_tensor(cv[2][:, p0:p0 + w], cv[2][:, p0:p0 + w], vc2[:, bass.ds(c + V2_SKIP, 1)],
                                                     yT[:, c, t0:t0 + w], ALU.mult, ALU.add))
                st.settle()
                dve.wait_ge(fo_stored, c * 16)
                for t0, p0, w in SEGS:
                    st.done(dve.tensor_tensor(cv[1][:, t0:t0 + w], cv[2][:, p0:p0 + w], cv[0][:, p0:p0 + w], ALU.mult))
                st.settle()
                dve.sem_inc(fo_there, 1)
                dve.sem_inc(fz_used, 1)
                st.leave(4)
            leave(dve)

        def hyena_act(act, st):
            enter(act, "hyena")
            with act.Fori(0, 4) as c:
                act.wait_ge(u_there, c + 1)
                act.dma_start(uT_s[c], cv[2][:]).then_inc(u_stored, 16)
                act.wait_ge(u_turned, c + 1)
                act.activation(uTok[:, :, bass.ds(c * P, P)], PS[0][:, 0:TOK].rearrange("p (t c) -> p t c", c=P),
                               ACT.Copy).then_inc(utok_there, 1)
            act.wait_ge(filt_in, 16 * N_FILT)
            for layer in range(2):
                act.wait_ge(sin_in, layer + 1)
                if layer == 0:
                    st.link(act.activation(h1[:], farg[:], ACT.Sin))
                else:
                    st.done(act.activation(h2p[:, 1:LAT + 1], farg[:, 0:LAT], ACT.Sin))
                    st.link(act.activation(h2p[:, LAT + 2:], farg[:, LAT:], ACT.Sin))
                act.sem_inc(sin_out, 1)
            act.wait_ge(u_stored, 64)
            for tt in range(NT):
                b = tt % 2
                if tt >= 2:
                    act.wait_ge(tap_read, tt - 1)
                for s in range(2):
                    ins = act.activation(dec[b][:, s, :], delta[:], ACT.Exp, scale=negt[:, s, tt:tt + 1])
                    st.done(ins)
                st.settle()
                act.sem_inc(dec_there, 1)
            act.wait_ge(abs_used, NT)
            for n, (w, t0) in enumerate(((512, 0), (512, 512), (CTX, LAT))):
                act.wait_ge(y_full, n + 1)
                S = n % 2
                for c in range(4):
                    src = PS[S][:, c * 512:c * 512 + w] if c < 3 else PM[:, S * 512:S * 512 + w]
                    st.done(act.activation(yT[:, c, t0:t0 + w], src, ACT.Copy))
                st.settle()
                act.sem_inc(y_read, 1)
            with act.Fori(0, 4) as c:
                act.wait_ge(fo_there, c + 1)
                act.dma_start(mixT[c + 4], cv[1][:, 0:TOK]).then_inc(fo_stored, 16)
            act.wait_ge(fo_stored, 64)
            leave(act)

        def hyena_pe(pe, st):
            enter(pe, "hyena")
            with pe.Fori(0, 4) as c:
                pe.wait_ge(u_there, c + 1)
                pe.wait_ge(utok_there, c)
                for tt in range(NT):
                    at = tt * P + (1 if tt < LT else 3)
                    ins = pe.transpose(PS[0][:, tt * P:(tt + 1) * P], cv[2][:, at:at + P], ident[:])
                ins.then_inc(u_turned, 1)
            pe.wait_ge(filt_in, 16 * N_FILT)
            pe.wait_ge(utok_there, 4)
            for at, w in FULL_CHUNKS:
                ins = pe.matmul(PS[0][:HY_F, at:at + w], w1[:], pos[:, at:at + w], start=True, stop=True)
            ins.then_inc(mlp_full, 1)
            pe.wait_ge(sin_out, 1)
            for at, w in FULL_CHUNKS:
                ins = pe.matmul(PS[1][:HY_F, at:at + w], w2[:], h1[:, at:at + w], start=True, stop=True)
            ins.then_inc(mlp_full, 1)
            pe.wait_ge(sin_out, 2)

            def sums(tt):
                pe.wait_ge(abs_there, tt + 1)
                s = 0 if tt < LT else 1
                pe.matmul(PM[:, s * 512:s * 512 + HW], ones[:], absum[tt % 2][:], start=tt in (0, LT),
                          stop=tt in (LT - 1, NT - 1), skip_group_check=True).then_inc(abs_used, 1)

            for tt in range(NT):
                b = tt % 2
                if tt >= 2:
                    pe.wait_ge(tap_read, tt - 1)
                at = tt * P + (1 if tt < LT else 2)
                pe.matmul(PS[b][:, 0:HW], h2p[:, at:at + P], w3[:, 0:HW], start=True, stop=True)
                pe.matmul(PS[b][:, HW:2 * HW], h2p[:, at - 1:at - 1 + P], w3[:, HW:2 * HW], start=True,
                          stop=True).then_inc(tap_full, 1)
                if tt:
                    sums(tt - 1)
            sums(NT - 1)
            pe.wait_ge(r1_free, 1)

            def forward(b, use, tts):
                pe.wait_ge(ds_full[b], 16 * (use + 1) if isinstance(use, int) else use * 16 + 16)
                pe.wait_ge(spec_read[b], use)
                n = len(tts)
                for q, outs in ((0, ((PS[b][:, 0:512], uTok), (PS[b][:, 1024:1536], Pt))),
                                (1, ((PS[b][:, 512:1024], uTok), (PM[:, b * 512:(b + 1) * 512], Mt)))):
                    for acc, src in outs:
                        for m, tt in enumerate(tts):
                            ins = pe.matmul(acc, dslab[b][:, q, m, :], src[:, tt, :], start=(m == 0), stop=(m == n - 1),
                                            skip_group_check=True)
                ins.then_inc(spec_full[b], 1)

            with pe.Fori(0, LT // 2) as i:
                for b in range(2):
                    forward(b, i, range(LT))
            for b in range(CT):
                forward(b, LT // 2, range(LT, NT))
            pe.wait_ge(spec_there, 1)
            for n, (seg, th, kk) in enumerate(INV):
                b, use = n % 2, n // 2
                S = th
                w = min(512, LAT if seg == "lat" else CTX)
                count = LT if seg == "lat" else CT
                if seg == "ctx" and kk == 0:
                    pe.wait_ge(y_read, 1)
                pe.wait_ge(is_full[b], 16 * (use + 1))
                flat = dslab[b][:].rearrange("p q k c -> p (q k c)")
                for c in range(4):
                    acc = PS[S][:, c * 512:c * 512 + w] if c < 3 else PM[:, S * 512:S * 512 + w]
                    for q in range(2):
                        ins = pe.matmul(acc, Y[:, q, kk + (0 if seg == "lat" else LT), c * P:(c + 1) * P],
                                        flat[:, q * w:(q + 1) * w], start=(kk == 0 and q == 0),
                                        stop=(kk == count - 1 and q == 1), skip_group_check=True)
                st.link(ins) if kk == count - 1 else ins.then_inc(is_used[b], 1)
                if kk == count - 1:
                    pe.sem_inc(y_full, 1)
                    pe.sem_inc(is_used[b], 1)
            leave(pe)

        ga = Area(AREA)
        gq, gv, gg = ga("gq", [P, TOK]), ga("gv", [P, TOK]), ga("gg", [P, TOK])
        gz = ga("gz", [P, 2, TOK])
        state = nc.alloc_sbuf_tensor_at("state", [P, 2, NT, P], F32, offset=ga.at - 2 * TOK * 4)
        glog = ga("glog", [P, 2, TOK])
        kdTok = nc.alloc_sbuf_tensor_at("kdTok", [P, 2, NT, P], F32, offset=ga.at - 2 * TOK * 4)
        gcum = ga("gcum", [P, 2, TOK])
        gk = ga("gk", [P, 2, TOK])
        garg = [ga(f"garg{b}", [P, 2, TOK]) for b in range(2)]
        gqe = [ga(f"gqe{b}", [P, TOK]) for b in range(2)]
        gke = [ga(f"gke{b}", [P, TOK]) for b in range(2)]
        attn = ga("attn", [P, TOK])
        gtmp = ga("gtmp", [P, TOK])
        vTok = ga("vTok", [P, NT, P])
        keepm = ga("keepm", [P, 2, TOK])
        lmask = ga("lmask", [P, LEVELS + 1, P])
        gdec = ga("gdec", [P, 2, NT])
        NS = LEVELS + 1

        gm_full = sem("gm_full")
        gh_full, gh_used = sem("gh_full"), sem("gh_used")
        v_turned, v_tok = sem("v_turned"), sem("v_tok")
        softp, log_there, k_there = sem("softp"), sem("log_there"), sem("k_there")
        arg_there, fac_there, qk_there = sem("arg_there"), sem("fac_there"), sem("qk_there")
        step_full, step_read = sem("step_full"), sem("step_read")
        qdec_there, kdec_there, kd_turned, kd_tok = sem("qdec_there"), sem("kdec_there"), sem("kd_turned"), sem("kd_tok")
        upd_full, state_there, o_full = sem("upd_full"), sem("state_there"), sem("o_full")
        osq_there, oss_full, oroot = sem("osq_there"), sem("oss_full"), sem("oroot")
        gate_there, mo_there, mo_stored = sem("gate_there"), sem("mo_there"), sem("mo_stored")

        def halves(ap, l):
            return ap.rearrange("p (n a h) -> p n a h", a=2, h=1 << l)

        def hgrn_sp(sp):
            enter(sp, "hgrn")
            sp.dma_start(lmask[:], T["levelmask"]).then_inc(gm_full, 16)
            with sp.Fori(0, 4) as h:
                sp.wait_ge(gh_used, h)
                for dst, tile in ((gq[:], 0), (gz[:, 0, :], 4), (gz[:, 1, :], 8), (gv[:], 12), (gg[:], 16)):
                    sp.dma_start(dst, zT[h + tile]).then_inc(gh_full, 16)

        def hgrn_act(act, st):
            enter(act, "hgrn")
            with act.Fori(0, 4) as h:
                st.enter(h, 8)
                act.wait_ge(gh_full, h * 80 + 80)
                act.wait_ge(gh_used, h)
                st.link(act.activation(gk[:], gz[:], ACT.Abs))
                st.link(act.activation(gk[:], gk[:], ACT.Exp, scale=-1.0))
                act.activation(gk[:], gk[:], ACT.Ln, bias=1.0).then_inc(softp, 1)
                act.wait_ge(v_turned, h + 1)
                act.activation(vTok[:].rearrange("p n c -> p (n c)"), PS[1][:, 0:TOK], ACT.Copy).then_inc(v_tok, 1)
                act.wait_ge(log_there, h + 1)
                act.activation(gk[:], gz[:], ACT.Exp, scale=-1.0).then_inc(k_there, 1)
                for s in range(1, NS):
                    act.wait_ge(arg_there, h * LEVELS + s)
                    act.activation(garg[s % 2][:], garg[s % 2][:], ACT.Exp).then_inc(fac_there, 1)
                act.wait_ge(qk_there, h * NS + NS - 1)
                st.done(act.activation(garg[0][:], gcum[:], ACT.Exp))
                st.done(act.activation(gdec[:, 0, :], gcum[:, 0, P - 1::P], ACT.Exp))
                st.done(act.activation(gdec[:, 1, :], gcum[:, 1, 0::P], ACT.Exp))
                st.settle()
                act.sem_inc(qdec_there, 1)
                act.wait_ge(arg_there_k, h + 1)
                act.activation(garg[1][:], garg[1][:], ACT.Exp).then_inc(kdec_there, 1)
                for d in range(2):
                    act.wait_ge(kd_turned, h * 2 + d + 1)
                    act.activation(kdTok[:, d].rearrange("p n c -> p (n c)"), PS[d][:, 0:TOK], ACT.Copy).then_inc(kd_tok, 1)
                act.wait_ge(o_full, h + 1)
                st.done(act.activation(gqe[0][:], PS[0][:, 0:TOK], ACT.Square))
                st.settle()
                act.sem_inc(osq_there, 1)
                act.wait_ge(oss_full, h + 1)
                st.link(act.activation(gke[0][:], PS[1][:, 0:TOK], ACT.Sqrt, bias=eps_col[:, 0:1], scale=1.0 / P))
                act.sem_inc(oroot, 1)
                st.link(act.activation(gg[:], gg[:], ACT.Silu))
                act.sem_inc(gate_there, 1)
                act.wait_ge(mo_there, h + 1)
                act.dma_start(mixT[h], gtmp[:]).then_inc(mo_stored, 16)
                st.leave(4)
            act.wait_ge(mo_stored, 64)
            leave(act)

        arg_there_k = sem("arg_there_k")

        def hgrn_dve(dve, st):
            enter(dve, "hgrn")
            st.link(dve.memset(keepm[:], 1.0))
            st.done(dve.memset(keepm[:, 0, 0::P], 0.0))
            st.done(dve.memset(keepm[:, 1, P - 1::P], 0.0))
            st.settle()
            dve.wait_ge(gm_full, 16)
            with dve.Fori(0, 4) as h:
                st.enter(h, 4 + 1 + LEVELS * (4 + 3) + (2 * NS - 1) + 2 + 1 + 4 + 2 * (NT - 1) + 3)
                dve.wait_ge(softp, h + 1)
                st.done(dve.scalar_tensor_tensor(glog[:], gz[:], 0.0, gk[:], ALU.min, ALU.subtract))
                st.link(dve.scalar_tensor_tensor(gz[:], gz[:], 0.0, gk[:], ALU.max, ALU.add))
                dve.sem_inc(log_there, 1)
                st.done(dve.tensor_tensor_scan(gcum[:, 0, :], keepm[:, 0, :], glog[:, 0, :], 0.0, ALU.mult, ALU.add))
                st.link(dve.tensor_tensor_scan(gcum[:, 1, ::-1], keepm[:, 1, ::-1], glog[:, 1, ::-1], 0.0, ALU.mult, ALU.add))

                def args(s):
                    l = s - 1
                    shape = [P, TOK >> (l + 1), 1 << l]
                    cf, cb = halves(gcum[:, 0, :], l), halves(gcum[:, 1, :], l)
                    rf = cf[:, :, 0, (1 << l) - 1:].broadcast_to(shape)
                    rb = cb[:, :, 1, 0:1].broadcast_to(shape)
                    eq, ek = halves(garg[s % 2][:, 0, :], l), halves(garg[s % 2][:, 1, :], l)
                    st.done(dve.tensor_tensor(eq[:, :, 1, :], cf[:, :, 1, :], rf, ALU.subtract))
                    st.done(dve.tensor_tensor(eq[:, :, 0, :], cb[:, :, 0, :], rb, ALU.subtract))
                    st.done(dve.tensor_tensor(ek[:, :, 0, :], rf, cf[:, :, 0, :], ALU.subtract))
                    st.done(dve.tensor_tensor(ek[:, :, 1, :], rb, cb[:, :, 1, :], ALU.subtract))
                    st.settle()
                    dve.sem_inc(arg_there, 1)

                def factors(s):
                    l = s - 1
                    dve.wait_ge(fac_there, h * LEVELS + s)
                    if s >= 2:
                        dve.wait_ge(step_full, h * NS + s - 1)
                    ek = halves(garg[s % 2][:, 1, :], l)
                    ke = halves(gke[s % 2][:], l)
                    st.done(dve.tensor_tensor(gqe[s % 2][:], gq[:], garg[s % 2][:, 0, :], ALU.mult))
                    for d in range(2):
                        st.done(dve.tensor_tensor(ke[:, :, d, :], halves(gk[:, d, :], l)[:, :, d, :], ek[:, :, d, :], ALU.mult))
                    st.settle()
                    dve.sem_inc(qk_there, 1)

                def collect(s):
                    mask = lmask[:, s, :].unsqueeze(1).broadcast_to([P, NT, P])
                    dst = attn if s == 0 else gtmp
                    dve.wait_ge(step_full, h * NS + s + 1)
                    if s == 1:
                        dve.wait_ge(mo_stored, h * 16)
                    st.link(dve.tensor_tensor(dst[:].rearrange("p (n c) -> p n c", c=P),
                                              PS[s % 2][:, 0:TOK].rearrange("p (n c) -> p n c", c=P), mask, ALU.mult))
                    dve.sem_inc(step_read, 1)
                    if s:
                        st.link(dve.tensor_tensor(attn[:], attn[:], gtmp[:], ALU.add))

                args(1)
                dve.wait_ge(k_there, h + 1)
                st.link(dve.tensor_tensor(gke[0][:], gk[:, 0, :], gk[:, 1, :], ALU.add))
                dve.sem_inc(qk_there, 1)
                for s in range(1, NS):
                    if s + 1 < NS:
                        args(s + 1)
                    factors(s)
                    collect(s - 1)
                c4 = gcum[:].rearrange("p d (n c) -> p d n c", c=P)
                g4 = garg[1][:].rearrange("p d (n c) -> p d n c", c=P)
                st.done(dve.tensor_tensor(g4[:, 0], c4[:, 0, :, P - 1:].broadcast_to([P, NT, P]), c4[:, 0], ALU.subtract))
                st.done(dve.tensor_tensor(g4[:, 1], c4[:, 1, :, 0:1].broadcast_to([P, NT, P]), c4[:, 1], ALU.subtract))
                st.settle()
                dve.sem_inc(arg_there_k, 1)
                collect(NS - 1)
                dve.wait_ge(kdec_there, h + 1)
                st.link(dve.tensor_tensor(garg[1][:], garg[1][:], gk[:], ALU.mult))
                dve.sem_inc(kd_there, 1)
                dve.wait_ge(qdec_there, h + 1)
                for d in range(2):
                    st.done(dve.tensor_tensor(garg[0][:, d, :], garg[0][:, d, :], gq[:], ALU.mult))
                st.done(dve.memset(state[:, 0, LT, :], 0.0))
                st.done(dve.memset(state[:, 1, NT - 1, :], 0.0))
                st.settle()
                for d in range(2):
                    order = list(range(LT, NT)) + list(range(LT))
                    if d:
                        order = list(range(NT - 1, LT - 1, -1)) + list(range(LT - 1, -1, -1))
                    dve.wait_ge(upd_full, h * 2 + d + 1)
                    for n, m in zip(order, order[1:]):
                        st.link(dve.scalar_tensor_tensor(state[:, d, m, :], state[:, d, n, :], gdec[:, d, n:n + 1],
                                                         PS[d][:, n * P:(n + 1) * P], ALU.mult, ALU.add))
                dve.sem_inc(state_there, 1)
                dve.wait_ge(oroot, h + 1)
                st.link(dve.reciprocal(gke[0][:], gke[0][:]))
                st.link(dve.tensor_tensor(gtmp[:], PS[0][:, 0:TOK], gke[0][:], ALU.mult))
                dve.wait_ge(gate_there, h + 1)
                st.link(dve.scalar_tensor_tensor(gtmp[:], gtmp[:], vc2[:, V2_HG:V2_HG + 1], gg[:], ALU.mult, ALU.mult))
                dve.sem_inc(mo_there, 1)
                dve.sem_inc(gh_used, 1)
                st.leave(4)
            leave(dve)

        kd_there = sem("kd_there")

        def hgrn_pe(pe, st):
            enter(pe, "hgrn")
            with pe.Fori(0, 4) as h:
                pe.wait_ge(gh_full, h * 80 + 80)
                pe.wait_ge(gh_used, h)
                for n in range(NT):
                    ins = pe.transpose(PS[1][:, n * P:(n + 1) * P], gv[:, n * P:(n + 1) * P], ident[:])
                ins.then_inc(v_turned, 1)
                for s in range(NS):
                    pe.wait_ge(qk_there, h * NS + s + 1)
                    if s == 1:
                        pe.wait_ge(v_tok, h + 1)
                    if s >= 2:
                        pe.wait_ge(step_read, h * NS + s - 1)
                    q = gq if s == 0 else gqe[s % 2]
                    for n in range(NT):
                        c = slice(n * P, (n + 1) * P)
                        ins = pe.matmul(PS[s % 2][:, c], gke[s % 2][:, c], q[:, c], start=True, stop=True)
                    ins.then_inc(step_full, 1)
                pe.wait_ge(kd_there, h + 1)
                pe.wait_ge(step_read, h * NS + NS)
                for d in range(2):
                    for n in range(NT):
                        ins = pe.transpose(PS[d][:, n * P:(n + 1) * P], garg[1][:, d, n * P:(n + 1) * P], ident[:])
                    ins.then_inc(kd_turned, 1)
                for d in range(2):
                    pe.wait_ge(kd_tok, h * 2 + d + 1)
                    for n in range(NT):
                        ins = pe.matmul(PS[d][:, n * P:(n + 1) * P], kdTok[:, d, n, :], vTok[:, n, :], start=True, stop=True)
                    ins.then_inc(upd_full, 1)
                pe.wait_ge(state_there, h + 1)
                for n in range(NT):
                    c = slice(n * P, (n + 1) * P)
                    pe.matmul(PS[0][:, c], vTok[:, n, :], attn[:, c], start=True, stop=False)
                    pe.matmul(PS[0][:, c], state[:, 0, n, :], garg[0][:, 0, c], start=False, stop=False)
                    ins = pe.matmul(PS[0][:, c], state[:, 1, n, :], garg[0][:, 1, c], start=False, stop=True)
                ins.then_inc(o_full, 1)
                pe.wait_ge(osq_there, h + 1)
                for at, w in FULL_CHUNKS:
                    ins = pe.matmul(PS[1][:, at:at + w], ones[:], gqe[0][:, at:at + w], start=True, stop=True)
                ins.then_inc(oss_full, 1)
            pe.wait_ge(oss_full, 4)
            leave(pe)

        ta = Area(AREA)
        aq, ak, av = ta("aq", [P, TOK]), ta("ak", [P, TOK]), ta("av", [P, TOK])
        qr, kr = ta("qr", [P, LAT]), ta("kr", [P, TOK])
        arot = ta("arot", [P, TOK])
        prob = [ta(f"prob{b}", [P, TOK]) for b in range(2)]
        probT = [ta(f"probT{b}", [P, TOK]) for b in range(2)]
        vtk = ta("vtk", [P, NT, P])
        od = ta("od", [P, LT, P])
        amo = ta("amo", [P, LAT])
        rope_da, rope_mla = ta("rope_da", [P, 2, LAT]), ta("rope_mla", [96, 2, LAT])
        rot_da, rot_mla = ta("rot_da", [P, P]), ta("rot_mla", [96, 96])
        cqn, ckvn, krr = ta("cqn", [P, 2, TOK]), ta("ckvn", [P, TOK]), ta("krr", [96, TOK])
        wuq, wukv = ta("wuq", [P, 2, 96]), ta("wukv", [P, 192])
        rsum, rinv, amax, ass = ta("rsum", [P, 16]), ta("rinv", [P, 16]), ta("amax", [P, 4]), ta("ass", [P, 8])

        at_full, ah_full, ah_used = sem("at_full"), sem("ah_full"), sem("ah_used")
        rot_full, qk_rot, kctx_there = sem("rot_full"), sem("qk_rot"), sem("kctx_there")
        vt_full, vt_there = sem("vt_full"), sem("vt_there")
        s_full, s_max, p_done, t_full, pt_ready, pv_full, o_read = (
            sem("s_full"), sem("s_max"), sem("p_done"), sem("t_full"), sem("pt_ready"), sem("pv_full"), sem("o_read"))
        od_sq, od_root, od_there, od_turned, amo_stored = (
            sem("od_sq"), sem("od_root"), sem("od_there"), sem("od_turned"), sem("amo_stored"))
        lat_in, lat_sq, lat_ss, lat_root, lat_n, kr_zero, kr_rot = (
            sem("lat_in"), sem("lat_sq"), sem("lat_ss"), sem("lat_root"), sem("lat_n"), sem("kr_zero"), sem("kr_rot"))
        mq_full, mq_copied = sem("mq_full"), sem("mq_copied")
        N_TAB = 4
        DU, MU = 2 * LT, LT

        def attn_sp(sp):
            enter(sp, "attn")
            for dst, name in ((rope_da, "rope_da"), (rope_mla, "rope_mla"), (rot_da, "rot_da"), (rot_mla, "rot_mla")):
                sp.dma_start(dst[:], T[name]).then_inc(at_full, 16)
            for k in range(2):
                sp.dma_start(cqn[:, k, :], zT[12 + k]).then_inc(lat_in, 16)
            sp.dma_start(ckvn[:], zT[14]).then_inc(lat_in, 16)
            sp.wait_ge(kr_zero, 1)
            sp.dma_start(krr[64:96, :], zT[15][64:96, :]).then_inc(lat_in, 16)
            sp.wait_ge(lat_n, 1)
            with sp.Fori(0, 4) as h:
                sp.wait_ge(ah_used, h)
                sp.dma_start(aq[:], zT[h]).then_inc(ah_full, 16)
                sp.dma_start(ak[:], zT[h + 4]).then_inc(ah_full, 16)
                sp.dma_start(av[:], zT[h + 8]).then_inc(ah_full, 16)
            uq = T["mla_w_uq"][0].rearrange("(k p) n -> p k n", p=P)
            with sp.Fori(0, 4) as h:
                sp.wait_ge(ah_used, h + 4)
                sp.dma_start(wuq[:], uq[:, :, bass.ds(h * 96, 96)]).then_inc(ah_full, 16)
                sp.dma_start(wukv[:], T["mla_w_ukv"][0][:, bass.ds(h * 192, 192)]).then_inc(ah_full, 16)

        def units_pe(pe, base, n, parts):
            for i in range(n + 2):
                if i < n:
                    pe.wait_ge(p_done, base + i)
                    tt, (lo, hi) = i * LT // n, parts[i % len(parts)]
                    for at, w in FULL_CHUNKS:
                        ins = pe.matmul(PS[0][:, at:at + w], qr[lo:hi, tt * P:(tt + 1) * P], kr[lo:hi, at:at + w],
                                        start=True, stop=True)
                    ins.then_inc(s_full, 1)
                if 1 <= i <= n:
                    u = i - 1
                    pe.wait_ge(p_done, base + u + 1)
                    pe.wait_ge(pt_ready, base + u)
                    for s in range(NT):
                        ins = pe.transpose(PS[1][:, s * P:(s + 1) * P], prob[u % 2][:, s * P:(s + 1) * P], ident[:])
                    ins.then_inc(t_full, 1)
                if i >= 2:
                    u = i - 2
                    pe.wait_ge(pt_ready, base + u + 1)
                    if u >= 2:
                        pe.wait_ge(o_read, base + u - 1)
                    for s in range(NT):
                        ins = pe.matmul(PM[:, (u % 2) * 512:(u % 2) * 512 + P], probT[u % 2][:, s * P:(s + 1) * P],
                                        vtk[:, s, :], start=(s == 0), stop=(s == NT - 1))
                    ins.then_inc(pv_full, 1)

        def units_act(act, base, n, scale):
            for i in range(n + 1):
                if i < n:
                    act.wait_ge(s_max, base + i + 1)
                    if i >= 2:
                        act.wait_ge(t_full, base + i - 1)
                    act.activation(prob[i % 2][:], PS[0][:, 0:TOK], ACT.Exp, bias=amax[:, 2 + i % 2:3 + i % 2], scale=scale,
                                   accum_out=rsum[:, i:i + 1]).then_inc(p_done, 1)
                if i >= 1:
                    u = i - 1
                    act.wait_ge(t_full, base + u + 1)
                    if u >= 2:
                        act.wait_ge(pv_full, base + u - 1)
                    act.activation(probT[u % 2][:], PS[1][:, 0:TOK], ACT.Copy).then_inc(pt_ready, 1)

        def units_dve(dve, st, base, n, scale):
            diff = n == DU
            for i in range(n + 2):
                if i < n:
                    dve.wait_ge(s_full, base + i + 1)
                    if i >= 2:
                        dve.wait_ge(p_done, base + i - 1)
                    st.link(dve.tensor_reduce(amax[:, i % 2:i % 2 + 1], PS[0][:, 0:TOK], AX.X, ALU.max))
                    dve.tensor_scalar(amax[:, 2 + i % 2:3 + i % 2], amax[:, i % 2:i % 2 + 1], -scale, None,
                                      ALU.mult).then_inc(s_max, 1)
                if i >= 2:
                    u = i - 2
                    acc = PM[:, (u % 2) * 512:(u % 2) * 512 + P]
                    dve.wait_ge(pv_full, base + u + 1)
                    dve.wait_ge(p_done, base + u + 1)
                    st.link(dve.reciprocal(rinv[:, u:u + 1], rsum[:, u:u + 1]))
                    if diff and u % 2:
                        st.link(dve.tensor_tensor(rinv[:, u:u + 1], rinv[:, u:u + 1], lam[:, 5:6], ALU.mult))
                        ins = dve.scalar_tensor_tensor(od[:, u // 2, :], acc, rinv[:, u:u + 1], od[:, u // 2, :], ALU.mult, ALU.add)
                    else:
                        ins = dve.tensor_scalar(od[:, u * LT // n, :], acc, rinv[:, u:u + 1], None, ALU.mult)
                    ins.then_inc(o_read, 1)
            dve.wait_ge(o_read, base + n)

        def unit_steps(n):
            return 2 * n + (n // 2 if n == DU else 0)

        def attn_pe(pe, st):
            enter(pe, "attn")
            pe.wait_ge(at_full, 16 * N_TAB)
            for j, k in ((0, 0), (0, 1), (1, 2)):
                pe.wait_ge(lat_sq, k + 1)
                for at, w in FULL_CHUNKS:
                    ins = pe.matmul(PS[j][:, at:at + w], ones[:], (aq, ak, av)[k][:, at:at + w], start=(k != 1),
                                    stop=(k >= 1), skip_group_check=True)
            ins.then_inc(lat_ss, 1)
            for at, w in LAT_CHUNKS:
                ins = pe.matmul(PM[:96, at:at + w], rot_mla[:], krr[:, at:at + w], start=True, stop=True)
            ins.then_inc(kr_rot, 1)
            pe.wait_ge(lat_n, 1)
            with pe.Fori(0, 4) as h:
                pe.wait_ge(ah_used, h)
                pe.wait_ge(ah_full, h * 48 + 48)
                for j, src in ((0, aq), (1, ak)):
                    for at, w in LAT_CHUNKS:
                        ins = pe.matmul(PS[j][:, at:at + w], rot_da[:], src[:, at:at + w], start=True, stop=True)
                    ins.then_inc(rot_full, 1)
                pe.wait_ge(qk_rot, h * 2 + 2)
                for s in range(NT):
                    ins = pe.transpose(PS[1][:, s * P:(s + 1) * P], av[:, s * P:(s + 1) * P], ident[:])
                ins.then_inc(vt_full, 1)
                pe.wait_ge(vt_there, h + 1)
                units_pe(pe, h * DU, DU, ((0, 64), (64, P)))
                pe.wait_ge(od_there, h + 1)
                for tt in range(LT):
                    ins = pe.transpose(PS[1][:, tt * P:(tt + 1) * P], od[:, tt, :], ident[:])
                ins.then_inc(od_turned, 1)
            with pe.Fori(0, 4) as h:
                pe.wait_ge(ah_used, h + 4)
                pe.wait_ge(ah_full, h * 32 + (4 * 48 + 32))
                for at, w in LAT_CHUNKS:
                    for k in range(2):
                        ins = pe.matmul(PS[0][:96, at:at + w], wuq[:, k, :], cqn[:, k, at:at + w], start=(k == 0), stop=(k == 1))
                ins.then_inc(mq_full, 1)
                for at, w in FULL_CHUNKS:
                    ins = pe.matmul(PS[1][:64, at:at + w], wukv[:, 0:64], ckvn[:, at:at + w], start=True, stop=True)
                ins.then_inc(mq_full, 1)
                pe.wait_ge(mq_copied, h * 2 + 2)
                for at, w in LAT_CHUNKS:
                    ins = pe.matmul(PS[0][:96, at:at + w], rot_mla[:], aq[:96, at:at + w], start=True, stop=True)
                ins.then_inc(rot_full, 1)
                for s in range(NT):
                    ins = pe.matmul(PS[1][:, s * P:(s + 1) * P], ckvn[:, s * P:(s + 1) * P], wukv[:, 64:192], start=True, stop=True)
                ins.then_inc(vt_full, 1)
                pe.wait_ge(qk_rot, h + 9)
                pe.wait_ge(vt_there, h + 5)
                units_pe(pe, h * MU + 4 * DU, MU, ((0, 96),))
                pe.wait_ge(od_there, h + 5)
                for tt in range(LT):
                    ins = pe.transpose(PS[1][:, tt * P:(tt + 1) * P], od[:, tt, :], ident[:])
                ins.then_inc(od_turned, 1)
            pe.wait_ge(od_turned, 8)
            leave(pe)

        def attn_act(act, st):
            enter(act, "attn")
            for k, dst in enumerate((aq, ak, av)):
                act.wait_ge(lat_in, 64)
                act.activation(dst[:], cqn[:, k, :] if k < 2 else ckvn[:], ACT.Square).then_inc(lat_sq, 1)
            act.wait_ge(lat_ss, 1)
            st.done(act.activation(prob[0][:], PS[0][:, 0:TOK], ACT.Sqrt, bias=eps_col[:, 0:1], scale=1.0 / 256))
            st.link(act.activation(prob[1][:], PS[1][:, 0:TOK], ACT.Sqrt, bias=eps_col[:, 0:1], scale=1.0 / 128))
            act.sem_inc(lat_root, 1)
            with act.Fori(0, 4) as h:
                st.enter(h, 1)
                act.wait_ge(ah_full, h * 48 + 48)
                act.activation(kr[:, LAT:], ak[:, LAT:], ACT.Copy).then_inc(kctx_there, 1)
                act.wait_ge(vt_full, h + 1)
                act.activation(vtk[:].rearrange("p n c -> p (n c)"), PS[1][:, 0:TOK], ACT.Copy).then_inc(vt_there, 1)
                units_act(act, h * DU, DU, 64 ** -0.5)
                act.wait_ge(od_sq, h + 1)
                act.activation(ass[:], ass[:], ACT.Sqrt, bias=eps_col[:, 0:1], scale=1.0 / P).then_inc(od_root, 1)
                act.wait_ge(od_turned, h + 1)
                act.wait_ge(amo_stored, h * 16)
                st.link(act.activation(amo[:], PS[1][:, 0:LAT], ACT.Copy, scale=lam[:, 6:7]))
                act.sem_inc(ah_used, 1)
                act.dma_start(mixT[h][:, 0:LAT], amo[:]).then_inc(amo_stored, 16)
                st.leave(4)
            with act.Fori(0, 4) as h:
                st.enter(h, 1)
                act.wait_ge(mq_full, h * 2 + 1)
                act.activation(aq[:96, 0:LAT], PS[0][:96, 0:LAT], ACT.Copy).then_inc(mq_copied, 1)
                act.wait_ge(mq_full, h * 2 + 2)
                act.activation(kr[:64, :], PS[1][:64, 0:TOK], ACT.Copy).then_inc(mq_copied, 1)
                act.wait_ge(vt_full, h + 5)
                act.activation(vtk[:].rearrange("p n c -> p (n c)"), PS[1][:, 0:TOK], ACT.Copy).then_inc(vt_there, 1)
                units_act(act, h * MU + 4 * DU, MU, 96 ** -0.5)
                act.wait_ge(od_turned, h + 5)
                act.wait_ge(amo_stored, h * 16 + 64)
                st.link(act.activation(amo[:], PS[1][:, 0:LAT], ACT.Copy))
                act.sem_inc(ah_used, 1)
                act.dma_start(mixT[h + 4][:, 0:LAT], amo[:]).then_inc(amo_stored, 16)
                st.leave(4)
            act.wait_ge(amo_stored, 128)
            leave(act)

        def rotate(dve, st, dst, src, acc, tab):
            st.done(dve.tensor_tensor(arot[:acc.shape[0], 0:LAT], acc, tab[:, 1, :], ALU.mult))
            st.link(dve.tensor_tensor(dst, src, tab[:, 0, :], ALU.mult))
            return dve.tensor_tensor(dst, dst, arot[:acc.shape[0], 0:LAT], ALU.add)

        def attn_dve(dve, st):
            enter(dve, "attn")
            st.link(dve.memset(krr[:], 0.0))
            dve.sem_inc(kr_zero, 1)
            dve.wait_ge(at_full, 16 * N_TAB)
            dve.wait_ge(lat_root, 1)
            for b in range(2):
                st.link(dve.reciprocal(prob[b][:], prob[b][:]))
            for k in range(2):
                st.done(dve.scalar_tensor_tensor(cqn[:, k, :], cqn[:, k, :], vc2[:, V2_QN + k:V2_QN + k + 1], prob[0][:],
                                                 ALU.mult, ALU.mult))
            st.link(dve.scalar_tensor_tensor(ckvn[:], ckvn[:], vc2[:, V2_KVN:V2_KVN + 1], prob[1][:], ALU.mult, ALU.mult))
            dve.wait_ge(kr_rot, 1)
            st.done(dve.tensor_tensor(arot[64:96, 0:LAT], PM[64:96, :], rope_mla[64:96, 1, :], ALU.mult))
            st.link(dve.tensor_tensor(krr[64:96, 0:LAT], krr[64:96, 0:LAT], rope_mla[64:96, 0, :], ALU.mult))
            st.link(dve.tensor_tensor(krr[64:96, 0:LAT], krr[64:96, 0:LAT], arot[64:96, 0:LAT], ALU.add))
            dve.sem_inc(lat_n, 1)
            with dve.Fori(0, 4) as h:
                st.enter(h, 2 * 2 + unit_steps(DU) + 4)
                for j, (dst, src) in enumerate(((qr[:], aq), (kr[:, 0:LAT], ak))):
                    dve.wait_ge(rot_full, h * 2 + j + 1)
                    rotate(dve, st, dst, src[:, 0:LAT], PS[j][:, 0:LAT], rope_da).then_inc(qk_rot, 1)
                    dve.wait_ge(qk_rot, h * 2 + j + 1)
                dve.wait_ge(kctx_there, h + 1)
                units_dve(dve, st, h * DU, DU, 64 ** -0.5)
                flat = od[:].rearrange("p t c -> p (t c)")
                st.link(dve.tensor_tensor(arot[:, 0:LAT], flat, flat, ALU.mult))
                st.link(dve.tensor_reduce(ass[:], arot[:, 0:LAT].rearrange("p (t c) -> p t c", c=P), AX.X, ALU.add))
                dve.sem_inc(od_sq, 1)
                dve.wait_ge(od_root, h + 1)
                st.link(dve.reciprocal(ass[:], ass[:]))
                st.link(dve.tensor_tensor(od[:], od[:], ass[:].unsqueeze(2).broadcast_to([P, LT, P]), ALU.mult))
                dve.sem_inc(od_there, 1)
                st.leave(4)
            with dve.Fori(0, 4) as h:
                st.enter(h, 1 + 2 + unit_steps(MU))
                dve.wait_ge(mq_copied, h * 2 + 2)
                st.link(dve.tensor_copy(kr[64:96, :], krr[64:96, :]))
                dve.wait_ge(rot_full, h + 9)
                rotate(dve, st, qr[:96, :], aq[:96, 0:LAT], PS[0][:96, 0:LAT], rope_mla).then_inc(qk_rot, 1)
                dve.wait_ge(qk_rot, h + 9)
                units_dve(dve, st, h * MU + 4 * DU, MU, 96 ** -0.5)
                dve.sem_inc(od_there, 1)
                st.leave(4)
            leave(dve)

        oa_ = Area(AREA_B + 8 * TOK * 4)
        xo = [nc.alloc_sbuf_tensor_at(f"xo{b}", [P, KT, P], F32, offset=AREA + b * 4096) for b in range(2)]
        xrow = [nc.alloc_sbuf_tensor_at(f"xrow{b}", [P, D], F32, offset=AREA + 8192 + b * 4096) for b in range(2)]
        xo_there = [sem(f"xo_there{b}") for b in range(2)]
        xo_turned = [sem(f"xo_turned{b}") for b in range(2)]
        xrow_there = [sem(f"xrow_there{b}") for b in range(2)]
        out_stored = [sem(f"out_stored{b}") for b in range(2)]
        out_rows = out.rearrange("a (t p) d -> (a t) p d", p=P)

        def final_dve(dve, st):
            enter(dve, "final")
            dve.wait_ge(s_root, len(NORMS))
            st.link(dve.reciprocal(nrs[:, 0:LAT], nrs[:, 0:LAT]))
            with dve.Fori(0, LT // 2) as i:
                st.enter(i, 2)
                for b in range(2):
                    cols = bass.ds(i * (2 * P) + b * P, P)
                    dve.wait_ge(xo_turned[b], i)
                    st.link(dve.tensor_tensor(xo[b][:], XT[:, :, cols], nrs[:, cols].unsqueeze(1).broadcast_to([P, KT, P]), ALU.mult))
                    dve.tensor_tensor(xo[b][:], xo[b][:], vc1[:, V1_FIN:V1_FIN + KT].unsqueeze(2).broadcast_to([P, KT, P]),
                                      ALU.mult).then_inc(xo_there[b], 1)
                st.leave(LT // 2)

        def final_pe(pe):
            norm_pe(pe, "final")
            with pe.Fori(0, LT // 2) as i:
                for b in range(2):
                    pe.wait_ge(xo_there[b], i + 1)
                    pe.wait_ge(xrow_there[b], i)
                    pe.wait_ge(s_root, len(NORMS))
                    for k in range(KT):
                        ins = pe.transpose(PS[b][:, k * P:(k + 1) * P], xo[b][:, k, :], ident[:])
                    ins.then_inc(xo_turned[b], 1)

        def final_act(act, st):
            norm_act(act, st, "final", split=False)
            with act.Fori(0, LT // 2) as i:
                for b in range(2):
                    act.wait_ge(xo_turned[b], i + 1)
                    act.wait_ge(out_stored[b], i * 16)
                    act.activation(xrow[b][:], PS[b][:, 0:D], ACT.Copy).then_inc(xrow_there[b], 1)
                    act.wait_ge(xrow_there[b], i + 1)
                    act.dma_start(out_rows[i * 2 + b], xrow[b][:]).then_inc(out_stored[b], 16)
            for b in range(2):
                act.wait_ge(out_stored[b], 16 * (LT // 2))

        block = ctx.enter_context(nc.Block())

        @block.sync
        def _(sp):
            load_sp(sp)
            ada_sp(sp)
            sp_linear(sp, "in0", w_src["in0"], 32)
            hyena_sp(sp)
            hgrn_sp(sp)
            mix_sp(sp, 0, TOK)
            sp_linear(sp, "out0", w_src["out0"], KT)
            sp_ffn(sp, 0)
            sp_linear(sp, "in1", w_src["in1"], ODD_MAIN - 1)
            base = SLAB0["in1"] // 2 + (ODD_MAIN - 1) // 2
            sp_slab(sp, (0, base), w_src["in1"][:, :, (ODD_MAIN - 1) * P:ODD_MAIN * P])
            sp_slab(sp, (1, base), w_src["in1"][:, :, ODD_MAIN * P:ODD_MAIN * P + 32], lambda b: raw[b][:, :, 64:96])
            attn_sp(sp)
            mix_sp(sp, 1, LAT)
            sp_linear(sp, "out1", w_src["out1"], KT)
            sp_ffn(sp, 1)

        @block.gpsimd
        def _(pool):
            pool.memset(one_p[:], 1.0).then_inc(one_there, 1)
            pool.wait_ge(one_there, 1)
            for name, _ in GEMMS:
                if name.startswith("ffn"):
                    pool_ffn(pool, int(name[3]))
                else:
                    pool_linear(pool, name)

        @block.tensor
        def _(pe):
            st = Steps(pe, pe_step)
            load_pe(pe)
            ada_pe(pe)
            norm_pe(pe, "norm0")
            in_pe(pe, "in0", 32)
            hyena_pe(pe, st)
            hgrn_pe(pe, st)
            out_pe(pe, 0)
            norm_pe(pe, "normf0")
            ffn_pe(pe, 0)
            norm_pe(pe, "norm1")
            in_pe(pe, "in1", 16)
            attn_pe(pe, st)
            out_pe(pe, 1)
            norm_pe(pe, "normf1")
            ffn_pe(pe, 1)
            final_pe(pe)

        @block.scalar
        def _(act):
            st = Steps(act, act_step)
            ada_act(act, st)
            norm_act(act, st, "norm0")
            spill_act(act, "in0", 32)
            hyena_act(act, st)
            hgrn_act(act, st)
            mix_act(act, 0, TOK)
            norm_act(act, st, "normf0")
            ffn_act(act, 0)
            norm_act(act, st, "norm1")
            spill_act(act, "in1", 16)
            attn_act(act, st)
            mix_act(act, 1, LAT)
            norm_act(act, st, "normf1")
            ffn_act(act, 1)
            final_act(act, st)

        @block.vector
        def _(dve):
            st = Steps(dve, dve_step)
            load_dve(dve, st)
            ada_dve(dve, st)
            norm_dve(dve, st, "norm0")
            hyena_dve(dve, st)
            hgrn_dve(dve, st)
            mix_dve(dve, 0, TOK)
            out_dve(dve, 0)
            norm_dve(dve, st, "normf0")
            ffn_dve(dve, 0)
            norm_dve(dve, st, "norm1")
            attn_dve(dve, st)
            mix_dve(dve, 1, LAT)
            out_dve(dve, 1)
            norm_dve(dve, st, "normf1")
            ffn_dve(dve, 1)
            final_dve(dve, st)


_INS = ['x', 'c', 'ctx', 'c_ctx', 'ada_w', 'ada_b', 'norm_mix_g', 'norm_ffn_g', 'ffn_w_gu', 'ffn_w_down', 'ev_w_in',
        'ev_w_out', 'hg_lower_bound', 'hg_out_norm_g', 'hy_short_w', 'hy_short_b', 'hy_filt_w1', 'hy_filt_b1',
        'hy_filt_freq1', 'hy_filt_w2', 'hy_filt_b2', 'hy_filt_freq2', 'hy_filt_w3', 'hy_skip', 'od_w_in', 'od_w_out',
        'da_lambda', 'da_subln_g', 'mla_q_norm_g', 'mla_w_uq', 'mla_kv_norm_g', 'mla_w_ukv', 'final_norm_g']


def kernel(**inputs):
    import numpy as _np
    import concourse.bacc as _bacc
    from concourse import mybir as _mybir
    from concourse.bass_utils import run_bass_kernel_spmd as _run

    nc = _bacc.Bacc("TRN2", target_bir_lowering=False, num_devices=1)
    arrays, T = {}, {}
    given = {n: _np.ascontiguousarray(inputs[n]) for n in _INS}
    given.update(constants())
    for name, a in given.items():
        arrays[f"in_{name}_dram"] = a
        T[name] = nc.dram_tensor(f"in_{name}_dram", a.shape, _mybir.dt.from_np(a.dtype), kind="ExternalInput").ap()
    out = nc.dram_tensor("out_dram", (1, LAT, D), _mybir.dt.float32, kind="ExternalOutput").ap()
    scratch = {n: nc.dram_tensor(n + "_dram", s, _mybir.dt.float32, kind="Internal").ap() for n, s in SCRATCH.items()}
    build(nc, T, out, scratch)
    r = _run(nc, [arrays], core_ids=[0])
    return r.results[0]["out_dram"]
```

```python
import math
from contextlib import ExitStack

import numpy as np

import concourse.bass as bass
from concourse import mybir

F32 = mybir.dt.float32
F32R = mybir.dt.float32r
ALU = mybir.AluOpType
ACT = mybir.ActivationFunctionType
AX = mybir.AxisListType

P = 128
D = 1024
KT = D // P
LAT, CTX = 1024, 256
TOK = LAT + CTX
NT = TOK // P
LT = LAT // P
CT = CTX // P
EPS = 1e-6
FFN = ((8 * D + 3 * 256 - 1) // (3 * 256)) * 256
FT = FFN // P
FG = FT // 2
EVEN_IN = 4096
ODD_MAIN = 15
GRID_W = 64
ROPE_BASE = 10000.0
HW = 512
HY_EMB, HY_F = 33, 64
LAM_INIT = 0.8 - 0.6 * math.exp(-0.3)
HALF = 64
LEVELS = 7
MAGIC = 12582912.0
TWO_PI_A = 6.28125
TWO_PI_B = float(np.float32(np.float64(2 * math.pi) - 6.28125))
TWO_PI_C = float(np.float32(2 * math.pi - 6.28125 - np.float64(np.float32(2 * math.pi - 6.28125))))
PI_CLAMP = 3.1415925

V1_ADA, V1_C, V1_CC, V1_FIN = 0, 96, 104, 112
V1_ROWS = 120
V2_MIX, V2_FFN, V2_SW, V2_SB, V2_SKIP, V2_HG, V2_SUB, V2_QN, V2_KVN = 0, 16, 32, 68, 80, 84, 85, 86, 88
V2_ROWS = 89

FULL_CHUNKS = [(0, 512), (512, 512), (1024, 256)]
LAT_CHUNKS = [(0, 512), (512, 512)]

GEMMS = [("in0", 32), ("out0", 8), ("ffn0", 6 * FG), ("in1", 16), ("out1", 8), ("ffn1", 6 * FG)]
SLAB0, USE0 = {}, {}
_s = _u = 0
for _n, _k in GEMMS:
    SLAB0[_n], USE0[_n] = _s, _u
    _s += _k
    _u += 12 * FG if _n.startswith("ffn") else _k
PHASES = [("load", 2), ("ada", 3), ("norm0", 3), ("in0", 3), ("hyena", 3), ("hgrn", 3), ("mix0", 2), ("out0", 2),
          ("normf0", 3), ("ffn0", 3), ("norm1", 3), ("in1", 2), ("attn", 3), ("mix1", 2), ("out1", 2),
          ("normf1", 3), ("ffn1", 3), ("final", 3)]
BEFORE = {}
_c = 0
for _n, _k in PHASES:
    BEFORE[_n] = _c
    _c += _k


def constants():
    f = np.float32
    out = {"ident": np.eye(P, dtype=f)}
    s, t = np.meshgrid(np.arange(P), np.arange(P), indexing="ij")
    masks = [(s // (2 << l) == t // (2 << l)) & ((s >> l) % 2 != (t >> l) % 2) for l in range(LEVELS)]
    out["levelmask"] = np.stack([np.eye(P, dtype=bool)] + masks, 1).astype(f)
    pos, negt, negts = [], [], []
    for L in (LAT, CTX):
        tt = np.linspace(0.0, 1.0, L, dtype=f)[:, None]
        w = (2.0 * math.pi * np.arange(L, dtype=f)[:, None] / L).astype(f)
        bands = np.linspace(1e-4, 15, 16, dtype=f)[None, :]
        pos.append(np.concatenate([tt, np.cos(bands * w), -np.sin(bands * w)], -1).astype(f).T)
        negt.append(-tt[:, 0])
        negts.append(-np.concatenate([tt[:1, 0], tt[:-1, 0]]))
    out["pos"] = np.ascontiguousarray(np.concatenate(pos, 1))
    out["negt"] = np.ascontiguousarray(
        np.stack([np.concatenate(negt).reshape(NT, P).T, np.concatenate(negts).reshape(NT, P).T], 1)).astype(f)
    out["delta"] = np.linspace(-math.log(1e-2) / 1.5, -math.log(1e-2) / 0.3, HW, dtype=f)
    for name, L in (("lat", LAT), ("ctx", CTX)):
        n = L // P
        i = np.arange(L, dtype=np.int64)
        ang = math.pi / (2 * L) * (np.outer(i, 2 * i + 1) % (4 * L))
        c, sn = np.cos(ang).astype(f), np.sin(ang).astype(f)
        cs = np.stack([c, sn])
        out["dft_" + name] = np.ascontiguousarray(
            cs.reshape(2, n, P, n, P).transpose(3, 2, 0, 1, 4).reshape(n, P, 2, n * P))
        inv = np.stack([c.T, -sn.T])
        w = min(512, L)
        out["inv_" + name] = np.ascontiguousarray(
            inv.reshape(2, n, P, L // w, w).transpose(3, 1, 2, 0, 4))
    tok = np.arange(LAT)
    row, col = tok // GRID_W, tok % GRID_W

    def rope(width):
        half = width // 2
        q = half // 2
        inv = (ROPE_BASE ** (-np.arange(q, dtype=f) / q)).astype(f)
        cos, sin = np.zeros((width, LAT), f), np.zeros((width, LAT), f)
        rot = np.zeros((width, width), f)
        for part, where in enumerate((row, col)):
            ang = inv[:, None] * where[None].astype(f)
            for a in range(2):
                r = part * half + a * q
                cos[r:r + q], sin[r:r + q] = np.cos(ang), np.sin(ang)
            for d in range(q):
                x1, x2 = part * half + d, part * half + q + d
                rot[x2, x1] = -1.0
                rot[x1, x2] = 1.0
        return cos, sin, rot

    c, sn, r = rope(64)
    out["rope_da"] = np.ascontiguousarray(np.stack([np.tile(c, (2, 1)), np.tile(sn, (2, 1))], 1))
    out["rot_da"] = np.kron(np.eye(2, dtype=f), r)
    c, sn, r = rope(32)
    cc = np.concatenate([np.ones((64, LAT), f), c])
    ss = np.concatenate([np.zeros((64, LAT), f), sn])
    out["rope_mla"] = np.ascontiguousarray(np.stack([cc, ss], 1))
    rot = np.zeros((96, 96), f)
    rot[64:, 64:] = r
    out["rot_mla"] = rot
    return out


class Steps:

    def __init__(self, eng, sem):
        self.eng, self.sem, self.base, self.k = eng, sem, 0, 0

    def done(self, ins):
        ins.then_inc(self.sem, 1)
        self.k += 1

    def settle(self):
        self.eng.wait_ge(self.sem, self.base + self.k)

    def link(self, ins):
        self.done(ins)
        self.settle()

    def enter(self, i, per):
        self.saved, self.per = self.base + self.k, per
        self.base, self.k = self.saved + i * per, 0

    def leave(self, n):
        assert self.k == self.per, (self.k, self.per)
        self.base, self.k = self.saved + n * self.per, 0


SCRATCH = {"fspec": (NT, P, 2, HW), "zT": (32, P, TOK), "mixT": (KT, P, TOK), "uT": (4, P, TOK + 4)}


def build(nc, T, out, scratch):
    with ExitStack() as ctx:
        def sem(name):
            return ctx.enter_context(nc.semaphore(name))

        fence = ctx.enter_context(nc.sbuf_tensor("fence", [P, 212000 - 128], mybir.dt.uint8))
        START = 16512
        END = START + 212000 - 256
        size = {F32: 4, F32R: 4}

        class Area:
            def __init__(self, at):
                self.at = at

            def __call__(self, name, shape, dt=F32):
                n = int(np.prod(shape[1:])) * size[dt]
                t = nc.alloc_sbuf_tensor_at(name, shape, dt, offset=self.at)
                self.at += (n + 31) // 32 * 32
                assert self.at <= END, (name, self.at - END)
                return t

        keep = Area(START)
        XT = keep("XT", [P, KT, TOK])
        raw = [keep(f"raw{b}", [P, KT, P]) for b in range(2)]
        WH = [keep(f"WH{b}", [P, KT, P], F32R) for b in range(2)]
        WL = [keep(f"WL{b}", [P, KT, P], F32R) for b in range(2)]
        ident = keep("ident", [P, P])
        ones = keep("ones", [P, P])
        vc1 = keep("vc1", [P, V1_ROWS])
        vc2 = keep("vc2", [P, V2_ROWS])
        mod = keep("mod", [P, 96, 2])
        gsc = keep("gsc", [P, 4, KT, 2])
        one_p = keep("one_p", [P, KT])
        csc = keep("csc", [P, KT, 2])
        lam = keep("lam", [P, 8])
        fcol = keep("fcol", [HY_F, 4])
        AREA = keep.at
        a = Area(AREA)
        AH = a("AH", [P, KT, TOK], F32R)
        AL = a("AL", [P, KT, TOK], F32R)
        AREA_B = a.at

        ALL = ctx.enter_context(nc.psum_tensor("ALL", [P, 8 * 512], F32))
        PS = [ALL[:, b * 1536:(b + 1) * 1536] for b in range(2)]
        PM = ALL[:, 3072:4096]

        one_there = sem("one_there")
        phase_done = sem("phase_done")
        raw_full = [sem(f"raw_full{b}") for b in range(2)]
        high_done = [sem(f"high_done{b}") for b in range(2)]
        w_ready = [sem(f"w_ready{b}") for b in range(2)]
        acc_full = [sem(f"acc_full{b}") for b in range(2)]
        acc_free = [sem(f"acc_free{b}") for b in range(2)]
        dve_step, act_step, pe_step = sem("dve_step"), sem("act_step"), sem("pe_step")

        def enter(eng, name):
            if BEFORE[name]:
                eng.wait_ge(phase_done, BEFORE[name])

        def leave(eng, last=None):
            eng.sem_inc(phase_done, 1)

        zT, mixT = scratch["zT"], scratch["mixT"]
        uT_s = scratch["uT"]

        def slab_in(w, k_rows=D):
            return w.rearrange("(k p) n -> p k n", p=P)

        w_src = {
            "in0": slab_in(T["ev_w_in"][0]), "out0": slab_in(T["ev_w_out"][0]),
            "in1": slab_in(T["od_w_in"][0]), "out1": slab_in(T["od_w_out"][0]),
            "gu0": slab_in(T["ffn_w_gu"][0]), "gu1": slab_in(T["ffn_w_gu"][1]),
        }
        down = [T["ffn_w_down"][l].rearrange("(g j p) n -> g p j n", j=2, p=P) for l in range(2)]

        def sp_slab(sp, n, src, dst=None):
            b, use = n
            sp.wait_ge(w_ready[b], use)
            sp.dma_start(raw[b][:] if dst is None else dst(b), src).then_inc(raw_full[b], 16)

        def sp_linear(sp, name, src, slabs):
            base = SLAB0[name] // 2
            with sp.Fori(0, slabs // 2) as i:
                for b in range(2):
                    sp_slab(sp, (b, base + i), src[:, :, bass.ds(i * (2 * P) + b * P, P)])

        def sp_ffn(sp, l):
            base = SLAB0[f"ffn{l}"] // 2
            gu = w_src[f"gu{l}"]

            def up(i, at):
                for j in range(2):
                    for half in range(2):
                        sp_slab(sp, (half, at + j), gu[:, :, bass.ds(i * 256 + (half * FFN + j * P), P)])

            def dn(i, at):
                for b in range(2):
                    sp_slab(sp, (b, at), down[l][i, :, :, b * 512:(b + 1) * 512],
                            lambda b: raw[b][:].rearrange("p (j a) c -> p j (a c)", j=2))

            up(0, base)
            with sp.Fori(0, FG - 1) as i:
                up(i + 1, base + 2 + i * 3)
                dn(i, base + 4 + i * 3)
            dn(FG - 1, base + 2 + 3 * (FG - 1))

        def pool_slab(pool, b, n, freed):
            pool.wait_ge(raw_full[b], 16 * (n + 1) if isinstance(n, int) else n * 16 + 16)
            pool.wait_ge(*freed)
            pool.tensor_tensor(WH[b][:], raw[b][:], one_p[:].unsqueeze(2).broadcast_to([P, KT, P]),
                               ALU.mult).then_inc(high_done[b], 1)
            pool.wait_ge(high_done[b], n + 1)
            pool.tensor_tensor(WL[b][:], raw[b][:], WH[b][:].bitcast(F32), ALU.subtract).then_inc(w_ready[b], 1)

        def pool_linear(pool, name):
            base, use = SLAB0[name] // 2, USE0[name] // 2
            with pool.Fori(0, dict(GEMMS)[name] // 2) as i:
                for b in range(2):
                    pool_slab(pool, b, base + i, (acc_full[b], use + i))

        def pool_ffn(pool, l):
            s, u = SLAB0[f"ffn{l}"] // 2, USE0[f"ffn{l}"] // 2

            def up(s, u, after_down):
                for j in range(2):
                    for b in range(2):
                        freed = (acc_full[1], u - 2) if after_down and (j, b) == (0, 0) else (acc_full[b], u + j)
                        pool_slab(pool, b, s + j, freed)

            def dn(s, u, after_down):
                for b in range(2):
                    pool_slab(pool, b, s, (acc_full[1], u - 2) if after_down and b == 0 else (acc_full[b], u))

            up(s, u, False)
            up(s + 2, u + 2, False)
            dn(s + 4, u + 4, False)
            with pool.Fori(1, FG - 1) as i:
                up(s + 2 + i * 3, u + 2 + i * 6, True)
                dn(s + 4 + i * 3, u + 4 + i * 6, False)
            dn(s + 2 + 3 * (FG - 1), u + 2 + 6 * (FG - 1), True)

        def products(pe, acc, chunks, kts, wh, wl, xh, xl):
            last = len(kts) - 1
            for n, k in enumerate(kts):
                for m, (w, x) in enumerate(((wh, xh), (wh, xl), (wl, xh))):
                    for at, width in chunks:
                        ins = pe.matmul(acc[:, at:at + width], w(k), x(k, at, width),
                                        start=(n == 0 and m == 0), stop=(n == last and m == 2),
                                        skip_group_check=True)
            return ins

        def full_slab(pe, b, chunks):
            return products(pe, PS[b], chunks, range(KT),
                            lambda k: WH[b][:, k, :], lambda k: WL[b][:, k, :],
                            lambda k, at, w: AH[:, k, at:at + w], lambda k, at, w: AL[:, k, at:at + w])

        def pe_linear(pe, name, slabs, chunks):
            base, use = SLAB0[name] // 2, USE0[name] // 2
            with pe.Fori(0, slabs // 2) as i:
                for b in range(2):
                    pe.wait_ge(w_ready[b], base + i + 1)
                    pe.wait_ge(acc_free[b], use + i)
                    full_slab(pe, b, chunks).then_inc(acc_full[b], 1)
            for b in range(2):
                pe.wait_ge(acc_full[b], use + slabs // 2)

        nb = Area(AREA_B)
        nsq = [nb(f"nsq{b}", [P, TOK]) for b in range(2)]
        ntmp = [nb(f"ntmp{b}", [P, TOK]) for b in range(2)]
        nhn = [nb(f"nhn{b}", [P, TOK]) for b in range(2)]
        nrs = nb("nrs", [P, TOK])
        s_sq = [sem(f"s_sq{b}") for b in range(2)]
        s_ss = sem("s_ss")
        s_root = sem("s_root")
        s_scaled = sem("s_scaled")
        s_hn = sem("s_hn")
        s_low = sem("s_low")
        NORMS = ["norm0", "normf0", "norm1", "normf1", "final"]

        def norm_chunks(name):
            return LAT_CHUNKS if name in ("normf1", "final") else FULL_CHUNKS

        def norm_pe(pe, name):
            enter(pe, name)
            z = NORMS.index(name)
            for k in range(KT):
                pe.wait_ge(s_sq[k % 2], 4 * z + k // 2 + 1)
                for at, w in norm_chunks(name):
                    ins = pe.matmul(PS[0][:, at:at + w], ones[:], nsq[k % 2][:, at:at + w], start=(k == 0),
                                    stop=(k == KT - 1), skip_group_check=True)
                ins.then_inc(s_ss, 1)
            pe.wait_ge(s_ss, KT * (z + 1))
            leave(pe)

        def norm_act(act, st, name, split=True):
            enter(act, name)
            z = NORMS.index(name)
            n = LAT if len(norm_chunks(name)) == 2 else TOK
            for k in range(KT):
                if k >= 2:
                    act.wait_ge(s_ss, KT * z + k - 1)
                act.activation(nsq[k % 2][:, :n], XT[:, k, :n], ACT.Square).then_inc(s_sq[k % 2], 1)
            act.wait_ge(s_ss, KT * (z + 1))
            act.activation(nrs[:, :n], PS[0][:, :n], ACT.Sqrt, bias=eps_col[:, 0:1], scale=1.0 / D).then_inc(s_root, 1)
            if not split:
                act.wait_ge(s_root, z + 1)
                return
            l = 0 if name in ("norm0", "normf0") else 1
            which = 0 if name in ("norm0", "norm1") else 1
            g, shift = l * 2 + which, l * 48 + which * 24
            for k in range(KT):
                act.wait_ge(s_scaled, KT * z + k + 1)
                if k >= 2:
                    act.wait_ge(s_low, KT * z + k - 1)
                for seg in range(2 if n == TOK else 1):
                    at, w = ((0, LAT), (LAT, CTX))[seg]
                    st.done(act.activation(nhn[k % 2][:, at:at + w], ntmp[k % 2][:, at:at + w], ACT.Identity,
                                           bias=mod[:, shift + k, seg:seg + 1], scale=gsc[:, g, k, seg:seg + 1]))
                st.settle()
                act.activation(AH[:, k, :n], nhn[k % 2][:, :n], ACT.Copy).then_inc(s_hn, 1)
            act.wait_ge(s_hn, KT * (z + 1))
            leave(act)

        def norm_dve(dve, st, name):
            enter(dve, name)
            z = NORMS.index(name)
            n = LAT if len(norm_chunks(name)) == 2 else TOK
            dve.wait_ge(s_root, z + 1)
            st.link(dve.reciprocal(nrs[:, :n], nrs[:, :n]))

            def scale(k):
                if k >= 2:
                    dve.wait_ge(s_hn, KT * z + k - 1)
                dve.tensor_tensor(ntmp[k % 2][:, :n], XT[:, k, :n], nrs[:, :n], ALU.mult).then_inc(s_scaled, 1)

            def low(k):
                dve.wait_ge(s_hn, KT * z + k + 1)
                dve.tensor_tensor(AL[:, k, :n], nhn[k % 2][:, :n], AH[:, k, :n].bitcast(F32),
                                  ALU.subtract).then_inc(s_low, 1)

            scale(0)
            for k in range(KT):
                if k + 1 < KT:
                    scale(k + 1)
                low(k)
            dve.wait_ge(s_low, KT * (z + 1))
            leave(dve)

        eps_col = keep_eps = nc.alloc_sbuf_tensor_at("eps_col", [P, 1], F32, offset=END)

        lb_ = Area(AREA_B)
        xs = [lb_(f"xs{b}", [P, D]) for b in range(2)]
        vr1 = lb_("vr1", [V1_ROWS, P])
        vr2 = lb_("vr2", [V2_ROWS, P])
        lrow = lb_("lrow", [P, 4, HALF])
        lprod = lb_("lprod", [P, 2, HALF])
        const_full = sem("const_full")
        xs_full = [sem(f"xs_full{b}") for b in range(2)]
        tile_turned = [sem(f"tile_turned{b}") for b in range(2)]
        tile_read = [sem(f"tile_read{b}") for b in range(2)]
        vec_turned = sem("vec_turned")
        once = sem("once")
        x_rows = T["x"].rearrange("a (t p) d -> (a t) p d", p=P)
        ctx_rows = T["ctx"].rearrange("a (t p) d -> (a t) p d", p=P)

        def rows(ap):
            return ap.rearrange("(r p) -> r p", p=P)

        def load_sp(sp):
            n = 0

            def ld(dst, src):
                nonlocal n
                sp.dma_start(dst, src).then_inc(const_full, 16)
                n += 1

            ld(ident[:], T["ident"])
            ld(vr1[V1_ADA:V1_ADA + 96, :], T["ada_b"].rearrange("l (r p) -> (l r) p", p=P))
            ld(vr1[V1_C:V1_C + 8, :], T["c"].rearrange("a (r p) -> (a r) p", p=P))
            ld(vr1[V1_CC:V1_CC + 8, :], rows(T["c_ctx"]))
            ld(vr1[V1_FIN:V1_FIN + 8, :], rows(T["final_norm_g"]))
            ld(vr2[V2_MIX:V2_MIX + 16, :], T["norm_mix_g"].rearrange("l (r p) -> (l r) p", p=P))
            ld(vr2[V2_FFN:V2_FFN + 16, :], T["norm_ffn_g"].rearrange("l (r p) -> (l r) p", p=P))
            ld(vr2[V2_SW:V2_SW + 36, :], T["hy_short_w"].rearrange("a l (r p) -> (a l r) p", p=P))
            ld(vr2[V2_SB:V2_SB + 12, :], T["hy_short_b"].rearrange("a (r p) -> (a r) p", p=P))
            ld(vr2[V2_SKIP:V2_SKIP + 4, :], T["hy_skip"].rearrange("a (r p) -> (a r) p", p=P))
            ld(vr2[V2_HG:V2_HG + 1, :], T["hg_out_norm_g"])
            ld(vr2[V2_SUB:V2_SUB + 1, :], T["da_subln_g"])
            ld(vr2[V2_QN:V2_QN + 2, :], T["mla_q_norm_g"].rearrange("a (r p) -> (a r) p", p=P))
            ld(vr2[V2_KVN:V2_KVN + 1, :], T["mla_kv_norm_g"])
            ld(lrow[:], T["da_lambda"][0].partition_broadcast(P))
            for j, name in enumerate(("hy_filt_b1", "hy_filt_freq1", "hy_filt_b2", "hy_filt_freq2")):
                ld(fcol[:, j:j + 1], T[name].rearrange("a f -> f a"))
            assert n == N_CONST

            def tile(b, use, src):
                sp.wait_ge(tile_turned[b], use)
                sp.dma_start(xs[b][:], src).then_inc(xs_full[b], 16)

            with sp.Fori(0, LT // 2) as i:
                for b in range(2):
                    tile(b, i, x_rows[i * 2 + b])
            for b in range(2):
                tile(b, LT // 2, ctx_rows[b])

        N_CONST = 19

        def load_pe(pe):
            pe.wait_ge(const_full, 16 * N_CONST)
            pe.transpose(PM[:, 0:V1_ROWS], vr1[:], ident[:V1_ROWS, :V1_ROWS])
            pe.transpose(PM[:, 128:128 + V2_ROWS], vr2[:], ident[:V2_ROWS, :V2_ROWS]).then_inc(vec_turned, 1)

            def tile(b, use):
                pe.wait_ge(xs_full[b], 16 * (use + 1))
                pe.wait_ge(tile_read[b], use)
                for k in range(KT):
                    ins = pe.transpose(PS[b][:, k * P:(k + 1) * P], xs[b][:, k * P:(k + 1) * P], ident[:])
                ins.then_inc(tile_turned[b], 1)

            with pe.Fori(0, NT // 2) as i:
                for b in range(2):
                    tile(b, i)
            for b in range(2):
                pe.wait_ge(tile_turned[b], NT // 2)
            leave(pe)

        def load_dve(dve, st):
            st.link(dve.memset(ones[:], 1.0))
            st.link(dve.memset(eps_col[:], EPS))
            dve.wait_ge(vec_turned, 1)
            st.link(dve.tensor_copy(vc1[:], PM[:, 0:V1_ROWS]))
            st.link(dve.tensor_copy(vc2[:], PM[:, 128:128 + V2_ROWS]))
            st.link(dve.tensor_tensor(lprod[:, 0, :], lrow[:, 0, :], lrow[:, 1, :], ALU.mult))
            st.link(dve.tensor_tensor(lprod[:, 1, :], lrow[:, 2, :], lrow[:, 3, :], ALU.mult))
            st.link(dve.tensor_reduce(lam[:, 0:2], lprod[:], AX.X, ALU.add))
            with dve.Fori(0, NT // 2) as i:
                for b in range(2):
                    dve.wait_ge(tile_turned[b], i + 1)
                    dve.tensor_copy(XT[:, :, bass.ds(i * (2 * P) + b * P, P)],
                                    PS[b][:, 0:D].rearrange("p (k c) -> p k c", c=P)).then_inc(tile_read[b], 1)
            for b in range(2):
                dve.wait_ge(tile_read[b], NT // 2)
            leave(dve)

        ab = Area(AREA)
        NADA = 4
        aw = [ab(f"aw{b}", [P, KT, 256]) for b in range(NADA)]
        Pt = ab("Pt", [P, NT, HW])
        Mt = ab("Mt", [P, NT, HW])
        MLP_AT = ab.at
        pos = ab("pos", [HY_EMB, TOK])
        farg = ab("farg", [HY_F, TOK])
        fint = ab("fint", [HY_F, TOK])
        h1 = ab("h1", [HY_F, TOK])
        MLP_END = ab.at
        h2p = ab("h2p", [HY_F, TOK + 2])
        w1 = ab("w1", [HY_EMB, HY_F])
        w2 = ab("w2", [HY_F, HY_F])
        w3 = ab("w3", [HY_F, 2 * HW])
        delta = ab("delta", [P, HW])
        negt = ab("negt", [P, 2, NT])
        absum = [ab(f"absum{b}", [P, HW]) for b in range(2)]
        dec = [ab(f"dec{b}", [P, 2, HW]) for b in range(2)]
        fa = [ab(f"fa{b}", [P, HW]) for b in range(2)]
        fg = [ab(f"fg{b}", [P, HW]) for b in range(2)]
        invn = ab("invn", [P, 2, HW])
        fst = [ab(f"fst{b}", [P, 2, HW]) for b in range(2)]
        mlp = Area(MLP_AT)
        fslab = [mlp(f"fslab{b}", [P, 2, LT, P]) for b in range(2)]
        assert mlp.at <= MLP_END
        a1b = Area(AREA_B + 2 * TOK * 4)
        aw1 = [a1b(f"aw1_{b}", [P, KT, 256]) for b in range(2)]
        apart = [a1b(f"apart{b}", [P, 2, 256]) for b in range(2)]
        ADA_ACC = ALL[:, 7 * 512:7 * 512 + 192]
        SUM_ACC = [ALL[:, 6 * 512:7 * 512], ALL[:, 5 * 512:6 * 512]]

        aw_full = [sem(f"aw_full{b}") for b in range(NADA)]
        aw_used = [sem(f"aw_used{b}") for b in range(NADA)]
        apart_there = sem("apart_there")
        apart_used = [sem(f"apart_used{b}") for b in range(2)]
        csc_there = sem("csc_there")
        filt_in, mlp_full, sin_in, sin_out = sem("filt_in"), sem("mlp_full"), sem("sin_in"), sem("sin_out")
        tap_full, dec_there, tap_read, abs_there, abs_used = (
            sem("tap_full"), sem("dec_there"), sem("tap_read"), sem("abs_there"), sem("abs_used"))
        taps_there = sem("taps_there")
        fs_full = [sem(f"fs_full{b}") for b in range(2)]
        filt_full = [sem(f"filt_full{b}") for b in range(2)]
        filt_scaled = [sem(f"filt_scaled{b}") for b in range(2)]
        filt_stored = [sem(f"filt_stored{b}") for b in range(2)]
        ada_w = T["ada_w"].rearrange("l (k p) n -> l p k n", p=P)
        fspec = scratch["fspec"]
        SLABS = 6 * D // 256
        N_FILT = 6
        ADA_NOW = 16
        assert ADA_NOW >= NADA + NT and ADA_NOW % NADA == 0

        def ada_slab_sp(sp, n):
            b = n % NADA
            if n >= NADA:
                sp.wait_ge(aw_used[b], n // NADA)
            sp.dma_start(aw[b][:], ada_w[0][:, :, n * 256:(n + 1) * 256]).then_inc(aw_full[b], 16)

        def ada_slab_pe(pe, n):
            b = n % NADA
            pe.wait_ge(aw_full[b], 16 * (n // NADA + 1))
            ada_products(pe, aw[b], lambda j: ADA_ACC[:, n * 4 + 2 * j:n * 4 + 2 * j + 2]).then_inc(aw_used[b], 1)

        def ada_products(pe, w, acc):
            for j in range(2):
                for k in range(KT):
                    ins = pe.matmul(acc(j), w[:, k, j * P:(j + 1) * P], csc[:, k, :], start=(k == 0), stop=(k == KT - 1),
                                    skip_group_check=True)
            return ins

        def ada_sp(sp):
            for n in range(NADA):
                ada_slab_sp(sp, n)
            enter(sp, "ada")
            for dst, name in ((pos, "pos"), (w1, "hy_filt_w1"), (w2, "hy_filt_w2"), (w3, "hy_filt_w3"), (negt, "negt")):
                sp.dma_start(dst[:], T[name][0] if name.startswith("hy") else T[name]).then_inc(filt_in, 16)
            sp.dma_start(delta[:], T["delta"].partition_broadcast(P)).then_inc(filt_in, 16)
            for n in range(NADA, ADA_NOW):
                ada_slab_sp(sp, n)
            sp.wait_ge(sin_out, 2)
            for kk in range(NT):
                b = kk % 2
                if kk >= 2:
                    sp.wait_ge(filt_full[b], kk // 2)
                if kk < LT:
                    sp.dma_start(fslab[b][:].rearrange("p q k c -> p q (k c)"), T["dft_lat"][kk]).then_inc(fs_full[b], 16)
                else:
                    sp.dma_start(fslab[b][:, :, 0:CT, :].rearrange("p q k c -> p q (k c)"),
                                 T["dft_ctx"][kk - LT]).then_inc(fs_full[b], 16)

        def ada_act(act, st):
            enter(act, "ada")
            st.done(act.activation(csc[:, :, 0], vc1[:, V1_C:V1_C + 8], ACT.Silu))
            st.done(act.activation(csc[:, :, 1], vc1[:, V1_CC:V1_CC + 8], ACT.Silu))
            st.settle()
            act.sem_inc(csc_there, 1)
            st.link(act.activation(lam[:, 2:4], lam[:, 0:2], ACT.Exp))
            act.sem_inc(csc_there, 1)
            act.wait_ge(filt_in, 16 * N_FILT)
            for layer in range(2):
                act.wait_ge(sin_in, layer + 1)
                if layer == 0:
                    st.link(act.activation(h1[:], farg[:], ACT.Sin))
                else:
                    st.done(act.activation(h2p[:, 1:LAT + 1], farg[:, 0:LAT], ACT.Sin))
                    st.link(act.activation(h2p[:, LAT + 2:], farg[:, LAT:], ACT.Sin))
                act.sem_inc(sin_out, 1)
            for tt in range(NT):
                b = tt % 2
                if tt >= 2:
                    act.wait_ge(tap_read, tt - 1)
                for s in range(2):
                    st.done(act.activation(dec[b][:, s, :], delta[:], ACT.Exp, scale=negt[:, s, tt:tt + 1]))
                st.settle()
                act.sem_inc(dec_there, 1)
            for kk in range(NT):
                b = kk % 2
                act.wait_ge(filt_scaled[b], kk // 2 + 1)
                act.dma_start(fspec[kk], fst[b][:]).then_inc(filt_stored[b], 16)
            for b in range(2):
                act.wait_ge(filt_stored[b], 16 * (NT // 2))
            leave(act)

        def ada_pe(pe):
            enter(pe, "ada")
            pe.wait_ge(csc_there, 1)
            pe.wait_ge(filt_in, 16 * N_FILT)
            for at, w in FULL_CHUNKS:
                ins = pe.matmul(PS[0][:HY_F, at:at + w], w1[:], pos[:, at:at + w], start=True, stop=True)
            ins.then_inc(mlp_full, 1)
            for n in range(NADA):
                ada_slab_pe(pe, n)
            pe.wait_ge(sin_out, 1)
            for at, w in FULL_CHUNKS:
                ins = pe.matmul(PS[1][:HY_F, at:at + w], w2[:], h1[:, at:at + w], start=True, stop=True)
            ins.then_inc(mlp_full, 1)
            pe.wait_ge(sin_out, 2)

            def sums(tt):
                pe.wait_ge(abs_there, tt + 1)
                pe.matmul(SUM_ACC[0 if tt < LT else 1], ones[:], absum[tt % 2][:], start=tt in (0, LT),
                          stop=tt in (LT - 1, NT - 1), skip_group_check=True).then_inc(abs_used, 1)

            for tt in range(NT):
                b = tt % 2
                if tt >= 2:
                    pe.wait_ge(tap_read, tt - 1)
                at = tt * P + (1 if tt < LT else 2)
                pe.matmul(PS[b][:, 0:HW], h2p[:, at:at + P], w3[:, 0:HW], start=True, stop=True)
                pe.matmul(PS[b][:, HW:2 * HW], h2p[:, at - 1:at - 1 + P], w3[:, HW:2 * HW], start=True,
                          stop=True).then_inc(tap_full, 1)
                if tt:
                    sums(tt - 1)
                ada_slab_pe(pe, NADA + tt)
            for n in range(NADA + NT, ADA_NOW):
                ada_slab_pe(pe, n)
            sums(NT - 1)
            pe.wait_ge(taps_there, 1)
            for kk in range(NT):
                b, tts = kk % 2, range(LT) if kk < LT else range(LT, NT)
                pe.wait_ge(fs_full[b], 16 * (kk // 2 + 1))
                if kk >= 2:
                    pe.wait_ge(filt_scaled[b], kk // 2)
                for q, src in ((0, Pt), (1, Mt)):
                    for m, tt in enumerate(tts):
                        ins = pe.matmul(PS[b][:, q * HW:(q + 1) * HW], fslab[b][:, q, m, :], src[:, tt, :], start=(m == 0),
                                        stop=(m == len(tts) - 1), skip_group_check=True)
                ins.then_inc(filt_full[b], 1)
            for b in range(NADA):
                pe.wait_ge(aw_used[b], ADA_NOW // NADA)
            leave(pe)

        def modulation(dve, st, n0, n1, norms):
            st.link(dve.tensor_tensor(mod[:, n0:n1, :], ADA_ACC[:, 2 * n0:2 * n1].rearrange("p (n c) -> p n c", c=2),
                                      vc1[:, V1_ADA + n0:V1_ADA + n1].unsqueeze(2).broadcast_to([P, n1 - n0, 2]), ALU.add))
            for l, which in norms:
                sc = l * 48 + which * 24 + 8
                v = (V2_MIX, V2_FFN)[which]
                assert n0 <= sc and sc + 8 <= n1
                st.done(dve.scalar_tensor_tensor(
                    gsc[:, l * 2 + which], mod[:, sc:sc + 8, :], 1.0,
                    vc2[:, v + l * 8:v + l * 8 + 8].unsqueeze(2).broadcast_to([P, 8, 2]), ALU.add, ALU.mult))
            st.settle()

        def ada_dve(dve, st):
            enter(dve, "ada")
            st.link(dve.memset(h2p[:], 0.0))
            for layer in range(2):
                dve.wait_ge(mlp_full, layer + 1)
                st.link(dve.tensor_scalar(farg[:], PS[layer][:HY_F, 0:TOK], fcol[:, 2 * layer:2 * layer + 1],
                                          fcol[:, 2 * layer + 1:2 * layer + 2], ALU.add, ALU.mult))
                st.link(dve.tensor_scalar(fint[:], farg[:], 1.0 / (2 * math.pi), MAGIC, ALU.mult, ALU.add))
                st.link(dve.tensor_scalar(fint[:], fint[:], -MAGIC, None, ALU.add))
                for part in (TWO_PI_A, TWO_PI_B, TWO_PI_C):
                    st.link(dve.scalar_tensor_tensor(farg[:], fint[:], -part, farg[:], ALU.mult, ALU.add))
                st.link(dve.tensor_scalar(farg[:], farg[:], PI_CLAMP, -PI_CLAMP, ALU.min, ALU.max))
                dve.sem_inc(sin_in, 1)
                dve.wait_ge(sin_out, layer + 1)
            for tt in range(NT):
                b = tt % 2
                dve.wait_ge(tap_full, tt + 1)
                dve.wait_ge(dec_there, tt + 1)
                if tt >= 2:
                    dve.wait_ge(abs_used, tt - 1)
                st.done(dve.tensor_tensor(fa[b][:], PS[b][:, 0:HW], dec[b][:, 0, :], ALU.mult))
                st.link(dve.tensor_tensor(fg[b][:], PS[b][:, HW:2 * HW], dec[b][:, 1, :], ALU.mult))
                dve.sem_inc(tap_read, 1)
                st.done(dve.tensor_tensor(Pt[:, tt, :], fa[b][:], fg[b][:], ALU.add))
                st.done(dve.tensor_tensor(Mt[:, tt, :], fg[b][:], fa[b][:], ALU.subtract))
                st.done(dve.scalar_tensor_tensor(absum[b][:], fa[b][:], -1.0, fa[b][:], ALU.mult, ALU.max))
                st.link(dve.scalar_tensor_tensor(fg[b][:], fg[b][:], -1.0, fg[b][:], ALU.mult, ALU.max))
                st.link(dve.tensor_tensor(absum[b][:], absum[b][:], fg[b][:], ALU.add))
                dve.sem_inc(abs_there, 1)
            dve.sem_inc(taps_there, 1)
            dve.wait_ge(abs_used, NT)
            for s, L in ((0, LAT), (1, CTX)):
                st.link(dve.reciprocal(invn[:, s, :], SUM_ACC[s]))
                st.link(dve.tensor_scalar(invn[:, s, :], invn[:, s, :], 1.0 / L, None, ALU.mult))
            for kk in range(NT):
                b, s = kk % 2, 0 if kk < LT else 1
                dve.wait_ge(filt_full[b], kk // 2 + 1)
                if kk >= 2:
                    dve.wait_ge(filt_stored[b], 16 * (kk // 2))
                st.done(dve.tensor_tensor(fst[b][:, 0, :], PS[b][:, 0:HW], invn[:, s, :], ALU.mult))
                st.link(dve.tensor_tensor(fst[b][:, 1, :], PS[b][:, HW:2 * HW], invn[:, s, :], ALU.mult))
                dve.sem_inc(filt_scaled[b], 1)
            for b in range(NADA):
                dve.wait_ge(aw_used[b], ADA_NOW // NADA)
            modulation(dve, st, 0, 2 * ADA_NOW, [(0, 0)])
            dve.wait_ge(csc_there, 2)
            st.link(dve.tensor_tensor(lam[:, 4:5], lam[:, 2:3], lam[:, 3:4], ALU.subtract))
            st.link(dve.tensor_scalar(lam[:, 5:6], lam[:, 4:5], LAM_INIT, -1.0, ALU.add, ALU.mult))
            st.link(dve.tensor_scalar(lam[:, 6:7], vc2[:, V2_SUB:V2_SUB + 1], 1.0 - LAM_INIT, None, ALU.mult))
            leave(dve)

        A0 = (SLABS - ADA_NOW) // 2
        A1 = A0 + SLABS // 2
        AW0 = ADA_NOW // NADA
        assert A1 == 16

        def in0_sp(sp):
            src = w_src["in0"]
            base = SLAB0["in0"] // 2
            for l, i0, i1, at in ((0, 0, A0, ADA_NOW * 256), (1, A0, A1, -A0 * 512)):
                with sp.Fori(i0, i1) as i:
                    for b in range(2):
                        sp_slab(sp, (b, base + i), src[:, :, bass.ds(i * (2 * P) + b * P, P)])
                        if b == 0:
                            enter(sp, "in0")
                        sp.wait_ge(aw_used[b], AW0 + i)
                        sp.dma_start(aw1[b][:], ada_w[l][:, :, bass.ds(i * 512 + (at + b * 256), 256)]).then_inc(aw_full[b], 16)

        def in0_pe(pe):
            enter(pe, "in0")
            base, use = SLAB0["in0"] // 2, USE0["in0"] // 2
            with pe.Fori(0, A1) as i:
                for b in range(2):
                    pe.wait_ge(w_ready[b], base + i + 1)
                    pe.wait_ge(acc_free[b], use + i)
                    full_slab(pe, b, FULL_CHUNKS).then_inc(acc_full[b], 1)
                    pe.wait_ge(apart_there, i * 2 + (b + 1))
                    for j in range(2):
                        for seg in range(2):
                            ins = pe.matmul(ALL[:, bass.ds(i * 8 + (7 * 512 + 4 * ADA_NOW + b * 4 + 2 * j + seg), 1)],
                                            apart[b][:, seg, j * P:(j + 1) * P], ones[:, 0:1], start=True, stop=True,
                                            skip_group_check=True)
                    ins.then_inc(apart_used[b], 1)
            for b in range(2):
                pe.wait_ge(acc_full[b], use + 16)
                pe.wait_ge(apart_used[b], A1)
            leave(pe)

        def in0_dve(dve, st):
            enter(dve, "in0")
            with dve.Fori(0, A1) as i:
                st.enter(i, 4 * KT)
                for b in range(2):
                    dve.wait_ge(aw_full[b], i * 16 + (AW0 + 1) * 16)
                    dve.wait_ge(apart_used[b], i)
                    for k in range(KT):
                        for seg in range(2):
                            w, c, dst = aw1[b][:, k, :], csc[:, k, seg:seg + 1], apart[b][:, seg, :]
                            if k == 0:
                                st.done(dve.tensor_scalar(dst, w, c, None, ALU.mult))
                            else:
                                st.done(dve.scalar_tensor_tensor(dst, w, c, dst, ALU.mult, ALU.add))
                        st.settle()
                    dve.sem_inc(aw_used[b], 1)
                    dve.sem_inc(apart_there, 1)
                st.leave(A1)
            for b in range(2):
                dve.wait_ge(apart_used[b], A1)
            modulation(dve, st, 2 * ADA_NOW, 4 * SLABS, [(0, 1), (1, 0), (1, 1)])
            leave(dve)

        zb = Area(AREA_B)
        zst = [zb(f"zst{b}", [P, TOK]) for b in range(2)]
        z_stored = [sem(f"z_stored{b}") for b in range(2)]
        Z0 = {"in0": 0, "in1": 16}

        def spill_act(act, name, slabs):
            enter(act, name)
            use, z0 = USE0[name] // 2, Z0[name]
            with act.Fori(0, slabs // 2) as i:
                for b in range(2):
                    act.wait_ge(acc_full[b], use + i + 1)
                    act.wait_ge(z_stored[b], 16 * (z0 + i))
                    act.activation(zst[b][:], PS[b][:, 0:TOK], ACT.Copy).then_inc(acc_free[b], 1)
                    act.wait_ge(acc_free[b], use + i + 1)
                    act.dma_start(zT[i * 2 + b], zst[b][:]).then_inc(z_stored[b], 16)
            for b in range(2):
                act.wait_ge(z_stored[b], 16 * (z0 + slabs // 2))
            leave(act)

        def in_pe(pe, name, slabs):
            enter(pe, name)
            pe_linear(pe, name, slabs, FULL_CHUNKS)
            leave(pe)

        mst = zst
        m_full = [sem(f"m_full{b}") for b in range(2)]
        m_high = [sem(f"m_high{b}") for b in range(2)]
        m_low = [sem(f"m_low{b}") for b in range(2)]

        def mix_sp(sp, l, n):
            enter(sp, f"mix{l}")
            with sp.Fori(0, KT // 2) as i:
                for b in range(2):
                    sp.wait_ge(m_low[b], l * (KT // 2) + i)
                    sp.dma_start(mst[b][:, :n], mixT[i * 2 + b][:, :n]).then_inc(m_full[b], 16)

        def mix_act(act, l, n):
            enter(act, f"mix{l}")
            with act.Fori(0, KT // 2) as i:
                for b in range(2):
                    act.wait_ge(m_full[b], 16 * (l * (KT // 2) + i + 1))
                    act.activation(AH[:, i * 2 + b, :n], mst[b][:, :n], ACT.Copy).then_inc(m_high[b], 1)
            for b in range(2):
                act.wait_ge(m_high[b], (l + 1) * (KT // 2))
            leave(act)

        def mix_dve(dve, l, n):
            enter(dve, f"mix{l}")
            with dve.Fori(0, KT // 2) as i:
                for b in range(2):
                    dve.wait_ge(m_high[b], l * (KT // 2) + i + 1)
                    dve.tensor_tensor(AL[:, i * 2 + b, :n], mst[b][:, :n], AH[:, i * 2 + b, :n].bitcast(F32),
                                      ALU.subtract).then_inc(m_low[b], 1)
            for b in range(2):
                dve.wait_ge(m_low[b], (l + 1) * (KT // 2))
            leave(dve)


        def gated_add(dve, acc, k, gate, n):
            for seg in range(2 if n == TOK else 1):
                at, w = ((0, LAT), (LAT, CTX))[seg]
                ins = dve.scalar_tensor_tensor(XT[:, k, at:at + w], acc[:, at:at + w], gate(seg), XT[:, k, at:at + w],
                                               ALU.mult, ALU.add)
            return ins

        def out_pe(pe, l):
            enter(pe, f"out{l}")
            pe_linear(pe, f"out{l}", KT, FULL_CHUNKS if l == 0 else LAT_CHUNKS)
            leave(pe)

        def out_dve(dve, l):
            enter(dve, f"out{l}")
            use = USE0[f"out{l}"] // 2
            with dve.Fori(0, KT // 2) as i:
                for b in range(2):
                    dve.wait_ge(acc_full[b], use + i + 1)
                    gated_add(dve, PS[b], i * 2 + b,
                              lambda seg: mod[:, i * 2 + (l * 48 + 16 + b), seg:seg + 1],
                              TOK if l == 0 else LAT).then_inc(acc_free[b], 1)
            for b in range(2):
                dve.wait_ge(acc_free[b], use + KT // 2)
            leave(dve)

        fb_ = Area(AREA_B)
        HH = fb_("HH", [P, 4, TOK], F32R)
        HL = fb_("HL", [P, 4, TOK], F32R)
        sg = fb_("sg", [P, TOK])
        hid = fb_("hid", [P, TOK])
        hh_there = sem("hh_there")
        hl_there = sem("hl_there")

        def ffn_n(l):
            return TOK if l == 0 else LAT

        def ffn_pe(pe, l):
            name = f"ffn{l}"
            enter(pe, name)
            chunks = FULL_CHUNKS if l == 0 else LAT_CHUNKS
            slab, use = SLAB0[name] // 2, USE0[name] // 2

            def up(s, u):
                for j in range(2):
                    for b in range(2):
                        pe.wait_ge(w_ready[b], s + j + 1)
                        pe.wait_ge(acc_free[b], u + j)
                        full_slab(pe, b, chunks).then_inc(acc_full[b], 1)

            def dn(g, par, s, u):
                pe.wait_ge(hl_there, 2 * (l * FG + g + 1))
                for q in range(2):
                    pe.wait_ge(w_ready[q], s + 1)
                    wh = WH[q][:].rearrange("p (j a) c -> p j a c", j=2)
                    wl = WL[q][:].rearrange("p (j a) c -> p j a c", j=2)
                    for a4 in range(4):
                        b = a4 % 2
                        pe.wait_ge(acc_free[b], u + 2 * q + a4 // 2)
                        products(pe, PS[b], chunks, range(2),
                                 lambda k: wh[:, k, a4, :], lambda k: wl[:, k, a4, :],
                                 lambda k, at, w: HH[:, par * 2 + k, at:at + w],
                                 lambda k, at, w: HL[:, par * 2 + k, at:at + w]).then_inc(acc_full[b], 1)

            up(slab, use)
            with pe.Fori(0, (FG - 1) // 2) as i:
                for h in range(2):
                    up(slab + 2 + 3 * h + i * 6, use + 2 + 6 * h + i * 12)
                    dn(i * 2 + h, h, slab + 4 + 3 * h + i * 6, use + 4 + 6 * h + i * 12)
            dn(FG - 1, (FG - 1) % 2, slab + 2 + 3 * (FG - 1), use + 2 + 6 * (FG - 1))
            pe.wait_ge(acc_full[1], use + 6 * FG)
            leave(pe)

        def ffn_act(act, l):
            name = f"ffn{l}"
            enter(act, name)
            use, n = USE0[name] // 2, ffn_n(l)

            def up(g, par, u):
                for j in range(2):
                    at = 2 * l * FG + g * 2 + j
                    act.wait_ge(acc_full[0], u + j + 1)
                    act.wait_ge(hl_there, at)
                    act.activation(sg[:, :n], PS[0][:, :n], ACT.Silu).then_inc(acc_free[0], 1)
                    act.wait_ge(acc_free[1], u + j + 1)
                    act.activation(HH[:, par * 2 + j, :n], hid[:, :n], ACT.Copy).then_inc(hh_there, 1)

            up(0, 0, use)
            with act.Fori(0, (FG - 1) // 2) as i:
                for h in range(2):
                    act.wait_ge(acc_full[1], use + 2 + 6 * h + i * 12)
                    up(i * 2 + h + 1, 1 - h, use + 2 + 6 * h + i * 12)
            act.wait_ge(hh_there, 2 * (l + 1) * FG)
            leave(act)

        def ffn_dve(dve, l):
            name = f"ffn{l}"
            enter(dve, name)
            use, n = USE0[name] // 2, ffn_n(l)

            def up(g, par, u):
                for j in range(2):
                    at = 2 * l * FG + g * 2 + j
                    dve.wait_ge(acc_full[1], u + j + 1)
                    dve.wait_ge(acc_free[0], u + j + 1)
                    dve.wait_ge(hl_there, at)
                    dve.tensor_tensor(hid[:, :n], sg[:, :n], PS[1][:, :n], ALU.mult).then_inc(acc_free[1], 1)
                    dve.wait_ge(hh_there, at + 1)
                    dve.tensor_tensor(HL[:, par * 2 + j, :n], hid[:, :n], HH[:, par * 2 + j, :n].bitcast(F32),
                                      ALU.subtract).then_inc(hl_there, 1)

            def dn(u):
                for k in range(KT):
                    b = k % 2
                    dve.wait_ge(acc_full[b], u + k // 2 + 1)
                    gated_add(dve, PS[b], k, lambda seg: mod[:, l * 48 + 40 + k, seg:seg + 1], n).then_inc(acc_free[b], 1)

            up(0, 0, use)
            with dve.Fori(0, (FG - 1) // 2) as i:
                for h in range(2):
                    dve.wait_ge(acc_full[1], use + 2 + 6 * h + i * 12)
                    up(i * 2 + h + 1, 1 - h, use + 2 + 6 * h + i * 12)
                    dn(use + 4 + 6 * h + i * 12)
            dn(use + 2 + 6 * (FG - 1))
            for b in range(2):
                dve.wait_ge(acc_free[b], use + 6 * FG)
            leave(dve)

        PADW = TOK + 4
        ha = Area(AREA)
        zp = [ha(f"zp{j}", [P, PADW]) for j in range(3)]
        cv = [ha(f"cv{j}", [P, PADW]) for j in range(3)]
        UTOK_AT = ha.at
        uTok = ha("uTok", [P, NT, HW])
        Y = ha("Y", [P, 2, NT, HW])
        dslab = [ha(f"dslab{b}", [P, 2, LT, P]) for b in range(2)]
        fsl = [ha(f"fsl{b}", [P, 2, HW]) for b in range(2)]
        ftmp = [ha(f"ftmp{j}", [P, HW]) for j in range(4)]
        yT = nc.alloc_sbuf_tensor_at("yT", [P, 4, TOK], F32, offset=UTOK_AT)

        hz_full, hz_used = sem("hz_full"), sem("hz_used")
        u_there, u_turned, u_stored, utok_there = sem("u_there"), sem("u_turned"), sem("u_stored"), sem("utok_there")
        ds_full = [sem(f"ds_full{b}") for b in range(2)]
        spec_full = [sem(f"spec_full{b}") for b in range(2)]
        spec_read = [sem(f"spec_read{b}") for b in range(2)]
        is_used = [sem(f"is_used{b}") for b in range(2)]
        spec_there = sem("spec_there")
        y_full, y_read = sem("y_full"), sem("y_read")
        fz_full, fz_used, fo_there, fo_stored = sem("fz_full"), sem("fz_used"), sem("fo_there"), sem("fo_stored")
        SEGS = ((0, 1, LAT), (LAT, LAT + 3, CTX))
        INV = [("lat", th, kk) for th in range(2) for kk in range(LT)] + [("ctx", 0, kk) for kk in range(CT)]

        def hyena_sp(sp):
            enter(sp, "hyena")
            with sp.Fori(0, 4) as c:
                sp.wait_ge(hz_used, c)
                for j, tile in ((0, 24), (1, 28)):
                    for t0, p0, w in SEGS:
                        sp.dma_start(zp[j][:, p0:p0 + w], zT[c + tile][:, t0:t0 + w]).then_inc(hz_full, 16)
            with sp.Fori(0, LT // 2) as i:
                for b in range(2):
                    sp.wait_ge(spec_read[b], i)
                    sp.dma_start(dslab[b][:].rearrange("p q k c -> p q (k c)"), T["dft_lat"][i * 2 + b]).then_inc(ds_full[b], 16)
                    sp.dma_start(fsl[b][:], fspec[i * 2 + b]).then_inc(ds_full[b], 16)
            for b in range(CT):
                sp.wait_ge(spec_read[b], LT // 2)
                sp.dma_start(dslab[b][:, :, 0:CT, :].rearrange("p q k c -> p q (k c)"), T["dft_ctx"][b]).then_inc(ds_full[b], 16)
                sp.dma_start(fsl[b][:], fspec[LT + b]).then_inc(ds_full[b], 16)
            for n, (seg, th, kk) in enumerate(INV):
                b, use = n % 2, n // 2
                sp.wait_ge(spec_full[b], LT // 2 + 1) if use == 0 else sp.wait_ge(is_used[b], use)
                w = min(512, LAT if seg == "lat" else CTX)
                flat = dslab[b][:].rearrange("p q k c -> p (q k c)")[:, 0:2 * w].rearrange("p (q w) -> p q w", q=2)
                sp.dma_start(flat, T["inv_" + seg][th, kk]).then_inc(ds_full[b], 16)
            sp.wait_ge(u_turned, 4)
            sp.wait_ge(u_stored, 64)
            with sp.Fori(0, 4) as c:
                sp.wait_ge(fz_used, c)
                for t0, p0, w in SEGS:
                    sp.dma_start(zp[2][:, p0:p0 + w], zT[c + 20][:, t0:t0 + w]).then_inc(fz_full, 16)
                sp.dma_start(cv[2][:], uT_s[c]).then_inc(fz_full, 16)

        def zero_pads(dve, st, bufs):
            for t in bufs:
                for c0, c1 in ((0, 1), (LAT + 1, LAT + 3), (PADW - 1, PADW)):
                    st.done(dve.memset(t[:, c0:c1], 0.0))
            st.settle()

        def short_conv(dve, st, dst, src, tile):
            inner = slice(1, PADW - 1)

            def col(tap):
                return vc2[:, V2_SW + tap * 12 + tile:V2_SW + tap * 12 + tile + 1] if isinstance(tile, int) else \
                    vc2[:, bass.ds(tile + (V2_SW + tap * 12), 1)]

            bias = vc2[:, bass.ds(tile + V2_SB, 1)]
            st.link(dve.tensor_scalar(dst[:, inner], src[:, inner], col(1), bias, ALU.mult, ALU.add))
            st.link(dve.scalar_tensor_tensor(dst[:, inner], src[:, 0:PADW - 2], col(0), dst[:, inner], ALU.mult, ALU.add))
            st.link(dve.scalar_tensor_tensor(dst[:, inner], src[:, 2:PADW], col(2), dst[:, inner], ALU.mult, ALU.add))

        def hyena_dve(dve, st):
            enter(dve, "hyena")
            zero_pads(dve, st, zp + cv[2:])
            with dve.Fori(0, 4) as c:
                st.enter(c, 7)
                dve.wait_ge(hz_full, c * 64 + 64)
                short_conv(dve, st, cv[0], zp[0], c + 4)
                short_conv(dve, st, cv[1], zp[1], c + 8)
                dve.sem_inc(hz_used, 1)
                dve.wait_ge(u_turned, c)
                dve.wait_ge(u_stored, c * 16)
                st.link(dve.tensor_tensor(cv[2][:, 1:PADW - 1], cv[0][:, 1:PADW - 1], cv[1][:, 1:PADW - 1], ALU.mult))
                dve.sem_inc(u_there, 1)
                st.leave(4)

            def spectrum(b, use, kk):
                ur, ui = PS[b][:, 0:512], PS[b][:, 512:1024]
                fr, fi = fsl[b][:, 0, :], fsl[b][:, 1, :]
                dve.wait_ge(spec_full[b], use + 1)
                st.done(dve.tensor_tensor(ftmp[0][:], ur, fr, ALU.mult))
                st.done(dve.tensor_tensor(ftmp[1][:], ui, fi, ALU.mult))
                st.done(dve.tensor_tensor(ftmp[2][:], ur, fi, ALU.mult))
                st.link(dve.tensor_tensor(ftmp[3][:], ui, fr, ALU.mult))
                dve.sem_inc(spec_read[b], 1)
                st.done(dve.tensor_tensor(Y[:, 0, kk, :], ftmp[0][:], ftmp[1][:], ALU.add))
                st.link(dve.tensor_tensor(Y[:, 1, kk, :], ftmp[2][:], ftmp[3][:], ALU.subtract))

            with dve.Fori(0, LT // 2) as i:
                st.enter(i, 12)
                for b in range(2):
                    spectrum(b, i, i * 2 + b)
                st.leave(LT // 2)
            for b in range(CT):
                spectrum(b, LT // 2, LT + b)
            dve.sem_inc(spec_there, 1)
            dve.wait_ge(y_read, 3)
            with dve.Fori(0, 4) as c:
                st.enter(c, 7)
                dve.wait_ge(fz_full, c * 48 + 48)
                short_conv(dve, st, cv[0], zp[2], c)
                for t0, p0, w in SEGS:
                    st.done(dve.scalar_tensor_tensor(cv[2][:, p0:p0 + w], cv[2][:, p0:p0 + w], vc2[:, bass.ds(c + V2_SKIP, 1)],
                                                     yT[:, c, t0:t0 + w], ALU.mult, ALU.add))
                st.settle()
                dve.wait_ge(fo_stored, c * 16)
                for t0, p0, w in SEGS:
                    st.done(dve.tensor_tensor(cv[1][:, t0:t0 + w], cv[2][:, p0:p0 + w], cv[0][:, p0:p0 + w], ALU.mult))
                st.settle()
                dve.sem_inc(fo_there, 1)
                dve.sem_inc(fz_used, 1)
                st.leave(4)
            leave(dve)

        def hyena_act(act, st):
            enter(act, "hyena")
            with act.Fori(0, 4) as c:
                act.wait_ge(u_there, c + 1)
                act.dma_start(uT_s[c], cv[2][:]).then_inc(u_stored, 16)
                act.wait_ge(u_turned, c + 1)
                act.activation(uTok[:, :, bass.ds(c * P, P)], PS[0][:, 0:TOK].rearrange("p (t c) -> p t c", c=P),
                               ACT.Copy).then_inc(utok_there, 1)
            for n, (w, t0) in enumerate(((512, 0), (512, 512), (CTX, LAT))):
                act.wait_ge(y_full, n + 1)
                S = n % 2
                for c in range(4):
                    src = PS[S][:, c * 512:c * 512 + w] if c < 3 else PM[:, S * 512:S * 512 + w]
                    st.done(act.activation(yT[:, c, t0:t0 + w], src, ACT.Copy))
                st.settle()
                act.sem_inc(y_read, 1)
            with act.Fori(0, 4) as c:
                act.wait_ge(fo_there, c + 1)
                act.dma_start(mixT[c + 4], cv[1][:, 0:TOK]).then_inc(fo_stored, 16)
            act.wait_ge(fo_stored, 64)
            leave(act)

        def hyena_pe(pe, st):
            enter(pe, "hyena")
            with pe.Fori(0, 4) as c:
                pe.wait_ge(u_there, c + 1)
                pe.wait_ge(utok_there, c)
                for tt in range(NT):
                    at = tt * P + (1 if tt < LT else 3)
                    ins = pe.transpose(PS[0][:, tt * P:(tt + 1) * P], cv[2][:, at:at + P], ident[:])
                ins.then_inc(u_turned, 1)
            pe.wait_ge(utok_there, 4)

            def forward(b, use, tts):
                pe.wait_ge(ds_full[b], use * 32 + 32)
                pe.wait_ge(spec_read[b], use)
                n = len(tts)
                for q in range(2):
                    for m, tt in enumerate(tts):
                        ins = pe.matmul(PS[b][:, q * 512:(q + 1) * 512], dslab[b][:, q, m, :], uTok[:, tt, :],
                                        start=(m == 0), stop=(m == n - 1), skip_group_check=True)
                ins.then_inc(spec_full[b], 1)

            with pe.Fori(0, LT // 2) as i:
                for b in range(2):
                    forward(b, i, range(LT))
            for b in range(CT):
                forward(b, LT // 2, range(LT, NT))
            pe.wait_ge(spec_there, 1)
            for n, (seg, th, kk) in enumerate(INV):
                b, use = n % 2, n // 2
                S = th
                w = min(512, LAT if seg == "lat" else CTX)
                count = LT if seg == "lat" else CT
                if seg == "ctx" and kk == 0:
                    pe.wait_ge(y_read, 1)
                pe.wait_ge(ds_full[b], 32 * (LT // 2 + 1) + 16 * (use + 1))
                flat = dslab[b][:].rearrange("p q k c -> p (q k c)")
                for c in range(4):
                    acc = PS[S][:, c * 512:c * 512 + w] if c < 3 else PM[:, S * 512:S * 512 + w]
                    for q in range(2):
                        ins = pe.matmul(acc, Y[:, q, kk + (0 if seg == "lat" else LT), c * P:(c + 1) * P],
                                        flat[:, q * w:(q + 1) * w], start=(kk == 0 and q == 0),
                                        stop=(kk == count - 1 and q == 1), skip_group_check=True)
                st.link(ins) if kk == count - 1 else ins.then_inc(is_used[b], 1)
                if kk == count - 1:
                    pe.sem_inc(y_full, 1)
                    pe.sem_inc(is_used[b], 1)
            leave(pe)

        ga = Area(AREA)
        gq, gv, gg = ga("gq", [P, TOK]), ga("gv", [P, TOK]), ga("gg", [P, TOK])
        gz = ga("gz", [P, 2, TOK])
        state = nc.alloc_sbuf_tensor_at("state", [P, 2, NT, P], F32, offset=ga.at - 2 * TOK * 4)
        glog = ga("glog", [P, 2, TOK])
        kdTok = nc.alloc_sbuf_tensor_at("kdTok", [P, 2, NT, P], F32, offset=ga.at - 2 * TOK * 4)
        gcum = ga("gcum", [P, 2, TOK])
        gk = ga("gk", [P, 2, TOK])
        garg = [ga(f"garg{b}", [P, 2, TOK]) for b in range(2)]
        gqe = [ga(f"gqe{b}", [P, TOK]) for b in range(2)]
        gke = [ga(f"gke{b}", [P, TOK]) for b in range(2)]
        attn = ga("attn", [P, TOK])
        gtmp = ga("gtmp", [P, TOK])
        vTok = ga("vTok", [P, NT, P])
        keepm = ga("keepm", [P, 2, TOK])
        lmask = ga("lmask", [P, LEVELS + 1, P])
        gdec = ga("gdec", [P, 2, NT])
        NS = LEVELS + 1

        gh_full, gh_used = sem("gh_full"), sem("gh_used")
        v_turned, v_tok = sem("v_turned"), sem("v_tok")
        softp, log_there, k_there = sem("softp"), sem("log_there"), sem("k_there")
        arg_there, fac_there, qk_there = sem("arg_there"), sem("fac_there"), sem("qk_there")
        step_full, step_read = sem("step_full"), sem("step_read")
        qdec_there, kdec_there, kd_turned, kd_tok = sem("qdec_there"), sem("kdec_there"), sem("kd_turned"), sem("kd_tok")
        upd_full, state_there, o_full = sem("upd_full"), sem("state_there"), sem("o_full")
        osq_there, oss_full, oroot = sem("osq_there"), sem("oss_full"), sem("oroot")
        gate_there, mo_there, mo_stored = sem("gate_there"), sem("mo_there"), sem("mo_stored")

        def halves(ap, l):
            return ap.rearrange("p (n a h) -> p n a h", a=2, h=1 << l)

        def hgrn_sp(sp):
            enter(sp, "hgrn")
            sp.dma_start(lmask[:], T["levelmask"]).then_inc(gh_full, 16)
            with sp.Fori(0, 4) as h:
                sp.wait_ge(gh_used, h)
                for dst, tile in ((gq[:], 0), (gz[:, 0, :], 4), (gz[:, 1, :], 8), (gv[:], 12), (gg[:], 16)):
                    sp.dma_start(dst, zT[h + tile]).then_inc(gh_full, 16)

        def hgrn_act(act, st):
            enter(act, "hgrn")
            with act.Fori(0, 4) as h:
                st.enter(h, 8)
                act.wait_ge(gh_full, h * 80 + 96)
                act.wait_ge(gh_used, h)
                st.link(act.activation(gk[:], gz[:], ACT.Abs))
                st.link(act.activation(gk[:], gk[:], ACT.Exp, scale=-1.0))
                act.activation(gk[:], gk[:], ACT.Ln, bias=1.0).then_inc(softp, 1)
                act.wait_ge(v_turned, h + 1)
                act.activation(vTok[:].rearrange("p n c -> p (n c)"), PS[1][:, 0:TOK], ACT.Copy).then_inc(v_tok, 1)
                act.wait_ge(log_there, h + 1)
                act.activation(gk[:], gz[:], ACT.Exp, scale=-1.0).then_inc(k_there, 1)
                for s in range(1, NS):
                    act.wait_ge(arg_there, h * NS + s)
                    act.activation(garg[s % 2][:], garg[s % 2][:], ACT.Exp).then_inc(fac_there, 1)
                act.wait_ge(qk_there, h * NS + NS - 1)
                st.done(act.activation(garg[0][:], gcum[:], ACT.Exp))
                st.done(act.activation(gdec[:, 0, :], gcum[:, 0, P - 1::P], ACT.Exp))
                st.done(act.activation(gdec[:, 1, :], gcum[:, 1, 0::P], ACT.Exp))
                st.settle()
                act.sem_inc(qdec_there, 1)
                act.wait_ge(arg_there, h * NS + NS)
                act.activation(garg[1][:], garg[1][:], ACT.Exp).then_inc(kdec_there, 1)
                for d in range(2):
                    act.wait_ge(kd_turned, h * 2 + d + 1)
                    act.activation(kdTok[:, d].rearrange("p n c -> p (n c)"), PS[d][:, 0:TOK], ACT.Copy).then_inc(kd_tok, 1)
                act.wait_ge(o_full, h + 1)
                st.done(act.activation(gqe[0][:], PS[0][:, 0:TOK], ACT.Square))
                st.settle()
                act.sem_inc(osq_there, 1)
                act.wait_ge(oss_full, h + 1)
                st.link(act.activation(gke[0][:], PS[1][:, 0:TOK], ACT.Sqrt, bias=eps_col[:, 0:1], scale=1.0 / P))
                act.sem_inc(oroot, 1)
                st.link(act.activation(gg[:], gg[:], ACT.Silu))
                act.sem_inc(gate_there, 1)
                act.wait_ge(mo_there, h + 1)
                act.dma_start(mixT[h], gtmp[:]).then_inc(mo_stored, 16)
                st.leave(4)
            act.wait_ge(mo_stored, 64)
            leave(act)

        def hgrn_dve(dve, st):
            enter(dve, "hgrn")
            st.link(dve.memset(keepm[:], 1.0))
            st.done(dve.memset(keepm[:, 0, 0::P], 0.0))
            st.done(dve.memset(keepm[:, 1, P - 1::P], 0.0))
            st.settle()
            with dve.Fori(0, 4) as h:
                st.enter(h, 4 + 1 + LEVELS * (4 + 3) + (2 * NS - 1) + 2 + 1 + 4 + 2 * (NT - 1) + 3)
                dve.wait_ge(softp, h + 1)
                st.done(dve.scalar_tensor_tensor(glog[:], gz[:], 0.0, gk[:], ALU.min, ALU.subtract))
                st.link(dve.scalar_tensor_tensor(gz[:], gz[:], 0.0, gk[:], ALU.max, ALU.add))
                dve.sem_inc(log_there, 1)
                st.done(dve.tensor_tensor_scan(gcum[:, 0, :], keepm[:, 0, :], glog[:, 0, :], 0.0, ALU.mult, ALU.add))
                st.link(dve.tensor_tensor_scan(gcum[:, 1, ::-1], keepm[:, 1, ::-1], glog[:, 1, ::-1], 0.0, ALU.mult, ALU.add))

                def args(s):
                    l = s - 1
                    shape = [P, TOK >> (l + 1), 1 << l]
                    cf, cb = halves(gcum[:, 0, :], l), halves(gcum[:, 1, :], l)
                    rf = cf[:, :, 0, (1 << l) - 1:].broadcast_to(shape)
                    rb = cb[:, :, 1, 0:1].broadcast_to(shape)
                    eq, ek = halves(garg[s % 2][:, 0, :], l), halves(garg[s % 2][:, 1, :], l)
                    st.done(dve.tensor_tensor(eq[:, :, 1, :], cf[:, :, 1, :], rf, ALU.subtract))
                    st.done(dve.tensor_tensor(eq[:, :, 0, :], cb[:, :, 0, :], rb, ALU.subtract))
                    st.done(dve.tensor_tensor(ek[:, :, 0, :], rf, cf[:, :, 0, :], ALU.subtract))
                    st.done(dve.tensor_tensor(ek[:, :, 1, :], rb, cb[:, :, 1, :], ALU.subtract))
                    st.settle()
                    dve.sem_inc(arg_there, 1)

                def factors(s):
                    l = s - 1
                    dve.wait_ge(fac_there, h * LEVELS + s)
                    if s >= 2:
                        dve.wait_ge(step_full, h * NS + s - 1)
                    ek = halves(garg[s % 2][:, 1, :], l)
                    ke = halves(gke[s % 2][:], l)
                    st.done(dve.tensor_tensor(gqe[s % 2][:], gq[:], garg[s % 2][:, 0, :], ALU.mult))
                    for d in range(2):
                        st.done(dve.tensor_tensor(ke[:, :, d, :], halves(gk[:, d, :], l)[:, :, d, :], ek[:, :, d, :], ALU.mult))
                    st.settle()
                    dve.sem_inc(qk_there, 1)

                def collect(s):
                    mask = lmask[:, s, :].unsqueeze(1).broadcast_to([P, NT, P])
                    dst = attn if s == 0 else gtmp
                    dve.wait_ge(step_full, h * NS + s + 1)
                    if s == 1:
                        dve.wait_ge(mo_stored, h * 16)
                    st.link(dve.tensor_tensor(dst[:].rearrange("p (n c) -> p n c", c=P),
                                              PS[s % 2][:, 0:TOK].rearrange("p (n c) -> p n c", c=P), mask, ALU.mult))
                    dve.sem_inc(step_read, 1)
                    if s:
                        st.link(dve.tensor_tensor(attn[:], attn[:], gtmp[:], ALU.add))

                args(1)
                dve.wait_ge(k_there, h + 1)
                st.link(dve.tensor_tensor(gke[0][:], gk[:, 0, :], gk[:, 1, :], ALU.add))
                dve.sem_inc(qk_there, 1)
                for s in range(1, NS):
                    if s + 1 < NS:
                        args(s + 1)
                    factors(s)
                    collect(s - 1)
                c4 = gcum[:].rearrange("p d (n c) -> p d n c", c=P)
                g4 = garg[1][:].rearrange("p d (n c) -> p d n c", c=P)
                st.done(dve.tensor_tensor(g4[:, 0], c4[:, 0, :, P - 1:].broadcast_to([P, NT, P]), c4[:, 0], ALU.subtract))
                st.done(dve.tensor_tensor(g4[:, 1], c4[:, 1, :, 0:1].broadcast_to([P, NT, P]), c4[:, 1], ALU.subtract))
                st.settle()
                dve.sem_inc(arg_there, 1)
                collect(NS - 1)
                dve.wait_ge(kdec_there, h + 1)
                st.link(dve.tensor_tensor(garg[1][:], garg[1][:], gk[:], ALU.mult))
                dve.sem_inc(kd_there, 1)
                dve.wait_ge(qdec_there, h + 1)
                for d in range(2):
                    st.done(dve.tensor_tensor(garg[0][:, d, :], garg[0][:, d, :], gq[:], ALU.mult))
                st.done(dve.memset(state[:, 0, LT, :], 0.0))
                st.done(dve.memset(state[:, 1, NT - 1, :], 0.0))
                st.settle()
                for d in range(2):
                    order = list(range(LT, NT)) + list(range(LT))
                    if d:
                        order = list(range(NT - 1, LT - 1, -1)) + list(range(LT - 1, -1, -1))
                    dve.wait_ge(upd_full, h * 2 + d + 1)
                    for n, m in zip(order, order[1:]):
                        st.link(dve.scalar_tensor_tensor(state[:, d, m, :], state[:, d, n, :], gdec[:, d, n:n + 1],
                                                         PS[d][:, n * P:(n + 1) * P], ALU.mult, ALU.add))
                dve.sem_inc(state_there, 1)
                dve.wait_ge(oroot, h + 1)
                st.link(dve.reciprocal(gke[0][:], gke[0][:]))
                st.link(dve.tensor_tensor(gtmp[:], PS[0][:, 0:TOK], gke[0][:], ALU.mult))
                dve.wait_ge(gate_there, h + 1)
                st.link(dve.scalar_tensor_tensor(gtmp[:], gtmp[:], vc2[:, V2_HG:V2_HG + 1], gg[:], ALU.mult, ALU.mult))
                dve.sem_inc(mo_there, 1)
                dve.sem_inc(gh_used, 1)
                st.leave(4)
            leave(dve)

        kd_there = sem("kd_there")

        def hgrn_pe(pe, st):
            enter(pe, "hgrn")
            with pe.Fori(0, 4) as h:
                pe.wait_ge(gh_full, h * 80 + 96)
                pe.wait_ge(gh_used, h)
                for n in range(NT):
                    ins = pe.transpose(PS[1][:, n * P:(n + 1) * P], gv[:, n * P:(n + 1) * P], ident[:])
                ins.then_inc(v_turned, 1)
                for s in range(NS):
                    pe.wait_ge(qk_there, h * NS + s + 1)
                    if s == 1:
                        pe.wait_ge(v_tok, h + 1)
                    if s >= 2:
                        pe.wait_ge(step_read, h * NS + s - 1)
                    q = gq if s == 0 else gqe[s % 2]
                    for n in range(NT):
                        c = slice(n * P, (n + 1) * P)
                        ins = pe.matmul(PS[s % 2][:, c], gke[s % 2][:, c], q[:, c], start=True, stop=True)
                    ins.then_inc(step_full, 1)
                pe.wait_ge(kd_there, h + 1)
                pe.wait_ge(step_read, h * NS + NS)
                for d in range(2):
                    for n in range(NT):
                        ins = pe.transpose(PS[d][:, n * P:(n + 1) * P], garg[1][:, d, n * P:(n + 1) * P], ident[:])
                    ins.then_inc(kd_turned, 1)
                for d in range(2):
                    pe.wait_ge(kd_tok, h * 2 + d + 1)
                    for n in range(NT):
                        ins = pe.matmul(PS[d][:, n * P:(n + 1) * P], kdTok[:, d, n, :], vTok[:, n, :], start=True, stop=True)
                    ins.then_inc(upd_full, 1)
                pe.wait_ge(state_there, h + 1)
                for n in range(NT):
                    c = slice(n * P, (n + 1) * P)
                    pe.matmul(PS[0][:, c], vTok[:, n, :], attn[:, c], start=True, stop=False)
                    pe.matmul(PS[0][:, c], state[:, 0, n, :], garg[0][:, 0, c], start=False, stop=False)
                    ins = pe.matmul(PS[0][:, c], state[:, 1, n, :], garg[0][:, 1, c], start=False, stop=True)
                ins.then_inc(o_full, 1)
                pe.wait_ge(osq_there, h + 1)
                for at, w in FULL_CHUNKS:
                    ins = pe.matmul(PS[1][:, at:at + w], ones[:], gqe[0][:, at:at + w], start=True, stop=True)
                ins.then_inc(oss_full, 1)
            pe.wait_ge(oss_full, 4)
            leave(pe)

        ta = Area(AREA)
        aq, ak, av = ta("aq", [P, TOK]), ta("ak", [P, TOK]), ta("av", [P, TOK])
        qr, kr = ta("qr", [P, LAT]), ta("kr", [P, TOK])
        arot = ta("arot", [P, TOK])
        prob = [ta(f"prob{b}", [P, TOK]) for b in range(2)]
        pd = [ta(f"pd{b}", [P, TOK]) for b in range(2)]
        probT = [ta(f"probT{b}", [P, TOK]) for b in range(2)]
        vtk = ta("vtk", [P, NT, P])
        od = ta("od", [P, LT, P])
        amo = ta("amo", [P, LAT])
        rope_da, rope_mla = ta("rope_da", [P, 2, LAT]), ta("rope_mla", [96, 2, LAT])
        rot_da, rot_mla = ta("rot_da", [P, P]), ta("rot_mla", [96, 96])
        cqn, ckvn, krr = ta("cqn", [P, 2, TOK]), ta("ckvn", [P, TOK]), ta("krr", [96, TOK])
        wuq, wukv = ta("wuq", [P, 2, 96]), ta("wukv", [P, 192])
        rsum, rinv, amax, ass = ta("rsum", [P, 16]), ta("rinv", [P, 16]), ta("amax", [P, 4]), ta("ass", [P, 8])

        at_full, ah_full, ah_used = sem("at_full"), sem("ah_full"), sem("ah_used")
        rot_full, qk_rot, kctx_there = sem("rot_full"), sem("qk_rot"), sem("kctx_there")
        vt_full, vt_there = sem("vt_full"), sem("vt_there")
        s_full, s_max, p_done, pd_there, t_full, pt_ready, pv_full, o_read = (
            sem("s_full"), sem("s_max"), sem("p_done"), sem("pd_there"), sem("t_full"), sem("pt_ready"), sem("pv_full"), sem("o_read"))
        od_sq, od_root, od_there, od_turned, amo_stored = (
            sem("od_sq"), sem("od_root"), sem("od_there"), sem("od_turned"), sem("amo_stored"))
        lat_in, lat_sq, lat_ss, lat_root, lat_n, kr_zero, kr_rot = (
            sem("lat_in"), sem("lat_sq"), sem("lat_ss"), sem("lat_root"), sem("lat_n"), sem("kr_zero"), sem("kr_rot"))
        mq_full, mq_copied = sem("mq_full"), sem("mq_copied")
        N_TAB = 4
        DU, MU = 2 * LT, LT

        def attn_sp(sp):
            enter(sp, "attn")
            for dst, name in ((rope_da, "rope_da"), (rope_mla, "rope_mla"), (rot_da, "rot_da"), (rot_mla, "rot_mla")):
                sp.dma_start(dst[:], T[name]).then_inc(at_full, 16)
            for k in range(2):
                sp.dma_start(cqn[:, k, :], zT[12 + k]).then_inc(lat_in, 16)
            sp.dma_start(ckvn[:], zT[14]).then_inc(lat_in, 16)
            sp.wait_ge(kr_zero, 1)
            sp.dma_start(krr[64:96, :], zT[15][64:96, :]).then_inc(lat_in, 16)
            sp.wait_ge(lat_n, 1)
            with sp.Fori(0, 4) as h:
                sp.wait_ge(qk_rot, h * 2)
                sp.wait_ge(kctx_there, h)
                sp.wait_ge(vt_full, h)
                sp.dma_start(aq[:], zT[h]).then_inc(ah_full, 16)
                sp.dma_start(ak[:], zT[h + 4]).then_inc(ah_full, 16)
                sp.dma_start(av[:], zT[h + 8]).then_inc(ah_full, 16)
            uq = T["mla_w_uq"][0].rearrange("(k p) n -> p k n", p=P)
            with sp.Fori(0, 4) as h:
                sp.wait_ge(ah_used, h + 4)
                sp.dma_start(wuq[:], uq[:, :, bass.ds(h * 96, 96)]).then_inc(ah_full, 16)
                sp.dma_start(wukv[:], T["mla_w_ukv"][0][:, bass.ds(h * 192, 192)]).then_inc(ah_full, 16)

        TURN = [(0, 4, 5 * 512), (4, 4, 6 * 512), (8, 2, 7 * 512 + P)]
        OUT = slice(7 * 512, 7 * 512 + P)

        def tiles_pe(pe, sb, tb, J, parts):
            for i in range(LT + 2):
                if i < LT:
                    pe.wait_ge(p_done, sb + i * J)
                    for j in range(J):
                        lo, hi = parts[j]
                        chunks = FULL_CHUNKS if j == 0 else [(256, 512), (768, 512), (0, 256)]
                        for at, w in chunks:
                            if j and at == 0:
                                pe.wait_ge(s_max, sb + i * J + 1)
                            ins = pe.matmul(ALL[:, j * TOK + at:j * TOK + at + w], qr[lo:hi, i * P:(i + 1) * P],
                                            kr[lo:hi, at:at + w], start=True, stop=True, skip_group_check=True)
                        ins.then_inc(s_full, 1)
                if i >= 2:
                    t = i - 2
                    pe.wait_ge(pt_ready, tb * 3 + (t * 3 + 3))
                    pe.wait_ge(o_read, tb + t)
                    for s in range(NT):
                        ins = pe.matmul(ALL[:, OUT], probT[t % 2][:, s * P:(s + 1) * P], vtk[:, s, :],
                                        start=(s == 0), stop=(s == NT - 1))
                    ins.then_inc(pv_full, 1)
                if 1 <= i <= LT:
                    t = i - 1
                    pe.wait_ge(pd_there, tb + t + 1)
                    pe.wait_ge(pt_ready, (tb + t) * 3)
                    for m, (s0, n, col) in enumerate(TURN):
                        if m == 2 and i >= 2:
                            pe.wait_ge(o_read, tb + i - 1)
                        for s in range(s0, s0 + n):
                            ins = pe.transpose(ALL[:, col + (s - s0) * P:col + (s - s0 + 1) * P],
                                               pd[t % 2][:, s * P:(s + 1) * P], ident[:])
                        ins.then_inc(t_full, 1)

        def tiles_act(act, sb, tb, J, scale):
            for i in range(LT + 1):
                for j in range(J):
                    if i < LT:
                        act.wait_ge(s_full, sb + (i + 1) * J)
                        act.wait_ge(s_max, sb + (i * J + j + 1))
                        act.wait_ge(pd_there, tb + i)
                        act.activation(prob[j][:], ALL[:, j * TOK:(j + 1) * TOK], ACT.Exp, bias=amax[:, 2 + j:3 + j],
                                       scale=scale, accum_out=rsum[:, i * J + j:i * J + j + 1]).then_inc(p_done, 1)
                if i >= 1:
                    t = i - 1
                    for m, (s0, n, col) in enumerate(TURN):
                        act.wait_ge(t_full, tb * 3 + (t * 3 + m + 1))
                        if t >= 2:
                            act.wait_ge(pv_full, tb + t - 1)
                        act.activation(probT[t % 2][:, s0 * P:(s0 + n) * P], ALL[:, col:col + n * P],
                                       ACT.Copy).then_inc(pt_ready, 1)

        def tiles_dve(dve, st, sb, tb, J, scale):
            for i in range(LT + 2):
                if 1 <= i <= LT:
                    t = i - 1
                    dve.wait_ge(p_done, sb + (t + 1) * J)
                    if t >= 2:
                        dve.wait_ge(t_full, tb * 3 + (t - 1) * 3)
                    c = slice(t * J, (t + 1) * J)
                    st.link(dve.reciprocal(rinv[:, c], rsum[:, c]))
                    ins = dve.tensor_scalar(pd[t % 2][:], prob[0][:], rinv[:, t * J:t * J + 1], None, ALU.mult)
                    if J == 2:
                        st.done(ins)
                        c1 = slice(t * J + 1, t * J + 2)
                        st.link(dve.tensor_tensor(rinv[:, c1], rinv[:, c1], lam[:, 5:6], ALU.mult))
                        ins = dve.scalar_tensor_tensor(pd[t % 2][:], prob[1][:], rinv[:, c1], pd[t % 2][:], ALU.mult, ALU.add)
                    ins.then_inc(pd_there, 1)
                if i < LT:
                    for j in range(J):
                        dve.wait_ge(s_full, sb + (i * J + j + 1))
                        dve.wait_ge(p_done, sb + (i * J + j))
                        st.link(dve.tensor_reduce(amax[:, j:j + 1], ALL[:, j * TOK:(j + 1) * TOK], AX.X, ALU.max))
                        dve.tensor_scalar(amax[:, 2 + j:3 + j], amax[:, j:j + 1], -scale, None, ALU.mult).then_inc(s_max, 1)
                if i >= 2:
                    t = i - 2
                    dve.wait_ge(pv_full, tb + t + 1)
                    dve.tensor_copy(od[:, t, :], ALL[:, OUT]).then_inc(o_read, 1)
            dve.wait_ge(o_read, tb + LT)

        def tile_steps(J):
            return LT * (1 + J) + (2 * LT if J == 2 else 0)

        def attn_pe(pe, st):
            enter(pe, "attn")
            pe.wait_ge(at_full, 16 * N_TAB)
            for j, k in ((0, 0), (0, 1), (1, 2)):
                pe.wait_ge(lat_sq, k + 1)
                for at, w in FULL_CHUNKS:
                    ins = pe.matmul(PS[j][:, at:at + w], ones[:], (aq, ak, av)[k][:, at:at + w], start=(k != 1),
                                    stop=(k >= 1), skip_group_check=True)
            ins.then_inc(lat_ss, 1)
            for at, w in LAT_CHUNKS:
                ins = pe.matmul(PM[:96, at:at + w], rot_mla[:], krr[:, at:at + w], start=True, stop=True)
            ins.then_inc(kr_rot, 1)
            pe.wait_ge(lat_n, 1)
            with pe.Fori(0, 4) as h:
                pe.wait_ge(ah_used, h)
                pe.wait_ge(ah_full, h * 48 + 48)
                for j, src in ((0, aq), (1, ak)):
                    for at, w in LAT_CHUNKS:
                        ins = pe.matmul(PS[j][:, at:at + w], rot_da[:], src[:, at:at + w], start=True, stop=True)
                    ins.then_inc(rot_full, 1)
                pe.wait_ge(qk_rot, h * 2 + 2)
                for s in range(NT):
                    ins = pe.transpose(PS[1][:, s * P:(s + 1) * P], av[:, s * P:(s + 1) * P], ident[:])
                ins.then_inc(vt_full, 1)
                pe.wait_ge(vt_there, h + 1)
                tiles_pe(pe, h * DU, h * LT, 2, ((0, 64), (64, P)))
                pe.wait_ge(od_there, h + 1)
                for tt in range(LT):
                    ins = pe.transpose(PS[1][:, tt * P:(tt + 1) * P], od[:, tt, :], ident[:])
                ins.then_inc(od_turned, 1)
            with pe.Fori(0, 4) as h:
                pe.wait_ge(ah_used, h + 4)
                pe.wait_ge(ah_full, h * 32 + (4 * 48 + 32))
                for at, w in LAT_CHUNKS:
                    for k in range(2):
                        ins = pe.matmul(PS[0][:96, at:at + w], wuq[:, k, :], cqn[:, k, at:at + w], start=(k == 0), stop=(k == 1))
                ins.then_inc(mq_full, 1)
                for at, w in FULL_CHUNKS:
                    ins = pe.matmul(PS[1][:64, at:at + w], wukv[:, 0:64], ckvn[:, at:at + w], start=True, stop=True)
                ins.then_inc(mq_full, 1)
                pe.wait_ge(mq_copied, h * 2 + 2)
                for at, w in LAT_CHUNKS:
                    ins = pe.matmul(PS[0][:96, at:at + w], rot_mla[:], aq[:96, at:at + w], start=True, stop=True)
                ins.then_inc(rot_full, 1)
                for s in range(NT):
                    ins = pe.matmul(PS[1][:, s * P:(s + 1) * P], ckvn[:, s * P:(s + 1) * P], wukv[:, 64:192], start=True, stop=True)
                ins.then_inc(vt_full, 1)
                pe.wait_ge(qk_rot, h + 9)
                pe.wait_ge(vt_there, h + 5)
                tiles_pe(pe, h * MU + 4 * DU, h * LT + 4 * LT, 1, ((0, 96),))
                pe.wait_ge(od_there, h + 5)
                for tt in range(LT):
                    ins = pe.transpose(PS[1][:, tt * P:(tt + 1) * P], od[:, tt, :], ident[:])
                ins.then_inc(od_turned, 1)
            pe.wait_ge(od_turned, 8)
            leave(pe)

        def attn_act(act, st):
            enter(act, "attn")
            for k, dst in enumerate((aq, ak, av)):
                act.wait_ge(lat_in, 64)
                act.activation(dst[:], cqn[:, k, :] if k < 2 else ckvn[:], ACT.Square).then_inc(lat_sq, 1)
            act.wait_ge(lat_ss, 1)
            st.done(act.activation(prob[0][:], PS[0][:, 0:TOK], ACT.Sqrt, bias=eps_col[:, 0:1], scale=1.0 / 256))
            st.link(act.activation(prob[1][:], PS[1][:, 0:TOK], ACT.Sqrt, bias=eps_col[:, 0:1], scale=1.0 / 128))
            act.sem_inc(lat_root, 1)
            with act.Fori(0, 4) as h:
                st.enter(h, 1)
                act.wait_ge(ah_full, h * 48 + 48)
                act.activation(kr[:, LAT:], ak[:, LAT:], ACT.Copy).then_inc(kctx_there, 1)
                act.wait_ge(vt_full, h + 1)
                act.activation(vtk[:].rearrange("p n c -> p (n c)"), PS[1][:, 0:TOK], ACT.Copy).then_inc(vt_there, 1)
                tiles_act(act, h * DU, h * LT, 2, 64 ** -0.5)
                act.wait_ge(od_sq, h + 1)
                act.activation(ass[:], ass[:], ACT.Sqrt, bias=eps_col[:, 0:1], scale=1.0 / P).then_inc(od_root, 1)
                act.wait_ge(od_turned, h + 1)
                act.wait_ge(amo_stored, h * 16)
                st.link(act.activation(amo[:], PS[1][:, 0:LAT], ACT.Copy, scale=lam[:, 6:7]))
                act.sem_inc(ah_used, 1)
                act.dma_start(mixT[h][:, 0:LAT], amo[:]).then_inc(amo_stored, 16)
                st.leave(4)
            with act.Fori(0, 4) as h:
                st.enter(h, 1)
                act.wait_ge(mq_full, h * 2 + 1)
                act.activation(aq[:96, 0:LAT], PS[0][:96, 0:LAT], ACT.Copy).then_inc(mq_copied, 1)
                act.wait_ge(mq_full, h * 2 + 2)
                act.activation(kr[:64, :], PS[1][:64, 0:TOK], ACT.Copy).then_inc(mq_copied, 1)
                act.wait_ge(vt_full, h + 5)
                act.activation(vtk[:].rearrange("p n c -> p (n c)"), PS[1][:, 0:TOK], ACT.Copy).then_inc(vt_there, 1)
                tiles_act(act, h * MU + 4 * DU, h * LT + 4 * LT, 1, 96 ** -0.5)
                act.wait_ge(od_turned, h + 5)
                act.wait_ge(amo_stored, h * 16 + 64)
                st.link(act.activation(amo[:], PS[1][:, 0:LAT], ACT.Copy))
                act.sem_inc(ah_used, 1)
                act.dma_start(mixT[h + 4][:, 0:LAT], amo[:]).then_inc(amo_stored, 16)
                st.leave(4)
            act.wait_ge(amo_stored, 128)
            leave(act)

        def rotate(dve, st, dst, src, acc, tab):
            st.done(dve.tensor_tensor(arot[:acc.shape[0], 0:LAT], acc, tab[:, 1, :], ALU.mult))
            st.link(dve.tensor_tensor(dst, src, tab[:, 0, :], ALU.mult))
            return dve.tensor_tensor(dst, dst, arot[:acc.shape[0], 0:LAT], ALU.add)

        def attn_dve(dve, st):
            enter(dve, "attn")
            st.link(dve.memset(krr[:], 0.0))
            dve.sem_inc(kr_zero, 1)
            dve.wait_ge(at_full, 16 * N_TAB)
            dve.wait_ge(lat_root, 1)
            for b in range(2):
                st.link(dve.reciprocal(prob[b][:], prob[b][:]))
            for k in range(2):
                st.done(dve.scalar_tensor_tensor(cqn[:, k, :], cqn[:, k, :], vc2[:, V2_QN + k:V2_QN + k + 1], prob[0][:],
                                                 ALU.mult, ALU.mult))
            st.link(dve.scalar_tensor_tensor(ckvn[:], ckvn[:], vc2[:, V2_KVN:V2_KVN + 1], prob[1][:], ALU.mult, ALU.mult))
            dve.wait_ge(kr_rot, 1)
            st.done(dve.tensor_tensor(arot[64:96, 0:LAT], PM[64:96, :], rope_mla[64:96, 1, :], ALU.mult))
            st.link(dve.tensor_tensor(krr[64:96, 0:LAT], krr[64:96, 0:LAT], rope_mla[64:96, 0, :], ALU.mult))
            st.link(dve.tensor_tensor(krr[64:96, 0:LAT], krr[64:96, 0:LAT], arot[64:96, 0:LAT], ALU.add))
            dve.sem_inc(lat_n, 1)
            with dve.Fori(0, 4) as h:
                st.enter(h, 2 * 2 + tile_steps(2) + 4)
                for j, (dst, src) in enumerate(((qr[:], aq), (kr[:, 0:LAT], ak))):
                    dve.wait_ge(rot_full, h * 2 + j + 1)
                    rotate(dve, st, dst, src[:, 0:LAT], PS[j][:, 0:LAT], rope_da).then_inc(qk_rot, 1)
                    dve.wait_ge(qk_rot, h * 2 + j + 1)
                dve.wait_ge(kctx_there, h + 1)
                tiles_dve(dve, st, h * DU, h * LT, 2, 64 ** -0.5)
                flat = od[:].rearrange("p t c -> p (t c)")
                st.link(dve.tensor_tensor(arot[:, 0:LAT], flat, flat, ALU.mult))
                st.link(dve.tensor_reduce(ass[:], arot[:, 0:LAT].rearrange("p (t c) -> p t c", c=P), AX.X, ALU.add))
                dve.sem_inc(od_sq, 1)
                dve.wait_ge(od_root, h + 1)
                st.link(dve.reciprocal(ass[:], ass[:]))
                st.link(dve.tensor_tensor(od[:], od[:], ass[:].unsqueeze(2).broadcast_to([P, LT, P]), ALU.mult))
                dve.sem_inc(od_there, 1)
                st.leave(4)
            with dve.Fori(0, 4) as h:
                st.enter(h, 1 + 2 + tile_steps(1))
                dve.wait_ge(mq_copied, h * 2 + 2)
                st.link(dve.tensor_copy(kr[64:96, :], krr[64:96, :]))
                dve.wait_ge(rot_full, h + 9)
                rotate(dve, st, qr[:96, :], aq[:96, 0:LAT], PS[0][:96, 0:LAT], rope_mla).then_inc(qk_rot, 1)
                dve.wait_ge(qk_rot, h + 9)
                tiles_dve(dve, st, h * MU + 4 * DU, h * LT + 4 * LT, 1, 96 ** -0.5)
                dve.sem_inc(od_there, 1)
                st.leave(4)
            leave(dve)

        xo = [nc.alloc_sbuf_tensor_at(f"xo{b}", [P, KT, P], F32, offset=AREA + b * 4096) for b in range(2)]
        xrow = [nc.alloc_sbuf_tensor_at(f"xrow{b}", [P, D], F32, offset=AREA + 8192 + b * 4096) for b in range(2)]
        xo_there = [sem(f"xo_there{b}") for b in range(2)]
        out_stored = [sem(f"out_stored{b}") for b in range(2)]
        out_rows = out.rearrange("a (t p) d -> (a t) p d", p=P)

        def final_dve(dve, st):
            enter(dve, "final")
            dve.wait_ge(s_root, len(NORMS))
            st.link(dve.reciprocal(nrs[:, 0:LAT], nrs[:, 0:LAT]))
            with dve.Fori(0, LT // 2) as i:
                st.enter(i, 2)
                for b in range(2):
                    cols = bass.ds(i * (2 * P) + b * P, P)
                    dve.wait_ge(tile_turned[b], NT // 2 + i)
                    st.link(dve.tensor_tensor(xo[b][:], XT[:, :, cols], nrs[:, cols].unsqueeze(1).broadcast_to([P, KT, P]), ALU.mult))
                    dve.tensor_tensor(xo[b][:], xo[b][:], vc1[:, V1_FIN:V1_FIN + KT].unsqueeze(2).broadcast_to([P, KT, P]),
                                      ALU.mult).then_inc(xo_there[b], 1)
                st.leave(LT // 2)

        def final_pe(pe):
            norm_pe(pe, "final")
            with pe.Fori(0, LT // 2) as i:
                for b in range(2):
                    pe.wait_ge(xo_there[b], i + 1)
                    pe.wait_ge(tile_read[b], NT // 2 + i)
                    pe.wait_ge(s_root, len(NORMS))
                    for k in range(KT):
                        ins = pe.transpose(PS[b][:, k * P:(k + 1) * P], xo[b][:, k, :], ident[:])
                    ins.then_inc(tile_turned[b], 1)

        def final_act(act, st):
            norm_act(act, st, "final", split=False)
            with act.Fori(0, LT // 2) as i:
                for b in range(2):
                    act.wait_ge(tile_turned[b], NT // 2 + i + 1)
                    act.wait_ge(out_stored[b], i * 16)
                    act.activation(xrow[b][:], PS[b][:, 0:D], ACT.Copy).then_inc(tile_read[b], 1)
                    act.wait_ge(tile_read[b], NT // 2 + i + 1)
                    act.dma_start(out_rows[i * 2 + b], xrow[b][:]).then_inc(out_stored[b], 16)
            for b in range(2):
                act.wait_ge(out_stored[b], 16 * (LT // 2))

        block = ctx.enter_context(nc.Block())

        @block.sync
        def _(sp):
            load_sp(sp)
            ada_sp(sp)
            in0_sp(sp)
            hyena_sp(sp)
            hgrn_sp(sp)
            mix_sp(sp, 0, TOK)
            sp_linear(sp, "out0", w_src["out0"], KT)
            sp_ffn(sp, 0)
            sp_linear(sp, "in1", w_src["in1"], ODD_MAIN - 1)
            base = SLAB0["in1"] // 2 + (ODD_MAIN - 1) // 2
            sp_slab(sp, (0, base), w_src["in1"][:, :, (ODD_MAIN - 1) * P:ODD_MAIN * P])
            sp_slab(sp, (1, base), w_src["in1"][:, :, ODD_MAIN * P:ODD_MAIN * P + 32], lambda b: raw[b][:, :, 64:96])
            attn_sp(sp)
            mix_sp(sp, 1, LAT)
            sp_linear(sp, "out1", w_src["out1"], KT)
            sp_ffn(sp, 1)

        @block.gpsimd
        def _(pool):
            pool.memset(one_p[:], 1.0).then_inc(one_there, 1)
            pool.wait_ge(one_there, 1)
            for name, _ in GEMMS:
                if name.startswith("ffn"):
                    pool_ffn(pool, int(name[3]))
                else:
                    pool_linear(pool, name)

        @block.tensor
        def _(pe):
            st = Steps(pe, pe_step)
            load_pe(pe)
            ada_pe(pe)
            norm_pe(pe, "norm0")
            in0_pe(pe)
            hyena_pe(pe, st)
            hgrn_pe(pe, st)
            out_pe(pe, 0)
            norm_pe(pe, "normf0")
            ffn_pe(pe, 0)
            norm_pe(pe, "norm1")
            in_pe(pe, "in1", 16)
            attn_pe(pe, st)
            out_pe(pe, 1)
            norm_pe(pe, "normf1")
            ffn_pe(pe, 1)
            final_pe(pe)

        @block.scalar
        def _(act):
            st = Steps(act, act_step)
            ada_act(act, st)
            norm_act(act, st, "norm0")
            spill_act(act, "in0", 32)
            hyena_act(act, st)
            hgrn_act(act, st)
            mix_act(act, 0, TOK)
            norm_act(act, st, "normf0")
            ffn_act(act, 0)
            norm_act(act, st, "norm1")
            spill_act(act, "in1", 16)
            attn_act(act, st)
            mix_act(act, 1, LAT)
            norm_act(act, st, "normf1")
            ffn_act(act, 1)
            final_act(act, st)

        @block.vector
        def _(dve):
            st = Steps(dve, dve_step)
            load_dve(dve, st)
            ada_dve(dve, st)
            norm_dve(dve, st, "norm0")
            in0_dve(dve, st)
            hyena_dve(dve, st)
            hgrn_dve(dve, st)
            mix_dve(dve, 0, TOK)
            out_dve(dve, 0)
            norm_dve(dve, st, "normf0")
            ffn_dve(dve, 0)
            norm_dve(dve, st, "norm1")
            attn_dve(dve, st)
            mix_dve(dve, 1, LAT)
            out_dve(dve, 1)
            norm_dve(dve, st, "normf1")
            ffn_dve(dve, 1)
            final_dve(dve, st)


_INS = ['x', 'c', 'ctx', 'c_ctx', 'ada_w', 'ada_b', 'norm_mix_g', 'norm_ffn_g', 'ffn_w_gu', 'ffn_w_down', 'ev_w_in',
        'ev_w_out', 'hg_lower_bound', 'hg_out_norm_g', 'hy_short_w', 'hy_short_b', 'hy_filt_w1', 'hy_filt_b1',
        'hy_filt_freq1', 'hy_filt_w2', 'hy_filt_b2', 'hy_filt_freq2', 'hy_filt_w3', 'hy_skip', 'od_w_in', 'od_w_out',
        'da_lambda', 'da_subln_g', 'mla_q_norm_g', 'mla_w_uq', 'mla_kv_norm_g', 'mla_w_ukv', 'final_norm_g']


def kernel(**inputs):
    import numpy as _np
    import concourse.bacc as _bacc
    from concourse import mybir as _mybir
    from concourse.bass_utils import run_bass_kernel_spmd as _run

    nc = _bacc.Bacc("TRN2", target_bir_lowering=False, num_devices=1)
    arrays, T = {}, {}
    given = {n: _np.ascontiguousarray(inputs[n]) for n in _INS}
    given.update(constants())
    for name, a in given.items():
        arrays[f"in_{name}_dram"] = a
        T[name] = nc.dram_tensor(f"in_{name}_dram", a.shape, _mybir.dt.from_np(a.dtype), kind="ExternalInput").ap()
    out = nc.dram_tensor("out_dram", (1, LAT, D), _mybir.dt.float32, kind="ExternalOutput").ap()
    scratch = {n: nc.dram_tensor(n + "_dram", s, _mybir.dt.float32, kind="Internal").ap() for n, s in SCRATCH.items()}
    build(nc, T, out, scratch)
    r = _run(nc, [arrays], core_ids=[0])
    return r.results[0]["out_dram"]
```

```python
import math
from contextlib import ExitStack

import numpy as np

import concourse.bass as bass
from concourse import mybir

F32 = mybir.dt.float32
F32R = mybir.dt.float32r
ALU = mybir.AluOpType
ACT = mybir.ActivationFunctionType
AX = mybir.AxisListType

P = 128
D = 1024
KT = D // P
LAT, CTX = 1024, 256
TOK = LAT + CTX
NT = TOK // P
LT = LAT // P
CT = CTX // P
EPS = 1e-6
FFN = ((8 * D + 3 * 256 - 1) // (3 * 256)) * 256
FT = FFN // P
FG = FT // 2
EVEN_IN = 4096
ODD_MAIN = 15
GRID_W = 64
ROPE_BASE = 10000.0
HW = 512
HY_EMB, HY_F = 33, 64
LAM_INIT = 0.8 - 0.6 * math.exp(-0.3)
HALF = 64
LEVELS = 7
MAGIC = 12582912.0
TWO_PI_A = 6.28125
TWO_PI_B = float(np.float32(np.float64(2 * math.pi) - 6.28125))
TWO_PI_C = float(np.float32(2 * math.pi - 6.28125 - np.float64(np.float32(2 * math.pi - 6.28125))))
PI_CLAMP = 3.1415925

V1_ADA, V1_C, V1_CC, V1_FIN = 0, 96, 104, 112
V1_ROWS = 120
V2_MIX, V2_FFN, V2_SW, V2_SB, V2_SKIP, V2_HG, V2_SUB, V2_QN, V2_KVN = 0, 16, 32, 68, 80, 84, 85, 86, 88
V2_ROWS = 89

FULL_CHUNKS = [(0, 512), (512, 512), (1024, 256)]
LAT_CHUNKS = [(0, 512), (512, 512)]

GEMMS = [("in0", 32), ("out0", 8), ("ffn0", 6 * FG), ("in1", 16), ("out1", 8), ("ffn1", 6 * FG)]
SLAB0, USE0 = {}, {}
_s = _u = 0
for _n, _k in GEMMS:
    SLAB0[_n], USE0[_n] = _s, _u
    _s += _k
    _u += 12 * FG if _n.startswith("ffn") else _k
PHASES = [("load", 2), ("ada", 3), ("norm0", 3), ("in0", 3), ("hyena", 3), ("hgrn", 4), ("mix0", 2), ("out0", 2),
          ("normf0", 3), ("ffn0", 3), ("norm1", 3), ("in1", 2), ("attn", 3), ("mix1", 2), ("out1", 2),
          ("normf1", 3), ("ffn1", 3), ("final", 3)]
BEFORE = {}
_c = 0
for _n, _k in PHASES:
    BEFORE[_n] = _c
    _c += _k


def constants():
    f = np.float32
    out = {"ident": np.eye(P, dtype=f)}
    s, t = np.meshgrid(np.arange(P), np.arange(P), indexing="ij")
    masks = [(s // (2 << l) == t // (2 << l)) & ((s >> l) % 2 != (t >> l) % 2) for l in range(LEVELS)]
    out["levelmask"] = np.stack([np.eye(P, dtype=bool)] + masks, 1).astype(f)
    pos, negt, negts = [], [], []
    for L in (LAT, CTX):
        tt = np.linspace(0.0, 1.0, L, dtype=f)[:, None]
        w = (2.0 * math.pi * np.arange(L, dtype=f)[:, None] / L).astype(f)
        bands = np.linspace(1e-4, 15, 16, dtype=f)[None, :]
        pos.append(np.concatenate([tt, np.cos(bands * w), -np.sin(bands * w)], -1).astype(f).T)
        negt.append(-tt[:, 0])
        negts.append(-np.concatenate([tt[:1, 0], tt[:-1, 0]]))
    out["pos"] = np.ascontiguousarray(np.concatenate(pos, 1))
    out["negt"] = np.ascontiguousarray(
        np.stack([np.concatenate(negt).reshape(NT, P).T, np.concatenate(negts).reshape(NT, P).T], 1)).astype(f)
    out["delta"] = np.linspace(-math.log(1e-2) / 1.5, -math.log(1e-2) / 0.3, HW, dtype=f)
    for name, L in (("lat", LAT), ("ctx", CTX)):
        n = L // P
        i = np.arange(L, dtype=np.int64)
        ang = math.pi / (2 * L) * (np.outer(i, 2 * i + 1) % (4 * L))
        c, sn = np.cos(ang).astype(f), np.sin(ang).astype(f)
        cs = np.stack([c, sn])
        out["dft_" + name] = np.ascontiguousarray(
            cs.reshape(2, n, P, n, P).transpose(3, 2, 0, 1, 4).reshape(n, P, 2, n * P))
        inv = np.stack([c.T, -sn.T])
        w = min(512, L)
        out["inv_" + name] = np.ascontiguousarray(
            inv.reshape(2, n, P, L // w, w).transpose(3, 1, 2, 0, 4))
    tok = np.arange(LAT)
    row, col = tok // GRID_W, tok % GRID_W

    def rope(width):
        half = width // 2
        q = half // 2
        inv = (ROPE_BASE ** (-np.arange(q, dtype=f) / q)).astype(f)
        cos, sin = np.zeros((width, LAT), f), np.zeros((width, LAT), f)
        rot = np.zeros((width, width), f)
        for part, where in enumerate((row, col)):
            ang = inv[:, None] * where[None].astype(f)
            for a in range(2):
                r = part * half + a * q
                cos[r:r + q], sin[r:r + q] = np.cos(ang), np.sin(ang)
            for d in range(q):
                x1, x2 = part * half + d, part * half + q + d
                rot[x2, x1] = -1.0
                rot[x1, x2] = 1.0
        return cos, sin, rot

    c, sn, r = rope(64)
    out["rope_da"] = np.ascontiguousarray(np.stack([np.tile(c, (2, 1)), np.tile(sn, (2, 1))], 1))
    out["rot_da"] = np.kron(np.eye(2, dtype=f), r)
    c, sn, r = rope(32)
    cc = np.concatenate([np.ones((64, LAT), f), c])
    ss = np.concatenate([np.zeros((64, LAT), f), sn])
    out["rope_mla"] = np.ascontiguousarray(np.stack([cc, ss], 1))
    rot = np.zeros((96, 96), f)
    rot[64:, 64:] = r
    out["rot_mla"] = rot
    return out


class Steps:

    def __init__(self, eng, sem):
        self.eng, self.sem, self.base, self.k = eng, sem, 0, 0

    def done(self, ins):
        ins.then_inc(self.sem, 1)
        self.k += 1

    def settle(self):
        self.eng.wait_ge(self.sem, self.base + self.k)

    def link(self, ins):
        self.done(ins)
        self.settle()

    def enter(self, i, per):
        self.saved, self.per = self.base + self.k, per
        self.base, self.k = self.saved + i * per, 0

    def leave(self, n):
        assert self.k == self.per, (self.k, self.per)
        self.base, self.k = self.saved + n * self.per, 0


SCRATCH = {"fspec": (NT, P, 2, HW), "zT": (32, P, TOK), "mixT": (KT, P, TOK)}


def build(nc, T, out, scratch):
    with ExitStack() as ctx:
        def sem(name):
            return ctx.enter_context(nc.semaphore(name))

        fence = ctx.enter_context(nc.sbuf_tensor("fence", [P, 212000 - 128], mybir.dt.uint8))
        START = 16512
        END = START + 212000 - 256
        size = {F32: 4, F32R: 4}

        class Area:
            def __init__(self, at):
                self.at = at

            def __call__(self, name, shape, dt=F32):
                n = int(np.prod(shape[1:])) * size[dt]
                t = nc.alloc_sbuf_tensor_at(name, shape, dt, offset=self.at)
                self.at += (n + 31) // 32 * 32
                assert self.at <= END, (name, self.at - END)
                return t

        keep = Area(START)
        XT = keep("XT", [P, KT, TOK])
        raw = [keep(f"raw{b}", [P, KT, P]) for b in range(2)]
        WH = [keep(f"WH{b}", [P, KT, P], F32R) for b in range(2)]
        WL = [keep(f"WL{b}", [P, KT, P], F32R) for b in range(2)]
        ident = keep("ident", [P, P])
        ones = keep("ones", [P, P])
        vc1 = keep("vc1", [P, V1_ROWS])
        vc2 = keep("vc2", [P, V2_ROWS])
        mod = keep("mod", [P, 96, 2])
        gsc = keep("gsc", [P, 4, KT, 2])
        one_p = keep("one_p", [P, KT])
        csc = keep("csc", [P, KT, 2])
        lam = keep("lam", [P, 8])
        fcol = keep("fcol", [HY_F, 4])
        AREA = keep.at
        a = Area(AREA)
        AH = a("AH", [P, KT, TOK], F32R)
        AL = a("AL", [P, KT, TOK], F32R)
        AREA_B = a.at

        ALL = ctx.enter_context(nc.psum_tensor("ALL", [P, 8 * 512], F32))
        PS = [ALL[:, b * 1536:(b + 1) * 1536] for b in range(2)]
        PM = ALL[:, 3072:4096]

        pool_step = sem("pool_step")
        phase_done = sem("phase_done")
        raw_full = [sem(f"raw_full{b}") for b in range(2)]
        high_done = [sem(f"high_done{b}") for b in range(2)]
        w_ready = [sem(f"w_ready{b}") for b in range(2)]
        acc_full = [sem(f"acc_full{b}") for b in range(2)]
        acc_free = [sem(f"acc_free{b}") for b in range(2)]
        dve_step, act_step, pe_step = sem("dve_step"), sem("act_step"), sem("pe_step")

        def enter(eng, name):
            if BEFORE[name]:
                eng.wait_ge(phase_done, BEFORE[name])

        def leave(eng, last=None):
            eng.sem_inc(phase_done, 1)

        zT, mixT = scratch["zT"], scratch["mixT"]

        def slab_in(w, k_rows=D):
            return w.rearrange("(k p) n -> p k n", p=P)

        w_src = {
            "in0": slab_in(T["ev_w_in"][0]), "out0": slab_in(T["ev_w_out"][0]),
            "in1": slab_in(T["od_w_in"][0]), "out1": slab_in(T["od_w_out"][0]),
            "gu0": slab_in(T["ffn_w_gu"][0]), "gu1": slab_in(T["ffn_w_gu"][1]),
        }
        down = [T["ffn_w_down"][l].rearrange("(g j p) n -> g p j n", j=2, p=P) for l in range(2)]

        def sp_slab(sp, n, src, dst=None):
            b, use = n
            sp.wait_ge(w_ready[b], use)
            sp.dma_start(raw[b][:] if dst is None else dst(b), src).then_inc(raw_full[b], 16)

        def sp_linear(sp, name, src, slabs):
            base = SLAB0[name] // 2
            with sp.Fori(0, slabs // 2) as i:
                for b in range(2):
                    sp_slab(sp, (b, base + i), src[:, :, bass.ds(i * (2 * P) + b * P, P)])

        def sp_ffn(sp, l):
            base = SLAB0[f"ffn{l}"] // 2
            gu = w_src[f"gu{l}"]

            def up(i, at):
                for j in range(2):
                    for half in range(2):
                        sp_slab(sp, (half, at + j), gu[:, :, bass.ds(i * 256 + (half * FFN + j * P), P)])

            def dn(i, at):
                for b in range(2):
                    sp_slab(sp, (b, at), down[l][i, :, :, b * 512:(b + 1) * 512],
                            lambda b: raw[b][:].rearrange("p (j a) c -> p j (a c)", j=2))

            up(0, base)
            with sp.Fori(0, FG - 1) as i:
                up(i + 1, base + 2 + i * 3)
                dn(i, base + 4 + i * 3)
            dn(FG - 1, base + 2 + 3 * (FG - 1))

        def pool_slab(pool, b, n, freed):
            pool.wait_ge(raw_full[b], 16 * (n + 1) if isinstance(n, int) else n * 16 + 16)
            pool.wait_ge(*freed)
            pool.tensor_tensor(WH[b][:], raw[b][:], one_p[:].unsqueeze(2).broadcast_to([P, KT, P]),
                               ALU.mult).then_inc(high_done[b], 1)
            pool.wait_ge(high_done[b], n + 1)
            pool.tensor_tensor(WL[b][:], raw[b][:], WH[b][:].bitcast(F32), ALU.subtract).then_inc(w_ready[b], 1)

        def pool_linear(pool, name):
            base, use = SLAB0[name] // 2, USE0[name] // 2
            with pool.Fori(0, dict(GEMMS)[name] // 2) as i:
                for b in range(2):
                    pool_slab(pool, b, base + i, (acc_full[b], use + i))

        def pool_ffn(pool, l):
            s, u = SLAB0[f"ffn{l}"] // 2, USE0[f"ffn{l}"] // 2

            def up(s, u, after_down):
                for j in range(2):
                    for b in range(2):
                        freed = (acc_full[1], u - 2) if after_down and (j, b) == (0, 0) else (acc_full[b], u + j)
                        pool_slab(pool, b, s + j, freed)

            def dn(s, u, after_down):
                for b in range(2):
                    pool_slab(pool, b, s, (acc_full[1], u - 2) if after_down and b == 0 else (acc_full[b], u))

            up(s, u, False)
            up(s + 2, u + 2, False)
            dn(s + 4, u + 4, False)
            with pool.Fori(1, FG - 1) as i:
                up(s + 2 + i * 3, u + 2 + i * 6, True)
                dn(s + 4 + i * 3, u + 4 + i * 6, False)
            dn(s + 2 + 3 * (FG - 1), u + 2 + 6 * (FG - 1), True)

        def products(pe, acc, chunks, kts, wh, wl, xh, xl):
            last = len(kts) - 1
            for n, k in enumerate(kts):
                for m, (w, x) in enumerate(((wh, xh), (wh, xl), (wl, xh))):
                    for at, width in chunks:
                        ins = pe.matmul(acc[:, at:at + width], w(k), x(k, at, width),
                                        start=(n == 0 and m == 0), stop=(n == last and m == 2),
                                        skip_group_check=True)
            return ins

        def full_slab(pe, b, chunks):
            return products(pe, PS[b], chunks, range(KT),
                            lambda k: WH[b][:, k, :], lambda k: WL[b][:, k, :],
                            lambda k, at, w: AH[:, k, at:at + w], lambda k, at, w: AL[:, k, at:at + w])

        def pe_linear(pe, name, slabs, chunks):
            base, use = SLAB0[name] // 2, USE0[name] // 2
            with pe.Fori(0, slabs // 2) as i:
                for b in range(2):
                    pe.wait_ge(w_ready[b], base + i + 1)
                    pe.wait_ge(acc_free[b], use + i)
                    full_slab(pe, b, chunks).then_inc(acc_full[b], 1)
            for b in range(2):
                pe.wait_ge(acc_full[b], use + slabs // 2)

        nb = Area(AREA_B)
        nsq = [nb(f"nsq{b}", [P, TOK]) for b in range(2)]
        ntmp = [nb(f"ntmp{b}", [P, TOK]) for b in range(2)]
        nhn = [nb(f"nhn{b}", [P, TOK]) for b in range(2)]
        nrs = nb("nrs", [P, TOK])
        s_sq = sem("s_sq")
        s_pair = sem("s_pair")
        s_ss = sem("s_ss")
        s_root = sem("s_root")
        s_scaled = sem("s_scaled")
        s_hn = sem("s_hn")
        s_low = sem("s_low")
        NORMS = ["norm0", "normf0", "norm1", "normf1", "final"]

        def norm_chunks(name):
            return LAT_CHUNKS if name in ("normf1", "final") else FULL_CHUNKS

        NP = KT // 2

        def norm_pe(pe, name):
            enter(pe, name)
            z = NORMS.index(name)
            for p in range(NP):
                pe.wait_ge(s_pair, NP * z + p + 1)
                for at, w in norm_chunks(name):
                    ins = pe.matmul(PS[0][:, at:at + w], ones[:], ntmp[p % 2][:, at:at + w], start=(p == 0),
                                    stop=(p == NP - 1), skip_group_check=True)
                ins.then_inc(s_ss, 1)
            pe.wait_ge(s_ss, NP * (z + 1))
            leave(pe)

        def square(k):
            return (nsq, nhn)[k // 2 % 2][k % 2]

        def norm_pairs(dve, name):
            z = NORMS.index(name)
            n = LAT if len(norm_chunks(name)) == 2 else TOK
            for p in range(NP):
                dve.wait_ge(s_sq, KT * z + 2 * p + 2)
                if p >= 2:
                    dve.wait_ge(s_ss, NP * z + p - 1)
                dve.tensor_tensor(ntmp[p % 2][:, :n], square(2 * p)[:, :n], square(2 * p + 1)[:, :n], ALU.add).then_inc(s_pair, 1)

        def norm_act(act, st, name, split=True):
            enter(act, name)
            z = NORMS.index(name)
            n = LAT if len(norm_chunks(name)) == 2 else TOK
            for k in range(KT):
                if k >= 4:
                    act.wait_ge(s_pair, NP * z + k // 2 - 1)
                act.activation(square(k)[:, :n], XT[:, k, :n], ACT.Square).then_inc(s_sq, 1)
            act.wait_ge(s_ss, NP * (z + 1))
            st.link(act.activation(nrs[:, :n], PS[0][:, :n], ACT.Ln, bias=eps_col[:, 0:1], scale=1.0 / D))
            act.activation(nrs[:, :n], nrs[:, :n], ACT.Exp, scale=-0.5).then_inc(s_root, 1)
            if not split:
                act.wait_ge(s_root, z + 1)
                return
            l = 0 if name in ("norm0", "normf0") else 1
            which = 0 if name in ("norm0", "norm1") else 1
            g, shift = l * 2 + which, l * 48 + which * 24
            for k in range(KT):
                act.wait_ge(s_scaled, KT * z + k + 1)
                if k >= 2:
                    act.wait_ge(s_low, KT * z + k - 1)
                for seg in range(2 if n == TOK else 1):
                    at, w = ((0, LAT), (LAT, CTX))[seg]
                    st.done(act.activation(nhn[k % 2][:, at:at + w], ntmp[k % 2][:, at:at + w], ACT.Identity,
                                           bias=mod[:, shift + k, seg:seg + 1], scale=gsc[:, g, k, seg:seg + 1]))
                st.settle()
                act.activation(AH[:, k, :n], nhn[k % 2][:, :n], ACT.Copy).then_inc(s_hn, 1)
            act.wait_ge(s_hn, KT * (z + 1))
            leave(act)

        def norm_dve(dve, st, name):
            enter(dve, name)
            z = NORMS.index(name)
            n = LAT if len(norm_chunks(name)) == 2 else TOK
            norm_pairs(dve, name)
            dve.wait_ge(s_root, z + 1)

            def scale(k):
                if k >= 2:
                    dve.wait_ge(s_hn, KT * z + k - 1)
                dve.tensor_tensor(ntmp[k % 2][:, :n], XT[:, k, :n], nrs[:, :n], ALU.mult).then_inc(s_scaled, 1)

            def low(k):
                dve.wait_ge(s_hn, KT * z + k + 1)
                dve.tensor_tensor(AL[:, k, :n], nhn[k % 2][:, :n], AH[:, k, :n].bitcast(F32),
                                  ALU.subtract).then_inc(s_low, 1)

            scale(0)
            for k in range(KT):
                if k + 1 < KT:
                    scale(k + 1)
                low(k)
            dve.wait_ge(s_low, KT * (z + 1))
            leave(dve)

        eps_col = nc.alloc_sbuf_tensor_at("eps_col", [P, 1], F32, offset=END)

        lb = Area(AREA_B)
        xs = [lb(f"xs{b}", [P, D]) for b in range(2)]
        vr1 = lb("vr1", [V1_ROWS, P])
        vr2 = lb("vr2", [V2_ROWS, P])
        lrow = lb("lrow", [P, 4, HALF])
        lprod = lb("lprod", [P, 2, HALF])
        const_full = sem("const_full")
        xs_full = [sem(f"xs_full{b}") for b in range(2)]
        tile_turned = [sem(f"tile_turned{b}") for b in range(2)]
        tile_read = [sem(f"tile_read{b}") for b in range(2)]
        vec_turned = sem("vec_turned")
        x_rows = T["x"].rearrange("a (t p) d -> (a t) p d", p=P)
        ctx_rows = T["ctx"].rearrange("a (t p) d -> (a t) p d", p=P)

        def rows(ap):
            return ap.rearrange("(r p) -> r p", p=P)

        def load_sp(sp):
            n = 0

            def ld(dst, src):
                nonlocal n
                sp.dma_start(dst, src).then_inc(const_full, 16)
                n += 1

            ld(ident[:], T["ident"])
            ld(vr1[V1_ADA:V1_ADA + 96, :], T["ada_b"].rearrange("l (r p) -> (l r) p", p=P))
            ld(vr1[V1_C:V1_C + 8, :], T["c"].rearrange("a (r p) -> (a r) p", p=P))
            ld(vr1[V1_CC:V1_CC + 8, :], rows(T["c_ctx"]))
            ld(vr1[V1_FIN:V1_FIN + 8, :], rows(T["final_norm_g"]))
            ld(vr2[V2_MIX:V2_MIX + 16, :], T["norm_mix_g"].rearrange("l (r p) -> (l r) p", p=P))
            ld(vr2[V2_FFN:V2_FFN + 16, :], T["norm_ffn_g"].rearrange("l (r p) -> (l r) p", p=P))
            ld(vr2[V2_SW:V2_SW + 36, :], T["hy_short_w"].rearrange("a l (r p) -> (a l r) p", p=P))
            ld(vr2[V2_SB:V2_SB + 12, :], T["hy_short_b"].rearrange("a (r p) -> (a r) p", p=P))
            ld(vr2[V2_SKIP:V2_SKIP + 4, :], T["hy_skip"].rearrange("a (r p) -> (a r) p", p=P))
            ld(vr2[V2_HG:V2_HG + 1, :], T["hg_out_norm_g"])
            ld(vr2[V2_SUB:V2_SUB + 1, :], T["da_subln_g"])
            ld(vr2[V2_QN:V2_QN + 2, :], T["mla_q_norm_g"].rearrange("a (r p) -> (a r) p", p=P))
            ld(vr2[V2_KVN:V2_KVN + 1, :], T["mla_kv_norm_g"])
            ld(lrow[:], T["da_lambda"][0].partition_broadcast(P))
            for j, name in enumerate(("hy_filt_b1", "hy_filt_freq1", "hy_filt_b2", "hy_filt_freq2")):
                ld(fcol[:, j:j + 1], T[name].rearrange("a f -> f a"))
            assert n == N_CONST

            def tile(b, use, src):
                sp.wait_ge(tile_turned[b], use)
                sp.dma_start(xs[b][:], src).then_inc(xs_full[b], 16)

            with sp.Fori(0, LT // 2) as i:
                for b in range(2):
                    tile(b, i, x_rows[i * 2 + b])
            for b in range(2):
                tile(b, LT // 2, ctx_rows[b])

        N_CONST = 19

        def load_pe(pe):
            pe.wait_ge(const_full, 16 * N_CONST)
            pe.transpose(PM[:, 0:V1_ROWS], vr1[:], ident[:V1_ROWS, :V1_ROWS])
            pe.transpose(PM[:, 128:128 + V2_ROWS], vr2[:], ident[:V2_ROWS, :V2_ROWS]).then_inc(vec_turned, 1)

            def tile(b, use):
                pe.wait_ge(xs_full[b], 16 * (use + 1))
                pe.wait_ge(tile_read[b], use)
                for k in range(KT):
                    ins = pe.transpose(PS[b][:, k * P:(k + 1) * P], xs[b][:, k * P:(k + 1) * P], ident[:])
                ins.then_inc(tile_turned[b], 1)

            with pe.Fori(0, NT // 2) as i:
                for b in range(2):
                    tile(b, i)
            for b in range(2):
                pe.wait_ge(tile_turned[b], NT // 2)
            leave(pe)

        def load_dve(dve, st):
            st.link(dve.memset(ones[:], 1.0))
            st.link(dve.memset(eps_col[:], EPS))
            dve.wait_ge(vec_turned, 1)
            st.link(dve.tensor_copy(vc1[:], PM[:, 0:V1_ROWS]))
            st.link(dve.tensor_copy(vc2[:], PM[:, 128:128 + V2_ROWS]))
            st.link(dve.tensor_tensor(lprod[:, 0, :], lrow[:, 0, :], lrow[:, 1, :], ALU.mult))
            st.link(dve.tensor_tensor(lprod[:, 1, :], lrow[:, 2, :], lrow[:, 3, :], ALU.mult))
            st.link(dve.tensor_reduce(lam[:, 0:2], lprod[:], AX.X, ALU.add))
            with dve.Fori(0, NT // 2) as i:
                for b in range(2):
                    dve.wait_ge(tile_turned[b], i + 1)
                    dve.tensor_copy(XT[:, :, bass.ds(i * (2 * P) + b * P, P)],
                                    PS[b][:, 0:D].rearrange("p (k c) -> p k c", c=P)).then_inc(tile_read[b], 1)
            for b in range(2):
                dve.wait_ge(tile_read[b], NT // 2)
            leave(dve)

        ab = Area(AREA)
        NADA = 4
        aw = [ab(f"aw{b}", [P, KT, 256]) for b in range(NADA)]
        Pt = ab("Pt", [P, NT, HW])
        Mt = ab("Mt", [P, NT, HW])
        MLP_AT = ab.at
        pos = ab("pos", [HY_EMB, TOK])
        farg = ab("farg", [HY_F, TOK])
        fint = ab("fint", [HY_F, TOK])
        h1 = ab("h1", [HY_F, TOK])
        MLP_END = ab.at
        h2p = ab("h2p", [HY_F, TOK + 2])
        w1 = ab("w1", [HY_EMB, HY_F])
        w2 = ab("w2", [HY_F, HY_F])
        w3 = ab("w3", [HY_F, 2 * HW])
        delta = ab("delta", [P, HW])
        negt = ab("negt", [P, 2, NT])
        absum = [ab(f"absum{b}", [P, HW]) for b in range(2)]
        dec = [ab(f"dec{b}", [P, 2, HW]) for b in range(2)]
        fa = [ab(f"fa{b}", [P, HW]) for b in range(2)]
        fg = [ab(f"fg{b}", [P, HW]) for b in range(2)]
        invn = ab("invn", [P, 2, HW])
        fst = [ab(f"fst{b}", [P, 2, HW]) for b in range(2)]
        mlp = Area(MLP_AT)
        fslab = [mlp(f"fslab{b}", [P, 2, LT, P]) for b in range(2)]
        assert mlp.at <= MLP_END
        a1b = Area(AREA_B + 2 * TOK * 4)
        aw1 = [a1b(f"aw1_{b}", [P, KT, 256]) for b in range(2)]
        apart = [a1b(f"apart{b}", [P, 2, 256]) for b in range(2)]
        ADA_ACC = ALL[:, 7 * 512:7 * 512 + 192]
        SUM_ACC = [ALL[:, 6 * 512:7 * 512], ALL[:, 5 * 512:6 * 512]]

        aw_full = [sem(f"aw_full{b}") for b in range(NADA)]
        aw_used = [sem(f"aw_used{b}") for b in range(NADA)]
        apart_there = sem("apart_there")
        apart_used = [sem(f"apart_used{b}") for b in range(2)]
        csc_there = sem("csc_there")
        filt_in, mlp_full, sin_in, sin_out = sem("filt_in"), sem("mlp_full"), sem("sin_in"), sem("sin_out")
        tap_full, dec_there, tap_read, abs_there, abs_used = (
            sem("tap_full"), sem("dec_there"), sem("tap_read"), sem("abs_there"), sem("abs_used"))
        taps_there = sem("taps_there")
        fs_full = [sem(f"fs_full{b}") for b in range(2)]
        filt_full = [sem(f"filt_full{b}") for b in range(2)]
        filt_scaled = [sem(f"filt_scaled{b}") for b in range(2)]
        filt_stored = [sem(f"filt_stored{b}") for b in range(2)]
        ada_w = T["ada_w"].rearrange("l (k p) n -> l p k n", p=P)
        fspec = scratch["fspec"]
        SLABS = 6 * D // 256
        N_FILT = 6
        ADA_NOW = 16
        assert ADA_NOW >= NADA + NT and ADA_NOW % NADA == 0

        def ada_slab_sp(sp, n):
            b = n % NADA
            if n >= NADA:
                sp.wait_ge(aw_used[b], n // NADA)
            sp.dma_start(aw[b][:], ada_w[0][:, :, n * 256:(n + 1) * 256]).then_inc(aw_full[b], 16)

        def ada_slab_pe(pe, n):
            b = n % NADA
            pe.wait_ge(aw_full[b], 16 * (n // NADA + 1))
            ada_products(pe, aw[b], lambda j: ADA_ACC[:, n * 4 + 2 * j:n * 4 + 2 * j + 2]).then_inc(aw_used[b], 1)

        def ada_products(pe, w, acc):
            for j in range(2):
                for k in range(KT):
                    ins = pe.matmul(acc(j), w[:, k, j * P:(j + 1) * P], csc[:, k, :], start=(k == 0), stop=(k == KT - 1),
                                    skip_group_check=True)
            return ins

        def ada_sp(sp):
            for n in range(NADA):
                ada_slab_sp(sp, n)
            enter(sp, "ada")
            for dst, name in ((pos, "pos"), (w1, "hy_filt_w1"), (w2, "hy_filt_w2"), (w3, "hy_filt_w3"), (negt, "negt")):
                sp.dma_start(dst[:], T[name][0] if name.startswith("hy") else T[name]).then_inc(filt_in, 16)
            sp.dma_start(delta[:], T["delta"].partition_broadcast(P)).then_inc(filt_in, 16)
            for n in range(NADA, ADA_NOW):
                ada_slab_sp(sp, n)
            sp.wait_ge(sin_out, 2)
            for kk in range(NT):
                b = kk % 2
                if kk >= 2:
                    sp.wait_ge(filt_full[b], kk // 2)
                if kk < LT:
                    sp.dma_start(fslab[b][:].rearrange("p q k c -> p q (k c)"), T["dft_lat"][kk]).then_inc(fs_full[b], 16)
                else:
                    sp.dma_start(fslab[b][:, :, 0:CT, :].rearrange("p q k c -> p q (k c)"),
                                 T["dft_ctx"][kk - LT]).then_inc(fs_full[b], 16)

        def ada_act(act, st):
            enter(act, "ada")
            st.done(act.activation(csc[:, :, 0], vc1[:, V1_C:V1_C + 8], ACT.Silu))
            st.done(act.activation(csc[:, :, 1], vc1[:, V1_CC:V1_CC + 8], ACT.Silu))
            st.settle()
            act.sem_inc(csc_there, 1)
            st.link(act.activation(lam[:, 2:4], lam[:, 0:2], ACT.Exp))
            act.sem_inc(csc_there, 1)
            act.wait_ge(filt_in, 16 * N_FILT)
            for layer in range(2):
                act.wait_ge(sin_in, layer + 1)
                if layer == 0:
                    st.link(act.activation(h1[:], farg[:], ACT.Sin))
                else:
                    st.done(act.activation(h2p[:, 1:LAT + 1], farg[:, 0:LAT], ACT.Sin))
                    st.link(act.activation(h2p[:, LAT + 2:], farg[:, LAT:], ACT.Sin))
                act.sem_inc(sin_out, 1)
            for tt in range(NT):
                b = tt % 2
                if tt >= 2:
                    act.wait_ge(tap_read, tt - 1)
                for s in range(2):
                    st.done(act.activation(dec[b][:, s, :], delta[:], ACT.Exp, scale=negt[:, s, tt:tt + 1]))
                st.settle()
                act.sem_inc(dec_there, 1)
            for kk in range(NT):
                b = kk % 2
                act.wait_ge(filt_scaled[b], kk // 2 + 1)
                act.dma_start(fspec[kk], fst[b][:]).then_inc(filt_stored[b], 16)
            for b in range(2):
                act.wait_ge(filt_stored[b], 16 * (NT // 2))
            leave(act)

        def ada_pe(pe):
            enter(pe, "ada")
            pe.wait_ge(csc_there, 1)
            pe.wait_ge(filt_in, 16 * N_FILT)
            for at, w in FULL_CHUNKS:
                ins = pe.matmul(PS[0][:HY_F, at:at + w], w1[:], pos[:, at:at + w], start=True, stop=True)
            ins.then_inc(mlp_full, 1)
            for n in range(NADA):
                ada_slab_pe(pe, n)
            pe.wait_ge(sin_out, 1)
            for at, w in FULL_CHUNKS:
                ins = pe.matmul(PS[1][:HY_F, at:at + w], w2[:], h1[:, at:at + w], start=True, stop=True)
            ins.then_inc(mlp_full, 1)
            pe.wait_ge(sin_out, 2)

            def sums(tt):
                pe.wait_ge(abs_there, tt + 1)
                pe.matmul(SUM_ACC[0 if tt < LT else 1], ones[:], absum[tt % 2][:], start=tt in (0, LT),
                          stop=tt in (LT - 1, NT - 1), skip_group_check=True).then_inc(abs_used, 1)

            for tt in range(NT):
                b = tt % 2
                if tt >= 2:
                    pe.wait_ge(tap_read, tt - 1)
                at = tt * P + (1 if tt < LT else 2)
                pe.matmul(PS[b][:, 0:HW], h2p[:, at:at + P], w3[:, 0:HW], start=True, stop=True)
                pe.matmul(PS[b][:, HW:2 * HW], h2p[:, at - 1:at - 1 + P], w3[:, HW:2 * HW], start=True,
                          stop=True).then_inc(tap_full, 1)
                if tt:
                    sums(tt - 1)
                ada_slab_pe(pe, NADA + tt)
            for n in range(NADA + NT, ADA_NOW):
                ada_slab_pe(pe, n)
            sums(NT - 1)
            pe.wait_ge(taps_there, 1)
            for kk in range(NT):
                b, tts = kk % 2, range(LT) if kk < LT else range(LT, NT)
                pe.wait_ge(fs_full[b], 16 * (kk // 2 + 1))
                if kk >= 2:
                    pe.wait_ge(filt_scaled[b], kk // 2)
                for q, src in ((0, Pt), (1, Mt)):
                    for m, tt in enumerate(tts):
                        ins = pe.matmul(PS[b][:, q * HW:(q + 1) * HW], fslab[b][:, q, m, :], src[:, tt, :], start=(m == 0),
                                        stop=(m == len(tts) - 1), skip_group_check=True)
                ins.then_inc(filt_full[b], 1)
            for b in range(NADA):
                pe.wait_ge(aw_used[b], ADA_NOW // NADA)
            leave(pe)

        def modulation(dve, st, n0, n1, norms):
            st.link(dve.tensor_tensor(mod[:, n0:n1, :], ADA_ACC[:, 2 * n0:2 * n1].rearrange("p (n c) -> p n c", c=2),
                                      vc1[:, V1_ADA + n0:V1_ADA + n1].unsqueeze(2).broadcast_to([P, n1 - n0, 2]), ALU.add))
            for l, which in norms:
                sc = l * 48 + which * 24 + 8
                v = (V2_MIX, V2_FFN)[which]
                assert n0 <= sc and sc + 8 <= n1
                st.done(dve.scalar_tensor_tensor(
                    gsc[:, l * 2 + which], mod[:, sc:sc + 8, :], 1.0,
                    vc2[:, v + l * 8:v + l * 8 + 8].unsqueeze(2).broadcast_to([P, 8, 2]), ALU.add, ALU.mult))
            st.settle()

        def ada_dve(dve, st):
            enter(dve, "ada")
            st.link(dve.memset(h2p[:], 0.0))
            for layer in range(2):
                dve.wait_ge(mlp_full, layer + 1)
                st.link(dve.tensor_scalar(farg[:], PS[layer][:HY_F, 0:TOK], fcol[:, 2 * layer:2 * layer + 1],
                                          fcol[:, 2 * layer + 1:2 * layer + 2], ALU.add, ALU.mult))
                st.link(dve.tensor_scalar(fint[:], farg[:], 1.0 / (2 * math.pi), MAGIC, ALU.mult, ALU.add))
                st.link(dve.tensor_scalar(fint[:], fint[:], -MAGIC, None, ALU.add))
                for part in (TWO_PI_A, TWO_PI_B, TWO_PI_C):
                    st.link(dve.scalar_tensor_tensor(farg[:], fint[:], -part, farg[:], ALU.mult, ALU.add))
                st.link(dve.tensor_scalar(farg[:], farg[:], PI_CLAMP, -PI_CLAMP, ALU.min, ALU.max))
                dve.sem_inc(sin_in, 1)
                dve.wait_ge(sin_out, layer + 1)
            for tt in range(NT):
                b = tt % 2
                dve.wait_ge(tap_full, tt + 1)
                dve.wait_ge(dec_there, tt + 1)
                if tt >= 2:
                    dve.wait_ge(abs_used, tt - 1)
                st.done(dve.tensor_tensor(fa[b][:], PS[b][:, 0:HW], dec[b][:, 0, :], ALU.mult))
                st.link(dve.tensor_tensor(fg[b][:], PS[b][:, HW:2 * HW], dec[b][:, 1, :], ALU.mult))
                dve.sem_inc(tap_read, 1)
                st.done(dve.tensor_tensor(Pt[:, tt, :], fa[b][:], fg[b][:], ALU.add))
                st.done(dve.tensor_tensor(Mt[:, tt, :], fg[b][:], fa[b][:], ALU.subtract))
                st.done(dve.scalar_tensor_tensor(absum[b][:], fa[b][:], -1.0, fa[b][:], ALU.mult, ALU.max))
                st.link(dve.scalar_tensor_tensor(fg[b][:], fg[b][:], -1.0, fg[b][:], ALU.mult, ALU.max))
                st.link(dve.tensor_tensor(absum[b][:], absum[b][:], fg[b][:], ALU.add))
                dve.sem_inc(abs_there, 1)
            dve.sem_inc(taps_there, 1)
            dve.wait_ge(abs_used, NT)
            for s, L in ((0, LAT), (1, CTX)):
                st.link(dve.reciprocal(invn[:, s, :], SUM_ACC[s]))
                st.link(dve.tensor_scalar(invn[:, s, :], invn[:, s, :], 1.0 / L, None, ALU.mult))
            for kk in range(NT):
                b, s = kk % 2, 0 if kk < LT else 1
                dve.wait_ge(filt_full[b], kk // 2 + 1)
                if kk >= 2:
                    dve.wait_ge(filt_stored[b], 16 * (kk // 2))
                st.done(dve.tensor_tensor(fst[b][:, 0, :], PS[b][:, 0:HW], invn[:, s, :], ALU.mult))
                st.link(dve.tensor_tensor(fst[b][:, 1, :], PS[b][:, HW:2 * HW], invn[:, s, :], ALU.mult))
                dve.sem_inc(filt_scaled[b], 1)
            for b in range(NADA):
                dve.wait_ge(aw_used[b], ADA_NOW // NADA)
            modulation(dve, st, 0, 2 * ADA_NOW, [(0, 0)])
            dve.wait_ge(csc_there, 2)
            st.link(dve.tensor_tensor(lam[:, 4:5], lam[:, 2:3], lam[:, 3:4], ALU.subtract))
            st.link(dve.tensor_scalar(lam[:, 5:6], lam[:, 4:5], LAM_INIT, -1.0, ALU.add, ALU.mult))
            st.link(dve.tensor_scalar(lam[:, 6:7], vc2[:, V2_SUB:V2_SUB + 1], 1.0 - LAM_INIT, None, ALU.mult))
            leave(dve)

        A0 = (SLABS - ADA_NOW) // 2
        A1 = A0 + SLABS // 2
        AW0 = ADA_NOW // NADA
        assert A1 == 16

        def in0_sp(sp):
            src = w_src["in0"]
            base = SLAB0["in0"] // 2
            for l, i0, i1, at in ((0, 0, A0, ADA_NOW * 256), (1, A0, A1, -A0 * 512)):
                with sp.Fori(i0, i1) as i:
                    for b in range(2):
                        sp_slab(sp, (b, base + i), src[:, :, bass.ds(i * (2 * P) + b * P, P)])
                        if b == 0:
                            enter(sp, "in0")
                        sp.wait_ge(aw_used[b], AW0 + i)
                        sp.dma_start(aw1[b][:], ada_w[l][:, :, bass.ds(i * 512 + (at + b * 256), 256)]).then_inc(aw_full[b], 16)

        def in0_pe(pe):
            enter(pe, "in0")
            base, use = SLAB0["in0"] // 2, USE0["in0"] // 2
            with pe.Fori(0, A1) as i:
                for b in range(2):
                    pe.wait_ge(w_ready[b], base + i + 1)
                    pe.wait_ge(acc_free[b], use + i)
                    full_slab(pe, b, FULL_CHUNKS).then_inc(acc_full[b], 1)
                    pe.wait_ge(apart_there, i * 2 + (b + 1))
                    for j in range(2):
                        for seg in range(2):
                            ins = pe.matmul(ALL[:, bass.ds(i * 8 + (7 * 512 + 4 * ADA_NOW + b * 4 + 2 * j + seg), 1)],
                                            apart[b][:, seg, j * P:(j + 1) * P], ones[:, 0:1], start=True, stop=True,
                                            skip_group_check=True)
                    ins.then_inc(apart_used[b], 1)
            for b in range(2):
                pe.wait_ge(acc_full[b], use + 16)
                pe.wait_ge(apart_used[b], A1)
            leave(pe)

        def in0_dve(dve, st):
            enter(dve, "in0")
            with dve.Fori(0, A1) as i:
                st.enter(i, 4 * KT)
                for b in range(2):
                    dve.wait_ge(aw_full[b], i * 16 + (AW0 + 1) * 16)
                    dve.wait_ge(apart_used[b], i)
                    for k in range(KT):
                        for seg in range(2):
                            w, c, dst = aw1[b][:, k, :], csc[:, k, seg:seg + 1], apart[b][:, seg, :]
                            if k == 0:
                                st.done(dve.tensor_scalar(dst, w, c, None, ALU.mult))
                            else:
                                st.done(dve.scalar_tensor_tensor(dst, w, c, dst, ALU.mult, ALU.add))
                        st.settle()
                    dve.sem_inc(aw_used[b], 1)
                    dve.sem_inc(apart_there, 1)
                st.leave(A1)
            for b in range(2):
                dve.wait_ge(apart_used[b], A1)
            modulation(dve, st, 2 * ADA_NOW, 4 * SLABS, [(0, 1), (1, 0), (1, 1)])
            leave(dve)

        zb = Area(AREA_B)
        zst = [zb(f"zst{b}", [P, TOK]) for b in range(2)]
        z_stored = [sem(f"z_stored{b}") for b in range(2)]
        Z0 = {"in0": 0, "in1": 16}

        def spill_act(act, name, slabs):
            enter(act, name)
            use, z0 = USE0[name] // 2, Z0[name]
            with act.Fori(0, slabs // 2) as i:
                for b in range(2):
                    act.wait_ge(acc_full[b], use + i + 1)
                    act.wait_ge(z_stored[b], 16 * (z0 + i))
                    act.activation(zst[b][:], PS[b][:, 0:TOK], ACT.Copy).then_inc(acc_free[b], 1)
                    act.wait_ge(acc_free[b], use + i + 1)
                    act.dma_start(zT[i * 2 + b], zst[b][:]).then_inc(z_stored[b], 16)
            for b in range(2):
                act.wait_ge(z_stored[b], 16 * (z0 + slabs // 2))
            leave(act)

        def in_pe(pe, name, slabs):
            enter(pe, name)
            pe_linear(pe, name, slabs, FULL_CHUNKS)
            leave(pe)

        mst = zst
        m_full = [sem(f"m_full{b}") for b in range(2)]
        m_high = [sem(f"m_high{b}") for b in range(2)]
        m_low = [sem(f"m_low{b}") for b in range(2)]

        def mix_sp(sp, l, n):
            enter(sp, f"mix{l}")
            with sp.Fori(0, KT // 2) as i:
                for b in range(2):
                    sp.wait_ge(m_low[b], l * (KT // 2) + i)
                    sp.dma_start(mst[b][:, :n], mixT[i * 2 + b][:, :n]).then_inc(m_full[b], 16)

        def mix_act(act, l, n):
            enter(act, f"mix{l}")
            with act.Fori(0, KT // 2) as i:
                for b in range(2):
                    act.wait_ge(m_full[b], 16 * (l * (KT // 2) + i + 1))
                    act.activation(AH[:, i * 2 + b, :n], mst[b][:, :n], ACT.Copy).then_inc(m_high[b], 1)
            for b in range(2):
                act.wait_ge(m_high[b], (l + 1) * (KT // 2))
            leave(act)

        def mix_dve(dve, l, n):
            enter(dve, f"mix{l}")
            with dve.Fori(0, KT // 2) as i:
                for b in range(2):
                    dve.wait_ge(m_high[b], l * (KT // 2) + i + 1)
                    dve.tensor_tensor(AL[:, i * 2 + b, :n], mst[b][:, :n], AH[:, i * 2 + b, :n].bitcast(F32),
                                      ALU.subtract).then_inc(m_low[b], 1)
            for b in range(2):
                dve.wait_ge(m_low[b], (l + 1) * (KT // 2))
            leave(dve)


        def gated_add(dve, acc, k, gate, n):
            for seg in range(2 if n == TOK else 1):
                at, w = ((0, LAT), (LAT, CTX))[seg]
                ins = dve.scalar_tensor_tensor(XT[:, k, at:at + w], acc[:, at:at + w], gate(seg), XT[:, k, at:at + w],
                                               ALU.mult, ALU.add)
            return ins

        def out_pe(pe, l):
            enter(pe, f"out{l}")
            pe_linear(pe, f"out{l}", KT, FULL_CHUNKS if l == 0 else LAT_CHUNKS)
            leave(pe)

        def out_dve(dve, l):
            enter(dve, f"out{l}")
            use = USE0[f"out{l}"] // 2
            with dve.Fori(0, KT // 2) as i:
                for b in range(2):
                    dve.wait_ge(acc_full[b], use + i + 1)
                    gated_add(dve, PS[b], i * 2 + b,
                              lambda seg: mod[:, i * 2 + (l * 48 + 16 + b), seg:seg + 1],
                              TOK if l == 0 else LAT).then_inc(acc_free[b], 1)
            for b in range(2):
                dve.wait_ge(acc_free[b], use + KT // 2)
            leave(dve)

        fb_ = Area(AREA_B)
        HH = fb_("HH", [P, 4, TOK], F32R)
        HL = fb_("HL", [P, 4, TOK], F32R)
        sg = fb_("sg", [P, TOK])
        hid = fb_("hid", [P, TOK])
        hh_there = sem("hh_there")
        hl_there = sem("hl_there")

        def ffn_n(l):
            return TOK if l == 0 else LAT

        def ffn_pe(pe, l):
            name = f"ffn{l}"
            enter(pe, name)
            chunks = FULL_CHUNKS if l == 0 else LAT_CHUNKS
            slab, use = SLAB0[name] // 2, USE0[name] // 2

            def up(s, u):
                for j in range(2):
                    for b in range(2):
                        pe.wait_ge(w_ready[b], s + j + 1)
                        pe.wait_ge(acc_free[b], u + j)
                        full_slab(pe, b, chunks).then_inc(acc_full[b], 1)

            def dn(g, par, s, u):
                pe.wait_ge(hl_there, 2 * (l * FG + g + 1))
                for q in range(2):
                    pe.wait_ge(w_ready[q], s + 1)
                    wh = WH[q][:].rearrange("p (j a) c -> p j a c", j=2)
                    wl = WL[q][:].rearrange("p (j a) c -> p j a c", j=2)
                    for a4 in range(4):
                        b = a4 % 2
                        pe.wait_ge(acc_free[b], u + 2 * q + a4 // 2)
                        products(pe, PS[b], chunks, range(2),
                                 lambda k: wh[:, k, a4, :], lambda k: wl[:, k, a4, :],
                                 lambda k, at, w: HH[:, par * 2 + k, at:at + w],
                                 lambda k, at, w: HL[:, par * 2 + k, at:at + w]).then_inc(acc_full[b], 1)

            up(slab, use)
            with pe.Fori(0, (FG - 1) // 2) as i:
                for h in range(2):
                    up(slab + 2 + 3 * h + i * 6, use + 2 + 6 * h + i * 12)
                    dn(i * 2 + h, h, slab + 4 + 3 * h + i * 6, use + 4 + 6 * h + i * 12)
            dn(FG - 1, (FG - 1) % 2, slab + 2 + 3 * (FG - 1), use + 2 + 6 * (FG - 1))
            pe.wait_ge(acc_full[1], use + 6 * FG)
            leave(pe)

        def ffn_act(act, l):
            name = f"ffn{l}"
            enter(act, name)
            use, n = USE0[name] // 2, ffn_n(l)

            def up(g, par, u):
                for j in range(2):
                    at = 2 * l * FG + g * 2 + j
                    act.wait_ge(acc_full[0], u + j + 1)
                    act.wait_ge(hl_there, at)
                    act.activation(sg[:, :n], PS[0][:, :n], ACT.Silu).then_inc(acc_free[0], 1)
                    act.wait_ge(acc_free[1], u + j + 1)
                    act.activation(HH[:, par * 2 + j, :n], hid[:, :n], ACT.Copy).then_inc(hh_there, 1)

            up(0, 0, use)
            with act.Fori(0, (FG - 1) // 2) as i:
                for h in range(2):
                    act.wait_ge(acc_full[1], use + 2 + 6 * h + i * 12)
                    up(i * 2 + h + 1, 1 - h, use + 2 + 6 * h + i * 12)
            act.wait_ge(hh_there, 2 * (l + 1) * FG)
            leave(act)

        def ffn_dve(dve, l):
            name = f"ffn{l}"
            enter(dve, name)
            use, n = USE0[name] // 2, ffn_n(l)

            def up(g, par, u):
                for j in range(2):
                    at = 2 * l * FG + g * 2 + j
                    dve.wait_ge(acc_full[1], u + j + 1)
                    dve.wait_ge(acc_free[0], u + j + 1)
                    dve.wait_ge(hl_there, at)
                    dve.tensor_tensor(hid[:, :n], sg[:, :n], PS[1][:, :n], ALU.mult).then_inc(acc_free[1], 1)
                    dve.wait_ge(hh_there, at + 1)
                    dve.tensor_tensor(HL[:, par * 2 + j, :n], hid[:, :n], HH[:, par * 2 + j, :n].bitcast(F32),
                                      ALU.subtract).then_inc(hl_there, 1)

            def dn(u):
                for k in range(KT):
                    b = k % 2
                    dve.wait_ge(acc_full[b], u + k // 2 + 1)
                    gated_add(dve, PS[b], k, lambda seg: mod[:, l * 48 + 40 + k, seg:seg + 1], n).then_inc(acc_free[b], 1)

            up(0, 0, use)
            with dve.Fori(0, (FG - 1) // 2) as i:
                for h in range(2):
                    dve.wait_ge(acc_full[1], use + 2 + 6 * h + i * 12)
                    up(i * 2 + h + 1, 1 - h, use + 2 + 6 * h + i * 12)
                    dn(use + 4 + 6 * h + i * 12)
            dn(use + 2 + 6 * (FG - 1))
            for b in range(2):
                dve.wait_ge(acc_free[b], use + 6 * FG)
            leave(dve)

        PADW = TOK + 4
        ha = Area(AREA)
        Z = ha("Z", [P, 5, PADW])
        U = ha("U", [P, 4, PADW])
        uTok = ha("uTok", [P, NT, HW])
        Y = ha("Y", [P, 2, NT, HW])
        dslab = [ha(f"dslab{b}", [P, 2, LT, P]) for b in range(2)]
        fsl = [ha(f"fsl{b}", [P, 2, HW]) for b in range(2)]
        ftmp = [ha(f"ftmp{j}", [P, HW]) for j in range(4)]

        hz_full = [sem(f"hz_full{b}") for b in range(2)]
        hz_used = sem("hz_used")
        u_there, u_turned, utok_there = sem("u_there"), sem("u_turned"), sem("utok_there")
        ds_full = [sem(f"ds_full{b}") for b in range(2)]
        spec_full = [sem(f"spec_full{b}") for b in range(2)]
        spec_read = [sem(f"spec_read{b}") for b in range(2)]
        is_used = [sem(f"is_used{b}") for b in range(2)]
        spec_there = sem("spec_there")
        y_full, y_read = sem("y_full"), sem("y_read")
        fo_there, fo_stored = sem("fo_there"), sem("fo_stored")
        SEGS = ((0, 1, LAT), (LAT, LAT + 3, CTX))
        WINDOWS = ((512, 0, 1), (512, 512, 513), (CTX, LAT, LAT + 3))
        INV = [("lat", th, kk) for th in range(2) for kk in range(LT)] + [("ctx", 0, kk) for kk in range(CT)]

        def result(n, c):
            S, w = n % 2, WINDOWS[n][0]
            return PS[S][:, c * 512:c * 512 + w] if c < 3 else PM[:, S * 512:S * 512 + w]

        def hyena_sp(sp):
            enter(sp, "hyena")
            for c in range(4):
                if c >= 2:
                    sp.wait_ge(hz_used, c - 1)
                for j, tile in ((0, 24), (1, 28)):
                    for t0, p0, w in SEGS:
                        sp.dma_start(Z[:, c % 2 * 2 + j, p0:p0 + w], zT[c + tile][:, t0:t0 + w]).then_inc(hz_full[c % 2], 16)
            with sp.Fori(0, LT // 2) as i:
                for b in range(2):
                    sp.wait_ge(spec_read[b], i)
                    sp.dma_start(dslab[b][:].rearrange("p q k c -> p q (k c)"), T["dft_lat"][i * 2 + b]).then_inc(ds_full[b], 16)
                    sp.dma_start(fsl[b][:], fspec[i * 2 + b]).then_inc(ds_full[b], 16)
                sp.wait_ge(hz_used, i + 4)
                for t0, p0, w in SEGS:
                    sp.dma_start(Z[:, 0, p0:p0 + w], zT[i + 20][:, t0:t0 + w]).then_inc(hz_full[0], 16)
            for b in range(CT):
                sp.wait_ge(spec_read[b], LT // 2)
                sp.dma_start(dslab[b][:, :, 0:CT, :].rearrange("p q k c -> p q (k c)"), T["dft_ctx"][b]).then_inc(ds_full[b], 16)
                sp.dma_start(fsl[b][:], fspec[LT + b]).then_inc(ds_full[b], 16)
            for n, (seg, th, kk) in enumerate(INV):
                b, use = n % 2, n // 2
                sp.wait_ge(spec_full[b], LT // 2 + 1) if use == 0 else sp.wait_ge(is_used[b], use)
                w = min(512, LAT if seg == "lat" else CTX)
                flat = dslab[b][:].rearrange("p q k c -> p (q k c)")[:, 0:2 * w].rearrange("p (q w) -> p q w", q=2)
                sp.dma_start(flat, T["inv_" + seg][th, kk]).then_inc(ds_full[b], 16)

        def zero_pads(dve, st):
            for c0, c1 in ((0, 1), (LAT + 1, LAT + 3), (PADW - 1, PADW)):
                st.done(dve.memset(Z[:, 0:4, c0:c1], 0.0))
            st.settle()

        def short_conv(dve, st, dst, src, tile):
            inner = slice(1, PADW - 1)

            def col(tap):
                return vc2[:, bass.ds(tile + (V2_SW + tap * 12), 1)]

            bias = vc2[:, bass.ds(tile + V2_SB, 1)]
            st.link(dve.tensor_scalar(dst[:, inner], src[:, inner], col(1), bias, ALU.mult, ALU.add))
            st.link(dve.scalar_tensor_tensor(dst[:, inner], src[:, 0:PADW - 2], col(0), dst[:, inner], ALU.mult, ALU.add))
            st.link(dve.scalar_tensor_tensor(dst[:, inner], src[:, 2:PADW], col(2), dst[:, inner], ALU.mult, ALU.add))

        def hyena_dve(dve, st):
            enter(dve, "hyena")
            zero_pads(dve, st)
            with dve.Fori(0, 2) as i:
                st.enter(i, 2 * 7)
                for b in range(2):
                    c = i * 2 + b
                    dve.wait_ge(hz_full[b], i * 64 + 64)
                    short_conv(dve, st, U[:, c, :], Z[:, b * 2, :], c + 4)
                    short_conv(dve, st, Z[:, 4, :], Z[:, b * 2 + 1, :], c + 8)
                    dve.sem_inc(hz_used, 1)
                    st.link(dve.tensor_tensor(U[:, c, 1:PADW - 1], U[:, c, 1:PADW - 1], Z[:, 4, 1:PADW - 1], ALU.mult))
                    dve.sem_inc(u_there, 1)
                st.leave(2)

            def spectrum(b, use, kk):
                ur, ui = PS[b][:, 0:512], PS[b][:, 512:1024]
                fr, fi = fsl[b][:, 0, :], fsl[b][:, 1, :]
                dve.wait_ge(spec_full[b], use + 1)
                st.done(dve.tensor_tensor(ftmp[0][:], ur, fr, ALU.mult))
                st.done(dve.tensor_tensor(ftmp[1][:], ui, fi, ALU.mult))
                st.done(dve.tensor_tensor(ftmp[2][:], ur, fi, ALU.mult))
                st.link(dve.tensor_tensor(ftmp[3][:], ui, fr, ALU.mult))
                dve.sem_inc(spec_read[b], 1)
                st.done(dve.tensor_tensor(Y[:, 0, kk, :], ftmp[0][:], ftmp[1][:], ALU.add))
                st.link(dve.tensor_tensor(Y[:, 1, kk, :], ftmp[2][:], ftmp[3][:], ALU.subtract))

            with dve.Fori(0, LT // 2) as i:
                st.enter(i, 12 + 3)
                for b in range(2):
                    spectrum(b, i, i * 2 + b)
                dve.wait_ge(hz_full[0], i * 32 + (128 + 32))
                short_conv(dve, st, Z[:, i + 1, :], Z[:, 0, :], i)
                dve.sem_inc(hz_used, 1)
                st.leave(LT // 2)
            for b in range(CT):
                spectrum(b, LT // 2, LT + b)
            dve.sem_inc(spec_there, 1)
            for n, (w, t0, p0) in enumerate(WINDOWS):
                dve.wait_ge(y_full, n + 1)
                for c in range(4):
                    st.done(dve.scalar_tensor_tensor(U[:, c, p0:p0 + w], U[:, c, p0:p0 + w],
                                                     vc2[:, V2_SKIP + c:V2_SKIP + c + 1], result(n, c), ALU.mult, ALU.add))
                st.settle()
                dve.sem_inc(y_read, 1)
                st.link(dve.tensor_tensor(U[:, :, p0:p0 + w], U[:, :, p0:p0 + w], Z[:, 1:5, p0:p0 + w], ALU.mult))
                dve.sem_inc(fo_there, 1)
            leave(dve)

        def hyena_act(act, st):
            enter(act, "hyena")
            with act.Fori(0, 4) as c:
                act.wait_ge(u_turned, c + 1)
                act.activation(uTok[:, :, bass.ds(c * P, P)], PS[0][:, 0:TOK].rearrange("p (t c) -> p t c", c=P),
                               ACT.Copy).then_inc(utok_there, 1)
            for n, (w, t0, p0) in enumerate(WINDOWS):
                act.wait_ge(fo_there, n + 1)
                act.dma_start(mixT[4:8].rearrange("k p t -> p k t")[:, :, t0:t0 + w], U[:, :, p0:p0 + w]).then_inc(fo_stored, 16)
            act.wait_ge(fo_stored, 16 * len(WINDOWS))
            leave(act)

        def hyena_pe(pe, st):
            enter(pe, "hyena")
            for c in range(4):
                pe.wait_ge(u_there, c + 1)
                pe.wait_ge(utok_there, c)
                for tt in range(NT):
                    at = tt * P + (1 if tt < LT else 3)
                    ins = pe.transpose(PS[0][:, tt * P:(tt + 1) * P], U[:, c, at:at + P], ident[:])
                ins.then_inc(u_turned, 1)
            pe.wait_ge(utok_there, 4)

            def forward(b, use, tts):
                pe.wait_ge(ds_full[b], use * 32 + 32)
                pe.wait_ge(spec_read[b], use)
                n = len(tts)
                for q in range(2):
                    for m, tt in enumerate(tts):
                        ins = pe.matmul(PS[b][:, q * 512:(q + 1) * 512], dslab[b][:, q, m, :], uTok[:, tt, :],
                                        start=(m == 0), stop=(m == n - 1), skip_group_check=True)
                ins.then_inc(spec_full[b], 1)

            with pe.Fori(0, LT // 2) as i:
                for b in range(2):
                    forward(b, i, range(LT))
            for b in range(CT):
                forward(b, LT // 2, range(LT, NT))
            pe.wait_ge(spec_there, 1)
            for n, (seg, th, kk) in enumerate(INV):
                b, use = n % 2, n // 2
                window = th if seg == "lat" else 2
                w = min(512, LAT if seg == "lat" else CTX)
                count = LT if seg == "lat" else CT
                if seg == "ctx" and kk == 0:
                    pe.wait_ge(y_read, 1)
                pe.wait_ge(ds_full[b], 32 * (LT // 2 + 1) + 16 * (use + 1))
                flat = dslab[b][:].rearrange("p q k c -> p (q k c)")
                for c in range(4):
                    acc = result(window, c)
                    for q in range(2):
                        ins = pe.matmul(acc, Y[:, q, kk + (0 if seg == "lat" else LT), c * P:(c + 1) * P],
                                        flat[:, q * w:(q + 1) * w], start=(kk == 0 and q == 0),
                                        stop=(kk == count - 1 and q == 1), skip_group_check=True)
                st.link(ins) if kk == count - 1 else ins.then_inc(is_used[b], 1)
                if kk == count - 1:
                    pe.sem_inc(y_full, 1)
                    pe.sem_inc(is_used[b], 1)
            leave(pe)

        ga = Area(AREA)
        gq, gv, gg = ga("gq", [P, TOK]), ga("gv", [P, TOK]), ga("gg", [P, TOK])
        gz = ga("gz", [P, 2, TOK])
        glog = ga("glog", [P, 2, TOK])
        gcum = ga("gcum", [P, 2, TOK])
        gk = ga("gk", [P, 2, TOK])
        garg = [ga(f"garg{b}", [P, 2, TOK]) for b in range(2)]
        gqe = [ga(f"gqe{b}", [P, TOK]) for b in range(2)]
        gke = [ga(f"gke{b}", [P, TOK]) for b in range(2)]
        attn = ga("attn", [P, TOK])
        gtmp = ga("gtmp", [P, TOK])
        groot = ga("groot", [P, TOK])
        vTok = ga("vTok", [P, NT, P])
        keepm = ga("keepm", [P, TOK])
        state = ga("state", [P, 2, NT, P])
        UPD = 3
        kdTok = [ga(f"kdTok{b}", [P, UPD, P]) for b in range(2)]
        lmask = ga("lmask", [P, LEVELS + 1, P])
        gdec = ga("gdec", [P, 2, NT])
        NS = LEVELS + 1
        ORDER = [list(range(LT, NT)) + list(range(LT)), list(range(NT - 1, LT - 1, -1)) + list(range(LT - 1, -1, -1))]
        GROUPS = [(d, list(zip(ORDER[d], ORDER[d][1:]))[g * UPD:(g + 1) * UPD])
                  for g in range((NT - 1) // UPD) for d in range(2)]
        NG = len(GROUPS)
        assert (NT - 1) % UPD == 0 and NG <= NS - 2
        KD_ACC, UPD_ACC = ALL[:, 6 * 512:6 * 512 + UPD * P], ALL[:, 7 * 512:7 * 512 + UPD * P]

        gh_full = sem("gh_full")
        gq_full, gv_full, gg_full, gq_used = sem("gq_full"), sem("gv_full"), sem("gg_full"), sem("gq_used")
        v_turned, v_tok = sem("v_turned"), sem("v_tok")
        softp, log_there, k_there, cum_there = sem("softp"), sem("log_there"), sem("k_there"), sem("cum_there")
        arg_there, fac_there, qk_there = sem("arg_there"), sem("fac_there"), sem("qk_there")
        step_full, step_read = sem("step_full"), sem("step_read")
        qdec_there, kdec_there, kd_there = sem("qdec_there"), sem("kdec_there"), sem("kd_there")
        kd_turned, kd_tok = sem("kd_turned"), sem("kd_tok")
        upd_full, upd_read, state_there, o_full = sem("upd_full"), sem("upd_read"), sem("state_there"), sem("o_full")
        osq_there, oss_full, oroot = sem("osq_there"), sem("oss_full"), sem("oroot")
        gate_there, mo_there, mo_stored = sem("gate_there"), sem("mo_there"), sem("mo_stored")

        def halves(ap, l):
            return ap.rearrange("p (n a h) -> p n a h", a=2, h=1 << l)

        HEADS = 4

        def of(h, per, c):
            return h[0] * per + (h[1] * per + c)

        def heads_in_turn(eng, st, body, seam, steps):
            with eng.Fori(0, HEADS - 1) as i:
                if st:
                    st.enter(i, steps)
                body((i, 0))
                seam((i, 0), (i, 1))
                if st:
                    st.leave(HEADS - 1)
            body((0, HEADS - 1))

        def hgrn_sp(sp):
            enter(sp, "hgrn")
            sp.dma_start(lmask[:], T["levelmask"]).then_inc(gh_full, 16)

            def load(dst, h, tile, full):
                sp.dma_start(dst, zT[of(h, 1, tile)]).then_inc(full, 16)

            load(gz[:, 0, :], (0, 0), 4, gh_full)
            load(gz[:, 1, :], (0, 0), 8, gh_full)
            load(gq[:], (0, 0), 0, gq_full)
            load(gv[:], (0, 0), 12, gv_full)
            load(gg[:], (0, 0), 16, gg_full)
            with sp.Fori(0, HEADS - 1) as i:
                h = (i, 1)
                sp.wait_ge(k_there, i + 1)
                load(gz[:, 0, :], h, 4, gh_full)
                load(gz[:, 1, :], h, 8, gh_full)
                sp.wait_ge(v_turned, i + 1)
                load(gv[:], h, 12, gv_full)
                sp.wait_ge(gq_used, i + 1)
                load(gq[:], h, 0, gq_full)
                sp.wait_ge(mo_there, i + 1)
                load(gg[:], h, 16, gg_full)
                sp.dma_start(mixT[i], gtmp[:]).then_inc(mo_stored, 16)
            sp.wait_ge(mo_there, HEADS)
            sp.dma_start(mixT[HEADS - 1], gtmp[:]).then_inc(mo_stored, 16)

        def hgrn_act(act, st):
            enter(act, "hgrn")

            def turned(h, g):
                act.wait_ge(kd_turned, of(h, NG, g + 1))
                if g >= 2:
                    act.wait_ge(upd_full, of(h, NG, g - 1))
                act.activation(kdTok[g % 2][:].rearrange("p n c -> p (n c)"), KD_ACC, ACT.Copy).then_inc(kd_tok, 1)

            def start(h):
                act.wait_ge(gh_full, of(h, 32, 48))
                if h[1]:
                    act.wait_ge(gq_used, of(h, 1, 0))
                st.link(act.activation(gk[:], gz[:], ACT.Abs))
                st.link(act.activation(gk[:], gk[:], ACT.Exp, scale=-1.0))
                act.activation(gk[:], gk[:], ACT.Ln, bias=1.0).then_inc(softp, 1)
                act.wait_ge(log_there, of(h, 1, 1))
                act.activation(gk[:], gz[:], ACT.Exp, scale=-1.0).then_inc(k_there, 1)
                act.wait_ge(cum_there, of(h, 1, 1))
                st.done(act.activation(gdec[:, 0, :], gcum[:, 0, P - 1::P], ACT.Exp))
                st.done(act.activation(gdec[:, 1, :], gcum[:, 1, 0::P], ACT.Exp))
                st.settle()

            def body(h):
                for s in range(1, NS):
                    act.wait_ge(arg_there, of(h, NS, s if s == 1 else s + 1))
                    act.activation(garg[s % 2][:], garg[s % 2][:], ACT.Exp).then_inc(fac_there, 1)
                    if s == 1:
                        act.wait_ge(arg_there, of(h, NS, 2))
                        act.activation(glog[:], glog[:], ACT.Exp).then_inc(kdec_there, 1)
                        act.wait_ge(v_turned, of(h, 1, 1))
                        act.activation(vTok[:].rearrange("p n c -> p (n c)"), PS[1][:, 0:TOK], ACT.Copy).then_inc(v_tok, 1)
                    if s >= 3:
                        turned(h, s - 3)
                act.wait_ge(qk_there, of(h, NS, NS - 1))
                act.activation(garg[0][:], gcum[:], ACT.Exp).then_inc(qdec_there, 1)
                for g in range(NS - 3, NG):
                    turned(h, g)
                act.wait_ge(gg_full, of(h, 16, 16))
                act.activation(gg[:], gg[:], ACT.Silu).then_inc(gate_there, 1)

            def end(h):
                act.wait_ge(o_full, of(h, 1, 1))
                st.done(act.activation(gqe[0][:], PS[0][:, 0:TOK], ACT.Square))
                st.done(act.activation(gtmp[:], PS[0][:, 0:TOK], ACT.Copy))
                st.settle()
                act.sem_inc(osq_there, 1)
                act.wait_ge(oss_full, of(h, 1, 1))
                st.link(act.activation(groot[:], PS[1][:, 0:TOK], ACT.Ln, bias=eps_col[:, 0:1], scale=1.0 / P))
                act.activation(groot[:], groot[:], ACT.Exp, scale=-0.5).then_inc(oroot, 1)

            def seam(h, following):
                start(following)
                end(h)

            start((0, 0))
            heads_in_turn(act, st, body, seam, 7)
            end((0, HEADS - 1))
            act.wait_ge(mo_stored, 16 * HEADS)
            leave(act)

        def hgrn_pool(pool):
            enter(pool, "hgrn")
            PER = 4 * LEVELS + 2

            def args(h, s):
                l = s - 1
                shape = [P, TOK >> (l + 1), 1 << l]
                cf, cb = halves(gcum[:, 0, :], l), halves(gcum[:, 1, :], l)
                rf = cf[:, :, 0, (1 << l) - 1:].broadcast_to(shape)
                rb = cb[:, :, 1, 0:1].broadcast_to(shape)
                eq, ek = halves(garg[s % 2][:, 0, :], l), halves(garg[s % 2][:, 1, :], l)
                if s == 2:
                    pool.wait_ge(o_full, h)
                if s >= 3:
                    pool.wait_ge(qk_there, h * NS + (s - 1))
                pool.tensor_tensor(eq[:, :, 1, :], cf[:, :, 1, :], rf, ALU.subtract).then_inc(pool_step, 1)
                pool.tensor_tensor(eq[:, :, 0, :], cb[:, :, 0, :], rb, ALU.subtract).then_inc(pool_step, 1)
                pool.tensor_tensor(ek[:, :, 0, :], rf, cf[:, :, 0, :], ALU.subtract).then_inc(pool_step, 1)
                pool.tensor_tensor(ek[:, :, 1, :], rb, cb[:, :, 1, :], ALU.subtract).then_inc(pool_step, 1)
                pool.wait_ge(pool_step, h * PER + (1 + 4 * s + (2 if s > 1 else 0)))
                pool.sem_inc(arg_there, 1)

            with pool.Fori(0, HEADS) as h:
                pool.wait_ge(cum_there, h + 1)
                args(h, 1)
                c4 = gcum[:].rearrange("p d (n c) -> p d n c", c=P)
                g4 = glog[:].rearrange("p d (n c) -> p d n c", c=P)
                pool.tensor_tensor(g4[:, 0], c4[:, 0, :, P - 1:].broadcast_to([P, NT, P]), c4[:, 0],
                                   ALU.subtract).then_inc(pool_step, 1)
                pool.tensor_tensor(g4[:, 1], c4[:, 1, :, 0:1].broadcast_to([P, NT, P]), c4[:, 1],
                                   ALU.subtract).then_inc(pool_step, 1)
                pool.wait_ge(pool_step, h * PER + 7)
                pool.sem_inc(arg_there, 1)
                for s in range(2, NS):
                    args(h, s)
            leave(pool)

        def hgrn_dve(dve, st):
            enter(dve, "hgrn")
            st.link(dve.memset(keepm[:], 1.0))
            st.done(dve.memset(keepm[:, 0::P], 0.0))
            for d in range(2):
                st.done(dve.memset(state[:, d, ORDER[d][0], :], 0.0))
            st.settle()

            def start(h):
                dve.wait_ge(softp, of(h, 1, 1))
                st.done(dve.scalar_tensor_tensor(glog[:], gz[:], 0.0, gk[:], ALU.min, ALU.subtract))
                st.link(dve.scalar_tensor_tensor(gz[:], gz[:], 0.0, gk[:], ALU.max, ALU.add))
                dve.sem_inc(log_there, 1)
                st.done(dve.tensor_tensor_scan(gcum[:, 0, :], keepm[:], glog[:, 0, :], 0.0, ALU.mult, ALU.add))
                st.link(dve.tensor_tensor_scan(gcum[:, 1, ::-1], keepm[:], glog[:, 1, ::-1], 0.0, ALU.mult, ALU.add))
                dve.sem_inc(cum_there, 1)
                dve.wait_ge(k_there, of(h, 1, 1))
                st.link(dve.tensor_tensor(gke[0][:], gk[:, 0, :], gk[:, 1, :], ALU.add))
                dve.sem_inc(qk_there, 1)

            def factors(h, s):
                l = s - 1
                dve.wait_ge(fac_there, of(h, LEVELS, s))
                if s >= 2:
                    dve.wait_ge(step_full, of(h, NS, s - 1))
                ek = halves(garg[s % 2][:, 1, :], l)
                ke = halves(gke[s % 2][:], l)
                st.done(dve.tensor_tensor(gqe[s % 2][:], gq[:], garg[s % 2][:, 0, :], ALU.mult))
                for d in range(2):
                    st.done(dve.tensor_tensor(ke[:, :, d, :], halves(gk[:, d, :], l)[:, :, d, :], ek[:, :, d, :], ALU.mult))
                st.settle()
                dve.sem_inc(qk_there, 1)

            def collect(h, s):
                mask = lmask[:, s, :].unsqueeze(1).broadcast_to([P, NT, P])
                dst = attn if s == 0 else gtmp
                dve.wait_ge(step_full, of(h, NS, s + 1))
                if s == 1:
                    dve.wait_ge(mo_stored, of(h, 16, 0))
                st.link(dve.tensor_tensor(dst[:].rearrange("p (n c) -> p n c", c=P),
                                          PS[s % 2][:, 0:TOK].rearrange("p (n c) -> p n c", c=P), mask, ALU.mult))
                dve.sem_inc(step_read, 1)
                if s:
                    st.link(dve.tensor_tensor(attn[:], attn[:], gtmp[:], ALU.add))

            def states(h, g):
                d, pairs = GROUPS[g]
                dve.wait_ge(upd_full, of(h, NG, g + 1))
                for j, (n, m) in enumerate(pairs):
                    st.link(dve.scalar_tensor_tensor(state[:, d, m, :], state[:, d, n, :], gdec[:, d, n:n + 1],
                                                     UPD_ACC[:, j * P:(j + 1) * P], ALU.mult, ALU.add))
                dve.sem_inc(upd_read, 1)

            def body(h):
                dve.wait_ge(gq_full, of(h, 16, 16))
                for s in range(1, NS):
                    factors(h, s)
                    if s == 1:
                        dve.wait_ge(kdec_there, of(h, 1, 1))
                        st.link(dve.tensor_tensor(glog[:], glog[:], gk[:], ALU.mult))
                        dve.sem_inc(kd_there, 1)
                    collect(h, s - 1)
                    if s >= 4:
                        states(h, s - 4)
                dve.wait_ge(qdec_there, of(h, 1, 1))
                for d in range(2):
                    st.done(dve.tensor_tensor(garg[0][:, d, :], garg[0][:, d, :], gq[:], ALU.mult))
                st.settle()
                dve.sem_inc(gq_used, 1)
                collect(h, NS - 1)
                for g in range(NS - 4, NG):
                    states(h, g)
                dve.sem_inc(state_there, 1)

            def end(h):
                dve.wait_ge(oroot, of(h, 1, 1))
                st.link(dve.tensor_tensor(gtmp[:], gtmp[:], groot[:], ALU.mult))
                dve.wait_ge(gate_there, of(h, 1, 1))
                st.link(dve.scalar_tensor_tensor(gtmp[:], gtmp[:], vc2[:, V2_HG:V2_HG + 1], gg[:], ALU.mult, ALU.mult))
                dve.sem_inc(mo_there, 1)

            def seam(h, following):
                start(following)
                end(h)

            start((0, 0))
            heads_in_turn(dve, st, body, seam, 5 + 3 * LEVELS + 1 + 1 + 2 * LEVELS + 2 + NG * UPD + 2)
            end((0, HEADS - 1))
            leave(dve)

        def hgrn_pe(pe, st):
            enter(pe, "hgrn")

            def step(h, s):
                pe.wait_ge(qk_there, of(h, NS, s + 1))
                if s == 1:
                    pe.wait_ge(v_tok, of(h, 1, 1))
                if s >= 2:
                    pe.wait_ge(step_read, of(h, NS, s - 1))
                q = gq if s == 0 else gqe[s % 2]
                for n in range(NT):
                    c = slice(n * P, (n + 1) * P)
                    ins = pe.matmul(PS[s % 2][:, c], gke[s % 2][:, c], q[:, c], start=True, stop=True)
                ins.then_inc(step_full, 1)

            def turn(h, g):
                d, pairs = GROUPS[g]
                pe.wait_ge(kd_there, of(h, 1, 1))
                pe.wait_ge(kd_tok, of(h, NG, g))
                for j, (n, _) in enumerate(pairs):
                    ins = pe.transpose(KD_ACC[:, j * P:(j + 1) * P], glog[:, d, n * P:(n + 1) * P], ident[:])
                ins.then_inc(kd_turned, 1)

            def update(h, g):
                pe.wait_ge(kd_tok, of(h, NG, g + 1))
                pe.wait_ge(upd_read, of(h, NG, g))
                for j, (n, _) in enumerate(GROUPS[g][1]):
                    ins = pe.matmul(UPD_ACC[:, j * P:(j + 1) * P], kdTok[g % 2][:, j, :], vTok[:, n, :], start=True, stop=True)
                ins.then_inc(upd_full, 1)

            with pe.Fori(0, HEADS) as i:
                h = (i, 0)
                pe.wait_ge(gq_full, i * 16 + 16)
                pe.wait_ge(osq_there, i)
                step(h, 0)
                pe.wait_ge(oroot, i)
                pe.wait_ge(gv_full, i * 16 + 16)
                for n in range(NT):
                    ins = pe.transpose(PS[1][:, n * P:(n + 1) * P], gv[:, n * P:(n + 1) * P], ident[:])
                ins.then_inc(v_turned, 1)
                for s in range(1, NS):
                    step(h, s)
                    if s >= 3:
                        update(h, s - 3)
                    if s >= 2:
                        turn(h, s - 2)
                for g in range(NS - 3, NG):
                    update(h, g)
                pe.wait_ge(state_there, i + 1)
                for n in range(NT):
                    c = slice(n * P, (n + 1) * P)
                    pe.matmul(PS[0][:, c], vTok[:, n, :], attn[:, c], start=True, stop=False)
                    pe.matmul(PS[0][:, c], state[:, 0, n, :], garg[0][:, 0, c], start=False, stop=False)
                    ins = pe.matmul(PS[0][:, c], state[:, 1, n, :], garg[0][:, 1, c], start=False, stop=True)
                ins.then_inc(o_full, 1)
                pe.wait_ge(osq_there, i + 1)
                for at, w in FULL_CHUNKS:
                    ins = pe.matmul(PS[1][:, at:at + w], ones[:], gqe[0][:, at:at + w], start=True, stop=True)
                ins.then_inc(oss_full, 1)
            pe.wait_ge(oss_full, HEADS)
            leave(pe)

        ta = Area(AREA)
        aq, ak, av = ta("aq", [P, TOK]), ta("ak", [P, TOK]), ta("av", [P, TOK])
        qr, kr = ta("qr", [P, LAT]), ta("kr", [P, TOK])
        arot = ta("arot", [P, TOK])
        prob = [ta(f"prob{b}", [P, TOK]) for b in range(2)]
        pd = [ta(f"pd{b}", [P, TOK]) for b in range(2)]
        probT = [ta(f"probT{b}", [P, TOK]) for b in range(2)]
        vtk = ta("vtk", [P, NT, P])
        od = ta("od", [P, LT, P])
        amo = ta("amo", [P, LAT])
        rope_da, rope_mla = ta("rope_da", [P, 2, LAT]), ta("rope_mla", [96, 2, LAT])
        rot_da, rot_mla = ta("rot_da", [P, P]), ta("rot_mla", [96, 96])
        cqn, ckvn, krr = ta("cqn", [P, 2, TOK]), ta("ckvn", [P, TOK]), ta("krr", [96, TOK])
        wuq, wukv = ta("wuq", [P, 2, 96]), ta("wukv", [P, 192])
        rsum, rinv, amax, ass = ta("rsum", [P, 16]), ta("rinv", [P, 16]), ta("amax", [P, 4]), ta("ass", [P, 8])

        at_full, ah_full, ah_used = sem("at_full"), sem("ah_full"), sem("ah_used")
        rot_full, qk_rot, kctx_there = sem("rot_full"), sem("qk_rot"), sem("kctx_there")
        vt_full, vt_there = sem("vt_full"), sem("vt_there")
        s_full, s_max, p_done, pd_there, t_full, pt_ready, pv_full, o_read = (
            sem("s_full"), sem("s_max"), sem("p_done"), sem("pd_there"), sem("t_full"), sem("pt_ready"), sem("pv_full"), sem("o_read"))
        od_sq, od_root, od_there, od_turned, amo_stored = (
            sem("od_sq"), sem("od_root"), sem("od_there"), sem("od_turned"), sem("amo_stored"))
        lat_in, lat_sq, lat_ss, lat_root, kr_zero, kr_rot = (
            sem("lat_in"), sem("lat_sq"), sem("lat_ss"), sem("lat_root"), sem("kr_zero"), sem("kr_rot"))
        mq_full, mq_copied = sem("mq_full"), sem("mq_copied")
        N_TAB = 4
        DU, MU = 2 * LT, LT

        def attn_sp(sp):
            enter(sp, "attn")
            for k in range(2):
                sp.dma_start(cqn[:, k, :], zT[12 + k]).then_inc(lat_in, 16)
            sp.dma_start(ckvn[:], zT[14]).then_inc(lat_in, 16)
            for dst, name in ((rope_da, "rope_da"), (rope_mla, "rope_mla"), (rot_da, "rot_da"), (rot_mla, "rot_mla")):
                sp.dma_start(dst[:], T[name]).then_inc(at_full, 16)
            sp.wait_ge(kr_zero, 1)
            sp.dma_start(krr[64:96, :], zT[15][64:96, :]).then_inc(lat_in, 16)
            with sp.Fori(0, 4) as h:
                sp.wait_ge(qk_rot, h * 2)
                sp.wait_ge(kctx_there, h)
                sp.wait_ge(vt_full, h)
                sp.dma_start(aq[:], zT[h]).then_inc(ah_full, 16)
                sp.dma_start(ak[:], zT[h + 4]).then_inc(ah_full, 16)
                sp.dma_start(av[:], zT[h + 8]).then_inc(ah_full, 16)
            uq = T["mla_w_uq"][0].rearrange("(k p) n -> p k n", p=P)
            with sp.Fori(0, 4) as h:
                sp.wait_ge(vt_full, h + 4)
                sp.dma_start(wuq[:], uq[:, :, bass.ds(h * 96, 96)]).then_inc(ah_full, 16)
                sp.dma_start(wukv[:], T["mla_w_ukv"][0][:, bass.ds(h * 192, 192)]).then_inc(ah_full, 16)

        TURN = [(0, 4, 5 * 512), (4, 4, 6 * 512), (8, 2, 7 * 512 + P)]
        OUT = slice(7 * 512, 7 * 512 + P)

        def tiles_pe(pe, sb, tb, J, parts):
            for i in range(LT + 2):
                if i < LT:
                    pe.wait_ge(p_done, sb + i * J)
                    for j in range(J):
                        lo, hi = parts[j]
                        chunks = FULL_CHUNKS if j == 0 else [(256, 512), (768, 512), (0, 256)]
                        for at, w in chunks:
                            if j and at == 0:
                                pe.wait_ge(s_max, sb + i * J + 1)
                            ins = pe.matmul(ALL[:, j * TOK + at:j * TOK + at + w], qr[lo:hi, i * P:(i + 1) * P],
                                            kr[lo:hi, at:at + w], start=True, stop=True, skip_group_check=True)
                        ins.then_inc(s_full, 1)
                if i >= 2:
                    t = i - 2
                    pe.wait_ge(pt_ready, tb * 3 + (t * 3 + 3))
                    pe.wait_ge(o_read, tb + t)
                    for s in range(NT):
                        ins = pe.matmul(ALL[:, OUT], probT[t % 2][:, s * P:(s + 1) * P], vtk[:, s, :],
                                        start=(s == 0), stop=(s == NT - 1))
                    ins.then_inc(pv_full, 1)
                if 1 <= i <= LT:
                    t = i - 1
                    pe.wait_ge(pd_there, tb + t + 1)
                    pe.wait_ge(pt_ready, (tb + t) * 3)
                    for m, (s0, n, col) in enumerate(TURN):
                        if m == 2 and i >= 2:
                            pe.wait_ge(o_read, tb + i - 1)
                        for s in range(s0, s0 + n):
                            ins = pe.transpose(ALL[:, col + (s - s0) * P:col + (s - s0 + 1) * P],
                                               pd[t % 2][:, s * P:(s + 1) * P], ident[:])
                        ins.then_inc(t_full, 1)

        def tiles_act(act, sb, tb, J, scale):
            for i in range(LT + 1):
                for j in range(J):
                    if i < LT:
                        act.wait_ge(s_full, sb + (i + 1) * J)
                        act.wait_ge(s_max, sb + (i * J + j + 1))
                        act.wait_ge(pd_there, tb + i)
                        act.activation(prob[j][:], ALL[:, j * TOK:(j + 1) * TOK], ACT.Exp, bias=amax[:, 2 + j:3 + j],
                                       scale=scale, accum_out=rsum[:, i * J + j:i * J + j + 1]).then_inc(p_done, 1)
                if i >= 1:
                    t = i - 1
                    for m, (s0, n, col) in enumerate(TURN):
                        act.wait_ge(t_full, tb * 3 + (t * 3 + m + 1))
                        if t >= 2:
                            act.wait_ge(pv_full, tb + t - 1)
                        act.activation(probT[t % 2][:, s0 * P:(s0 + n) * P], ALL[:, col:col + n * P],
                                       ACT.Copy).then_inc(pt_ready, 1)

        def tiles_dve(dve, st, sb, tb, J, scale):
            for i in range(LT + 2):
                if 1 <= i <= LT:
                    t = i - 1
                    dve.wait_ge(p_done, sb + (t + 1) * J)
                    if t >= 2:
                        dve.wait_ge(t_full, tb * 3 + (t - 1) * 3)
                    c = slice(t * J, (t + 1) * J)
                    st.link(dve.reciprocal(rinv[:, c], rsum[:, c]))
                    ins = dve.tensor_scalar(pd[t % 2][:], prob[0][:], rinv[:, t * J:t * J + 1], None, ALU.mult)
                    if J == 2:
                        st.done(ins)
                        c1 = slice(t * J + 1, t * J + 2)
                        st.link(dve.tensor_tensor(rinv[:, c1], rinv[:, c1], lam[:, 5:6], ALU.mult))
                        ins = dve.scalar_tensor_tensor(pd[t % 2][:], prob[1][:], rinv[:, c1], pd[t % 2][:], ALU.mult, ALU.add)
                    ins.then_inc(pd_there, 1)
                if i < LT:
                    for j in range(J):
                        dve.wait_ge(s_full, sb + (i * J + j + 1))
                        dve.wait_ge(p_done, sb + (i * J + j))
                        st.link(dve.tensor_reduce(amax[:, j:j + 1], ALL[:, j * TOK:(j + 1) * TOK], AX.X, ALU.max))
                        dve.tensor_scalar(amax[:, 2 + j:3 + j], amax[:, j:j + 1], -scale, None, ALU.mult).then_inc(s_max, 1)
                if i >= 2:
                    t = i - 2
                    dve.wait_ge(pv_full, tb + t + 1)
                    dve.tensor_copy(od[:, t, :], ALL[:, OUT]).then_inc(o_read, 1)
            dve.wait_ge(o_read, tb + LT)

        def tile_steps(J):
            return LT * (1 + J) + (2 * LT if J == 2 else 0)

        def attn_pe(pe, st):
            enter(pe, "attn")
            pe.wait_ge(at_full, 16 * N_TAB)
            for j, k in ((0, 0), (0, 1), (1, 2)):
                pe.wait_ge(lat_sq, k + 1)
                for at, w in FULL_CHUNKS:
                    ins = pe.matmul(PS[j][:, at:at + w], ones[:], (pd[0], pd[1], probT[0])[k][:, at:at + w], start=(k != 1),
                                    stop=(k >= 1), skip_group_check=True)
            ins.then_inc(lat_ss, 1)
            for at, w in LAT_CHUNKS:
                ins = pe.matmul(PM[:96, at:at + w], rot_mla[:], krr[:, at:at + w], start=True, stop=True)
            ins.then_inc(kr_rot, 1)
            pe.wait_ge(lat_root, 1)

            def rotation(h):
                pe.wait_ge(ah_full, of(h, 48, 48))
                for j, src in ((0, aq), (1, ak)):
                    for at, w in LAT_CHUNKS:
                        ins = pe.matmul(PS[j][:, at:at + w], rot_da[:], src[:, at:at + w], start=True, stop=True)
                    ins.then_inc(rot_full, 1)

            def values(h):
                pe.wait_ge(qk_rot, of(h, 2, 2))
                for s in range(NT):
                    ins = pe.transpose(PS[1][:, s * P:(s + 1) * P], av[:, s * P:(s + 1) * P], ident[:])
                ins.then_inc(vt_full, 1)

            def turn_result(h):
                pe.wait_ge(od_there, of(h, 1, 1))
                for tt in range(LT):
                    ins = pe.transpose(PM[:, tt * P:(tt + 1) * P], od[:, tt, :], ident[:])
                ins.then_inc(od_turned, 1)

            def body(h):
                pe.wait_ge(vt_there, of(h, 1, 1))
                pe.wait_ge(ah_used, of(h, 1, 0))
                tiles_pe(pe, of(h, DU, 0), of(h, LT, 0), 2, ((0, 64), (64, P)))

            def seam(h, following):
                rotation(following)
                turn_result(h)
                values(following)

            rotation((0, 0))
            values((0, 0))
            heads_in_turn(pe, None, body, seam, 0)

            def latent_queries(h):
                pe.wait_ge(ah_full, of(h, 32, 4 * 48 + 32))
                for at, w in LAT_CHUNKS:
                    for k in range(2):
                        ins = pe.matmul(PS[0][:96, at:at + w], wuq[:, k, :], cqn[:, k, at:at + w], start=(k == 0), stop=(k == 1))
                ins.then_inc(mq_full, 1)
                for at, w in FULL_CHUNKS:
                    ins = pe.matmul(PS[1][:64, at:at + w], wukv[:, 0:64], ckvn[:, at:at + w], start=True, stop=True)
                ins.then_inc(mq_full, 1)

            def latent_rest(h):
                pe.wait_ge(mq_copied, of(h, 2, 2))
                for at, w in LAT_CHUNKS:
                    ins = pe.matmul(PS[0][:96, at:at + w], rot_mla[:], aq[:96, at:at + w], start=True, stop=True)
                ins.then_inc(rot_full, 1)
                for s in range(NT):
                    ins = pe.matmul(PS[1][:, s * P:(s + 1) * P], ckvn[:, s * P:(s + 1) * P], wukv[:, 64:192], start=True, stop=True)
                ins.then_inc(vt_full, 1)

            def latent_body(h):
                pe.wait_ge(qk_rot, of(h, 1, 9))
                pe.wait_ge(vt_there, of(h, 1, 5))
                pe.wait_ge(ah_used, of(h, 1, 4))
                tiles_pe(pe, of(h, MU, 4 * DU), of(h, LT, 4 * LT), 1, ((0, 96),))

            def latent_seam(h, following):
                latent_queries(following)
                turn_result((h[0], h[1] + HEADS))
                latent_rest(following)

            latent_seam((0, -1), (0, 0))
            heads_in_turn(pe, None, latent_body, latent_seam, 0)
            turn_result((0, 2 * HEADS - 1))
            pe.wait_ge(od_turned, 8)
            leave(pe)

        def attn_act(act, st):
            enter(act, "attn")
            for k, dst in enumerate((pd[0], pd[1], probT[0])):
                act.wait_ge(lat_in, 64)
                act.activation(dst[:], cqn[:, k, :] if k < 2 else ckvn[:], ACT.Square).then_inc(lat_sq, 1)
            act.wait_ge(lat_ss, 1)
            st.done(act.activation(prob[0][:], PS[0][:, 0:TOK], ACT.Ln, bias=eps_col[:, 0:1], scale=1.0 / 256))
            st.link(act.activation(prob[1][:], PS[1][:, 0:TOK], ACT.Ln, bias=eps_col[:, 0:1], scale=1.0 / 128))
            for b in range(2):
                st.done(act.activation(prob[b][:], prob[b][:], ACT.Exp, scale=-0.5))
            st.settle()
            act.sem_inc(lat_root, 1)

            def context_keys(h):
                act.wait_ge(ah_full, of(h, 48, 48))
                act.activation(kr[:, LAT:], ak[:, LAT:], ACT.Copy).then_inc(kctx_there, 1)

            def values(h):
                act.wait_ge(vt_full, of(h, 1, 1))
                act.activation(vtk[:].rearrange("p n c -> p (n c)"), PS[1][:, 0:TOK], ACT.Copy).then_inc(vt_there, 1)

            def result(h, scale):
                act.wait_ge(od_turned, of(h, 1, 1))
                act.wait_ge(amo_stored, of(h, 16, 0))
                st.link(act.activation(amo[:], PM, ACT.Copy, scale=scale))
                act.sem_inc(ah_used, 1)
                act.dma_start(mixT[of(h, 1, 0)][:, 0:LAT], amo[:]).then_inc(amo_stored, 16)

            def subln(h):
                act.wait_ge(od_sq, of(h, 1, 1))
                act.activation(ass[:], ass[:], ACT.Sqrt, bias=eps_col[:, 0:1], scale=1.0 / P).then_inc(od_root, 1)

            def body(h):
                tiles_act(act, of(h, DU, 0), of(h, LT, 0), 2, 64 ** -0.5)

            def seam(h, following):
                context_keys(following)
                subln(h)
                result(h, lam[:, 6:7])
                values(following)

            context_keys((0, 0))
            values((0, 0))
            heads_in_turn(act, st, body, seam, 1)

            def latent_queries(h):
                act.wait_ge(mq_full, of(h, 2, 1))
                act.activation(aq[:96, 0:LAT], PS[0][:96, 0:LAT], ACT.Copy).then_inc(mq_copied, 1)
                act.wait_ge(mq_full, of(h, 2, 2))
                act.activation(kr[:64, :], PS[1][:64, 0:TOK], ACT.Copy).then_inc(mq_copied, 1)

            def latent_body(h):
                tiles_act(act, of(h, MU, 4 * DU), of(h, LT, 4 * LT), 1, 96 ** -0.5)

            def latent_seam(h, following):
                latent_queries(following)
                result((h[0], h[1] + HEADS), 1.0)
                values((following[0], following[1] + HEADS))

            subln((0, HEADS - 1))
            latent_queries((0, 0))
            result((0, HEADS - 1), lam[:, 6:7])
            values((0, HEADS))
            heads_in_turn(act, st, latent_body, latent_seam, 1)
            result((0, 2 * HEADS - 1), 1.0)
            act.wait_ge(amo_stored, 128)
            leave(act)

        def rotate(dve, st, dst, src, acc, tab):
            st.done(dve.tensor_tensor(arot[:acc.shape[0], 0:LAT], acc, tab[:, 1, :], ALU.mult))
            st.link(dve.tensor_tensor(dst, src, tab[:, 0, :], ALU.mult))
            return dve.tensor_tensor(dst, dst, arot[:acc.shape[0], 0:LAT], ALU.add)

        def attn_dve(dve, st):
            enter(dve, "attn")
            st.link(dve.memset(krr[:], 0.0))
            dve.sem_inc(kr_zero, 1)
            dve.wait_ge(at_full, 16 * N_TAB)
            dve.wait_ge(lat_root, 1)
            for k in range(2):
                st.done(dve.scalar_tensor_tensor(cqn[:, k, :], cqn[:, k, :], vc2[:, V2_QN + k:V2_QN + k + 1], prob[0][:],
                                                 ALU.mult, ALU.mult))
            st.link(dve.scalar_tensor_tensor(ckvn[:], ckvn[:], vc2[:, V2_KVN:V2_KVN + 1], prob[1][:], ALU.mult, ALU.mult))
            dve.wait_ge(kr_rot, 1)
            st.done(dve.tensor_tensor(arot[64:96, 0:LAT], PM[64:96, :], rope_mla[64:96, 1, :], ALU.mult))
            st.link(dve.tensor_tensor(krr[64:96, 0:LAT], krr[64:96, 0:LAT], rope_mla[64:96, 0, :], ALU.mult))
            st.link(dve.tensor_tensor(krr[64:96, 0:LAT], krr[64:96, 0:LAT], arot[64:96, 0:LAT], ALU.add))

            def rotation(h, j):
                dst, src = ((qr[:], aq), (kr[:, 0:LAT], ak))[j]
                dve.wait_ge(rot_full, of(h, 2, j + 1))
                rotate(dve, st, dst, src[:, 0:LAT], PS[j][:, 0:LAT], rope_da).then_inc(qk_rot, 1)
                dve.wait_ge(qk_rot, of(h, 2, j + 1))

            def squares(h):
                flat = od[:].rearrange("p t c -> p (t c)")
                st.link(dve.tensor_tensor(arot[:, 0:LAT], flat, flat, ALU.mult))
                st.link(dve.tensor_reduce(ass[:], arot[:, 0:LAT].rearrange("p (t c) -> p t c", c=P), AX.X, ALU.add))
                dve.sem_inc(od_sq, 1)

            def subln(h):
                dve.wait_ge(od_root, of(h, 1, 1))
                st.link(dve.reciprocal(ass[:], ass[:]))
                st.link(dve.tensor_tensor(od[:], od[:], ass[:].unsqueeze(2).broadcast_to([P, LT, P]), ALU.mult))
                dve.sem_inc(od_there, 1)

            def body(h):
                dve.wait_ge(kctx_there, of(h, 1, 1))
                tiles_dve(dve, st, of(h, DU, 0), of(h, LT, 0), 2, 64 ** -0.5)

            def seam(h, following):
                squares(h)
                rotation(following, 0)
                subln(h)
                rotation(following, 1)

            for j in range(2):
                rotation((0, 0), j)
            heads_in_turn(dve, st, body, seam, 2 * 2 + tile_steps(2) + 4)
            squares((0, HEADS - 1))
            subln((0, HEADS - 1))

            def latent_rotation(h):
                dve.wait_ge(mq_copied, of(h, 2, 2))
                st.link(dve.tensor_copy(kr[64:96, :], krr[64:96, :]))
                dve.wait_ge(rot_full, of(h, 1, 9))
                rotate(dve, st, qr[:96, :], aq[:96, 0:LAT], PS[0][:96, 0:LAT], rope_mla).then_inc(qk_rot, 1)
                dve.wait_ge(qk_rot, of(h, 1, 9))

            def latent_body(h):
                tiles_dve(dve, st, of(h, MU, 4 * DU), of(h, LT, 4 * LT), 1, 96 ** -0.5)
                dve.sem_inc(od_there, 1)

            latent_rotation((0, 0))
            heads_in_turn(dve, st, latent_body, lambda h, following: latent_rotation(following), 1 + 2 + tile_steps(1))
            leave(dve)

        xo = [nc.alloc_sbuf_tensor_at(f"xo{b}", [P, KT, P], F32, offset=AREA + b * 4096) for b in range(2)]
        xrow = [nc.alloc_sbuf_tensor_at(f"xrow{b}", [P, D], F32, offset=AREA + 8192 + b * 4096) for b in range(2)]
        xo_there = [sem(f"xo_there{b}") for b in range(2)]
        out_stored = [sem(f"out_stored{b}") for b in range(2)]
        out_rows = out.rearrange("a (t p) d -> (a t) p d", p=P)

        def final_dve(dve, st):
            enter(dve, "final")
            norm_pairs(dve, "final")
            dve.wait_ge(s_root, len(NORMS))
            with dve.Fori(0, LT // 2) as i:
                st.enter(i, 2)
                for b in range(2):
                    cols = bass.ds(i * (2 * P) + b * P, P)
                    dve.wait_ge(tile_turned[b], NT // 2 + i)
                    st.link(dve.tensor_tensor(xo[b][:], XT[:, :, cols], nrs[:, cols].unsqueeze(1).broadcast_to([P, KT, P]), ALU.mult))
                    dve.tensor_tensor(xo[b][:], xo[b][:], vc1[:, V1_FIN:V1_FIN + KT].unsqueeze(2).broadcast_to([P, KT, P]),
                                      ALU.mult).then_inc(xo_there[b], 1)
                st.leave(LT // 2)

        def final_pe(pe):
            norm_pe(pe, "final")
            with pe.Fori(0, LT // 2) as i:
                for b in range(2):
                    pe.wait_ge(xo_there[b], i + 1)
                    pe.wait_ge(tile_read[b], NT // 2 + i)
                    pe.wait_ge(s_root, len(NORMS))
                    for k in range(KT):
                        ins = pe.transpose(PS[b][:, k * P:(k + 1) * P], xo[b][:, k, :], ident[:])
                    ins.then_inc(tile_turned[b], 1)

        def final_act(act, st):
            norm_act(act, st, "final", split=False)
            with act.Fori(0, LT // 2) as i:
                for b in range(2):
                    act.wait_ge(tile_turned[b], NT // 2 + i + 1)
                    act.wait_ge(out_stored[b], i * 16)
                    act.activation(xrow[b][:], PS[b][:, 0:D], ACT.Copy).then_inc(tile_read[b], 1)
                    act.wait_ge(tile_read[b], NT // 2 + i + 1)
                    act.dma_start(out_rows[i * 2 + b], xrow[b][:]).then_inc(out_stored[b], 16)
            for b in range(2):
                act.wait_ge(out_stored[b], 16 * (LT // 2))

        block = ctx.enter_context(nc.Block())

        @block.sync
        def _(sp):
            load_sp(sp)
            ada_sp(sp)
            in0_sp(sp)
            hyena_sp(sp)
            hgrn_sp(sp)
            mix_sp(sp, 0, TOK)
            sp_linear(sp, "out0", w_src["out0"], KT)
            sp_ffn(sp, 0)
            sp_linear(sp, "in1", w_src["in1"], ODD_MAIN - 1)
            base = SLAB0["in1"] // 2 + (ODD_MAIN - 1) // 2
            sp_slab(sp, (0, base), w_src["in1"][:, :, (ODD_MAIN - 1) * P:ODD_MAIN * P])
            sp_slab(sp, (1, base), w_src["in1"][:, :, ODD_MAIN * P:ODD_MAIN * P + 32], lambda b: raw[b][:, :, 64:96])
            attn_sp(sp)
            mix_sp(sp, 1, LAT)
            sp_linear(sp, "out1", w_src["out1"], KT)
            sp_ffn(sp, 1)

        @block.gpsimd
        def _(pool):
            pool.memset(one_p[:], 1.0).then_inc(pool_step, 1)
            pool.wait_ge(pool_step, 1)
            for name, _ in GEMMS:
                if name.startswith("ffn"):
                    pool_ffn(pool, int(name[3]))
                else:
                    pool_linear(pool, name)
                if name == "in0":
                    hgrn_pool(pool)

        @block.tensor
        def _(pe):
            st = Steps(pe, pe_step)
            load_pe(pe)
            ada_pe(pe)
            norm_pe(pe, "norm0")
            in0_pe(pe)
            hyena_pe(pe, st)
            hgrn_pe(pe, st)
            out_pe(pe, 0)
            norm_pe(pe, "normf0")
            ffn_pe(pe, 0)
            norm_pe(pe, "norm1")
            in_pe(pe, "in1", 16)
            attn_pe(pe, st)
            out_pe(pe, 1)
            norm_pe(pe, "normf1")
            ffn_pe(pe, 1)
            final_pe(pe)

        @block.scalar
        def _(act):
            st = Steps(act, act_step)
            ada_act(act, st)
            norm_act(act, st, "norm0")
            spill_act(act, "in0", 32)
            hyena_act(act, st)
            hgrn_act(act, st)
            mix_act(act, 0, TOK)
            norm_act(act, st, "normf0")
            ffn_act(act, 0)
            norm_act(act, st, "norm1")
            spill_act(act, "in1", 16)
            attn_act(act, st)
            mix_act(act, 1, LAT)
            norm_act(act, st, "normf1")
            ffn_act(act, 1)
            final_act(act, st)

        @block.vector
        def _(dve):
            st = Steps(dve, dve_step)
            load_dve(dve, st)
            ada_dve(dve, st)
            norm_dve(dve, st, "norm0")
            in0_dve(dve, st)
            hyena_dve(dve, st)
            hgrn_dve(dve, st)
            mix_dve(dve, 0, TOK)
            out_dve(dve, 0)
            norm_dve(dve, st, "normf0")
            ffn_dve(dve, 0)
            norm_dve(dve, st, "norm1")
            attn_dve(dve, st)
            mix_dve(dve, 1, LAT)
            out_dve(dve, 1)
            norm_dve(dve, st, "normf1")
            ffn_dve(dve, 1)
            final_dve(dve, st)


_INS = ['x', 'c', 'ctx', 'c_ctx', 'ada_w', 'ada_b', 'norm_mix_g', 'norm_ffn_g', 'ffn_w_gu', 'ffn_w_down', 'ev_w_in',
        'ev_w_out', 'hg_lower_bound', 'hg_out_norm_g', 'hy_short_w', 'hy_short_b', 'hy_filt_w1', 'hy_filt_b1',
        'hy_filt_freq1', 'hy_filt_w2', 'hy_filt_b2', 'hy_filt_freq2', 'hy_filt_w3', 'hy_skip', 'od_w_in', 'od_w_out',
        'da_lambda', 'da_subln_g', 'mla_q_norm_g', 'mla_w_uq', 'mla_kv_norm_g', 'mla_w_ukv', 'final_norm_g']


def kernel(**inputs):
    import numpy as _np
    import concourse.bacc as _bacc
    from concourse import mybir as _mybir
    from concourse.bass_utils import run_bass_kernel_spmd as _run

    nc = _bacc.Bacc("TRN2", target_bir_lowering=False, num_devices=1)
    arrays, T = {}, {}
    given = {n: _np.ascontiguousarray(inputs[n]) for n in _INS}
    given.update(constants())
    for name, a in given.items():
        arrays[f"in_{name}_dram"] = a
        T[name] = nc.dram_tensor(f"in_{name}_dram", a.shape, _mybir.dt.from_np(a.dtype), kind="ExternalInput").ap()
    out = nc.dram_tensor("out_dram", (1, LAT, D), _mybir.dt.float32, kind="ExternalOutput").ap()
    scratch = {n: nc.dram_tensor(n + "_dram", s, _mybir.dt.float32, kind="Internal").ap() for n, s in SCRATCH.items()}
    build(nc, T, out, scratch)
    r = _run(nc, [arrays], core_ids=[0])
    return r.results[0]["out_dram"]
```
